# Optimizing a Trainium2 kernel written in Bass

```python
import jax, jax.numpy as jnp
from jax import lax
import numpy as np

D_MODEL = 1024
BATCH = 1
SEQ = 256
DEPTH = 2

N_MIXERS = 2
HEAD_DIM = 64
FOX_HEADS = D_MODEL // HEAD_DIM
DIL_HEADS = D_MODEL // HEAD_DIM
DIL_CONFIGS = ((128, 1), (512, 4), (2048, 16))
N_DIL_GROUPS = len(DIL_CONFIGS)
ROPE_THETA = 500000.0
ROPE_DIM = HEAD_DIM // 4
D_FF = 2816
Q_BLOCK = 128
EPS = 1e-6
MACARON_WEIGHT = 0.5
N_SUBLAYERS = 3
N_FOX_LAYERS = (DEPTH + 1) // 2
N_DIL_LAYERS = DEPTH // 2
FOX_IN = 3 * FOX_HEADS * HEAD_DIM + FOX_HEADS
DIL_IN = N_DIL_GROUPS * 3 * DIL_HEADS * HEAD_DIM


def rms_norm(x, g):
    xf = x.astype(jnp.float32)
    y = xf * lax.rsqrt(jnp.mean(xf * xf, axis=-1, keepdims=True) + EPS)
    return (y * g.astype(jnp.float32)).astype(x.dtype)

def modulate(h, shift, scale):
    return h * (1.0 + scale[:, None, :]) + shift[:, None, :]

def swiglu(h, w_gate, w_up, w_down):
    return (jax.nn.silu(h @ w_gate) * (h @ w_up)) @ w_down

def rope_tables(positions):
    half = ROPE_DIM // 2
    inv_freq = ROPE_THETA ** (-(jnp.arange(half, dtype=jnp.float32) * 2.0 / ROPE_DIM))
    ang = positions.astype(jnp.float32)[..., None] * inv_freq
    return jnp.cos(ang)[:, :, None, :], jnp.sin(ang)[:, :, None, :]

def apply_rope(x, cos, sin):
    half = ROPE_DIM // 2
    xr = x[..., :ROPE_DIM].astype(jnp.float32)
    x1, x2 = xr[..., :half], xr[..., half:]
    rot = jnp.concatenate([x1 * cos - x2 * sin, x2 * cos + x1 * sin], axis=-1).astype(x.dtype)
    return jnp.concatenate([rot, x[..., ROPE_DIM:]], axis=-1)

def fox_attention(h, w_in, b_f, q_gain, k_gain, w_out):
    B, S, _ = h.shape
    H, hd = FOX_HEADS, HEAD_DIM
    proj = h @ w_in
    qkv = proj[..., : 3 * H * hd].reshape(B, S, 3, H, hd)
    f_logit = proj[..., 3 * H * hd:].astype(jnp.float32) + b_f.astype(jnp.float32)
    q = rms_norm(qkv[:, :, 0], q_gain).transpose(0, 2, 1, 3)
    k = rms_norm(qkv[:, :, 1], k_gain).transpose(0, 2, 1, 3)
    v = qkv[:, :, 2].transpose(0, 2, 1, 3)
    cum = jnp.cumsum(jax.nn.log_sigmoid(f_logit), axis=1).transpose(0, 2, 1)
    scale = hd ** -0.5
    outs = []
    for blk in range(S // Q_BLOCK):
        q0 = blk * Q_BLOCK
        kv_len = q0 + Q_BLOCK
        logits = jnp.einsum("bhqd,bhkd->bhqk", q[:, :, q0:kv_len], k[:, :, :kv_len]).astype(jnp.float32) * scale
        logits = logits + cum[:, :, q0:kv_len, None] - cum[:, :, None, :kv_len]
        q_idx = q0 + jnp.arange(Q_BLOCK)
        k_idx = jnp.arange(kv_len)
        mask = k_idx[None, :] <= q_idx[:, None]
        logits = jnp.where(mask[None, None], logits, -jnp.inf)
        p = jax.nn.softmax(logits, axis=-1).astype(v.dtype)
        outs.append(jnp.einsum("bhqk,bhkd->bhqd", p, v[:, :, :kv_len]))
    o = jnp.concatenate(outs, axis=2).transpose(0, 2, 1, 3).reshape(B, S, H * hd)
    return o @ w_out

def dilated_group(q, k, v, window, dilation):
    B, S, H, hd = q.shape
    n_keys = window // dilation + 1
    offsets = dilation * jnp.arange(n_keys)
    scale = hd ** -0.5

    def block_fn(q0):
        qb = lax.dynamic_slice_in_dim(q, q0, Q_BLOCK, axis=1)
        t = q0 + jnp.arange(Q_BLOCK)
        idx = t[:, None] - offsets[None, :]
        valid = idx >= 0
        idx_c = jnp.maximum(idx, 0)
        kb = jnp.take(k, idx_c, axis=1)
        vb = jnp.take(v, idx_c, axis=1)
        logits = jnp.einsum("bqhd,bqkhd->bhqk", qb, kb).astype(jnp.float32) * scale
        logits = jnp.where(valid[None, None], logits, -jnp.inf)
        lse = jax.nn.logsumexp(logits, axis=-1)
        p = jnp.exp(logits - lse[..., None]).astype(v.dtype)
        ob = jnp.einsum("bhqk,bqkhd->bqhd", p, vb)
        return ob, lse

    starts = jnp.arange(S // Q_BLOCK) * Q_BLOCK
    o, lse = lax.map(block_fn, starts)
    o = o.transpose(1, 0, 2, 3, 4).reshape(B, S, H, hd)
    lse = lse.transpose(1, 0, 3, 2).reshape(B, S, H)
    return o, lse

def dilated_attention(h, cos, sin, w_in, q_gain, k_gain, w_out):
    B, S, _ = h.shape
    H, hd = DIL_HEADS, HEAD_DIM
    proj = (h @ w_in).reshape(B, S, N_DIL_GROUPS, 3, H, hd)
    outs, lses = [], []
    for g, (window, dilation) in enumerate(DIL_CONFIGS):
        q = apply_rope(rms_norm(proj[:, :, g, 0], q_gain[g]), cos, sin)
        k = apply_rope(rms_norm(proj[:, :, g, 1], k_gain[g]), cos, sin)
        o, lse = dilated_group(q, k, proj[:, :, g, 2], window, dilation)
        outs.append(o)
        lses.append(lse)
    alpha = jax.nn.softmax(jnp.stack(lses, axis=0), axis=0)
    o = jnp.sum(alpha[..., None] * jnp.stack(outs, axis=0).astype(jnp.float32), axis=0).astype(h.dtype)
    return o.reshape(B, S, H * hd) @ w_out

def first_inputs(seed: int = 0) -> dict:
    key = jax.random.key(seed)
    ks = jax.random.split(key, 20)
    D = D_MODEL
    nrm = jax.random.normal
    x = nrm(ks[0], (BATCH, SEQ, D), jnp.float32)
    c = nrm(ks[1], (BATCH, D), jnp.float32)
    offs = jax.random.randint(ks[2], (BATCH, 1), 0, 4096, dtype=jnp.int32)
    positions = (offs + jnp.arange(SEQ, dtype=jnp.int32)[None, :]).astype(jnp.int32)
    mod_w = nrm(ks[3], (DEPTH, D, N_SUBLAYERS * 3 * D), jnp.float32) * (0.5 * D ** -0.5)
    mod_b = nrm(ks[4], (DEPTH, N_SUBLAYERS * 3 * D), jnp.float32) * 0.01
    norm_g = 1.0 + 0.02 * nrm(ks[5], (DEPTH, N_SUBLAYERS, D), jnp.float32)
    ffn_w_gate = nrm(ks[6], (DEPTH, 2, D, D_FF), jnp.float32) * D ** -0.5
    ffn_w_up = nrm(ks[7], (DEPTH, 2, D, D_FF), jnp.float32) * D ** -0.5
    ffn_w_down = nrm(ks[8], (DEPTH, 2, D_FF, D), jnp.float32) * D_FF ** -0.5
    fox_w_in = nrm(ks[9], (N_FOX_LAYERS, D, FOX_IN), jnp.float32) * D ** -0.5
    fox_b_f = jax.random.uniform(ks[10], (N_FOX_LAYERS, FOX_HEADS), jnp.float32, 1.0, 6.0)
    fox_q_g = 1.0 + 0.02 * nrm(ks[11], (N_FOX_LAYERS, HEAD_DIM), jnp.float32)
    fox_k_g = 1.0 + 0.02 * nrm(ks[12], (N_FOX_LAYERS, HEAD_DIM), jnp.float32)
    fox_w_out = nrm(ks[13], (N_FOX_LAYERS, FOX_HEADS * HEAD_DIM, D), jnp.float32) * (FOX_HEADS * HEAD_DIM) ** -0.5
    dil_w_in = nrm(ks[14], (N_DIL_LAYERS, D, DIL_IN), jnp.float32) * D ** -0.5
    dil_q_g = 1.0 + 0.02 * nrm(ks[15], (N_DIL_LAYERS, N_DIL_GROUPS, HEAD_DIM), jnp.float32)
    dil_k_g = 1.0 + 0.02 * nrm(ks[16], (N_DIL_LAYERS, N_DIL_GROUPS, HEAD_DIM), jnp.float32)
    dil_w_out = nrm(ks[17], (N_DIL_LAYERS, DIL_HEADS * HEAD_DIM, D), jnp.float32) * (DIL_HEADS * HEAD_DIM) ** -0.5
    return {"x": x, "c": c, "positions": positions, "mod_w": mod_w, "mod_b": mod_b,
            "norm_g": norm_g, "ffn_w_gate": ffn_w_gate, "ffn_w_up": ffn_w_up,
            "ffn_w_down": ffn_w_down, "fox_w_in": fox_w_in, "fox_b_f": fox_b_f,
            "fox_q_g": fox_q_g, "fox_k_g": fox_k_g, "fox_w_out": fox_w_out,
            "dil_w_in": dil_w_in, "dil_q_g": dil_q_g, "dil_k_g": dil_k_g, "dil_w_out": dil_w_out}

def first_block(x, c, positions, mod_w, mod_b, norm_g, ffn_w_gate, ffn_w_up, ffn_w_down,
              fox_w_in, fox_b_f, fox_q_g, fox_k_g, fox_w_out,
              dil_w_in, dil_q_g, dil_k_g, dil_w_out):
    B = x.shape[0]
    D = x.shape[-1]
    cos, sin = rope_tables(positions)
    c_act = jax.nn.silu(c)
    for i in range(DEPTH):
        mod = (c_act @ mod_w[i] + mod_b[i]).reshape(B, N_SUBLAYERS, 3, D)
        shift, scale, gate = mod[:, :, 0], mod[:, :, 1], mod[:, :, 2]
        h = modulate(rms_norm(x, norm_g[i, 0]), shift[:, 0], scale[:, 0])
        x = x + MACARON_WEIGHT * gate[:, 0, None, :] * swiglu(h, ffn_w_gate[i, 0], ffn_w_up[i, 0], ffn_w_down[i, 0])
        h = modulate(rms_norm(x, norm_g[i, 1]), shift[:, 1], scale[:, 1])
        j = i // N_MIXERS
        if i % N_MIXERS == 0:
            y = fox_attention(h, fox_w_in[j], fox_b_f[j], fox_q_g[j], fox_k_g[j], fox_w_out[j])
        else:
            y = dilated_attention(h, cos, sin, dil_w_in[j], dil_q_g[j], dil_k_g[j], dil_w_out[j])
        x = x + gate[:, 1, None, :] * y
        h = modulate(rms_norm(x, norm_g[i, 2]), shift[:, 2], scale[:, 2])
        x = x + MACARON_WEIGHT * gate[:, 2, None, :] * swiglu(h, ffn_w_gate[i, 1], ffn_w_up[i, 1], ffn_w_down[i, 1])
    return x


D_MIX = D_MODEL
C_CONV = D_MIX // 4
NSA_HEADS = 4
C_NSA = NSA_HEADS * HEAD_DIM
C_SGU = D_MIX // 4
C_POOL = D_MIX // 4
CONV_K = 31
CMP_LEN = 32
CMP_STRIDE = 16
SEL_LEN = 64
SEL_TOPK = 16
WINDOW = 512
SGU_CHUNK = 128
SGU_GROUPS = 4
POOL_WINDOWS = (2, 4, 8, 16)
FFN_DIM = 2816
FFN_CONV_K = 3
ROPE_THETA_2 = 10000.0
RMS_EPS = 1e-6
LN_EPS = 1e-5
NEG_INF = -1e30
FORCE_SCORE = 1e6
N_IN = 2 * C_CONV + C_NSA + 6 * HEAD_DIM + 3 * NSA_HEADS + 2 * C_SGU + C_POOL


def rms_norm_2(x, g):
    xf = x.astype(jnp.float32)
    y = xf * lax.rsqrt(jnp.mean(xf * xf, axis=-1, keepdims=True) + RMS_EPS)
    return y.astype(x.dtype) * g

def layer_norm(x, g, b):
    xf = x.astype(jnp.float32)
    mu = jnp.mean(xf, axis=-1, keepdims=True)
    var = jnp.mean(jnp.square(xf - mu), axis=-1, keepdims=True)
    return ((xf - mu) * lax.rsqrt(var + LN_EPS)).astype(x.dtype) * g + b

def causal_dwconv(x, w, b):
    k, c = w.shape
    y = lax.conv_general_dilated(x, w[:, None, :].astype(x.dtype), window_strides=(1,),
                                 padding=[(k - 1, 0)], dimension_numbers=('NWC', 'WIO', 'NWC'),
                                 feature_group_count=c)
    return y + b

def rope_tables_2(seq):
    half = HEAD_DIM // 2
    inv = ROPE_THETA_2 ** (-jnp.arange(half, dtype=jnp.float32) * 2.0 / HEAD_DIM)
    ang = jnp.arange(seq, dtype=jnp.float32)[:, None] * inv[None, :]
    return jnp.cos(ang), jnp.sin(ang)

def apply_rope_2(x, cos, sin):
    half = HEAD_DIM // 2
    shp = (cos.shape[0],) + (1,) * (x.ndim - 3) + (half,)
    c = cos.reshape(shp).astype(x.dtype)
    s = sin.reshape(shp).astype(x.dtype)
    x1, x2 = x[..., :half], x[..., half:]
    return jnp.concatenate([x1 * c - x2 * s, x2 * c + x1 * s], axis=-1)

def masked_softmax(s, mask):
    p = jax.nn.softmax(jnp.where(mask, s, NEG_INF), axis=-1)
    return jnp.where(mask, p, 0.0)

def conformer_conv(z, w, b, ln_g, ln_b):
    a, gate = jnp.split(z, 2, axis=-1)
    y = causal_dwconv(a * jax.nn.sigmoid(gate), w, b)
    return jax.nn.silu(layer_norm(y, ln_g, ln_b))

def nsa_attention(q, k_cmp, v_cmp, k_slc, v_slc, k_win, v_win, gates,
                  pe_k, pe_v, ck_w1, ck_w2, cv_w1, cv_w2, cos, sin):
    bsz, seq = q.shape[0], q.shape[1]
    scale = HEAD_DIM ** -0.5
    n_cmp = (seq - CMP_LEN) // CMP_STRIDE + 1
    n_sel = seq // SEL_LEN
    top_n = min(SEL_TOPK, n_sel)
    ratio = SEL_LEN // CMP_STRIDE
    n_ov = CMP_LEN // CMP_STRIDE
    front = n_ov - 1
    right = ratio * n_sel + ratio - front - n_cmp

    blk_idx = jnp.arange(n_cmp)[:, None] * CMP_STRIDE + jnp.arange(CMP_LEN)[None, :]

    def compress(t, pe, w1, w2):
        blocks = (t[:, blk_idx] + pe).reshape(bsz, n_cmp, CMP_LEN * HEAD_DIM)
        return jax.nn.gelu(blocks @ w1) @ w2

    kc = compress(k_cmp, pe_k, ck_w1, ck_w2)
    vc = compress(v_cmp, pe_v, cv_w1, cv_w2)
    cmp_end = jnp.arange(n_cmp) * CMP_STRIDE + CMP_LEN - 1

    q_cmp = q * scale
    q_rot = apply_rope_2(q, cos, sin) * scale
    ks_blocks = apply_rope_2(k_slc, cos, sin).reshape(bsz, n_sel, SEL_LEN, HEAD_DIM)
    vs_blocks = v_slc.reshape(bsz, n_sel, SEL_LEN, HEAD_DIM)
    kw_pad = jnp.pad(apply_rope_2(k_win, cos, sin), ((0, 0), (WINDOW, 0), (0, 0)))
    vw_pad = jnp.pad(v_win, ((0, 0), (WINDOW, 0), (0, 0)))
    sel_j = jnp.arange(n_sel)
    gather = jax.vmap(lambda blocks, idx: blocks[idx])

    def query_block(i):
        t0 = i * Q_BLOCK
        pos = t0 + jnp.arange(Q_BLOCK)
        qc = lax.dynamic_slice_in_dim(q_cmp, t0, Q_BLOCK, axis=1)
        qr = lax.dynamic_slice_in_dim(q_rot, t0, Q_BLOCK, axis=1)
        g = lax.dynamic_slice_in_dim(gates, t0, Q_BLOCK, axis=1)

        s = jnp.einsum('bthd,bnd->bhtn', qc, kc, preferred_element_type=jnp.float32)
        p_cmp = masked_softmax(s, cmp_end[None, :] <= pos[:, None])
        o_cmp = jnp.einsum('bhtn,bnd->bthd', p_cmp.astype(vc.dtype), vc)

        pp = jnp.pad(p_cmp.sum(axis=1), ((0, 0), (0, 0), (front, right)))
        imp = jnp.zeros((bsz, Q_BLOCK, n_sel), jnp.float32)
        for m in range(ratio):
            for n in range(n_ov):
                imp = imp + pp[..., m - n + front::ratio][..., :n_sel]
        cur = (pos // SEL_LEN)[:, None]
        forced = (sel_j[None, :] == 0) | (sel_j[None, :] == cur) | (sel_j[None, :] == cur - 1)
        valid = sel_j[None, :] * SEL_LEN <= pos[:, None]
        imp = jnp.where(valid, jnp.where(forced, FORCE_SCORE, imp), NEG_INF)
        top_val, top_idx = lax.top_k(imp, top_n)

        ksel = gather(ks_blocks, top_idx).reshape(bsz, Q_BLOCK, top_n * SEL_LEN, HEAD_DIM)
        vsel = gather(vs_blocks, top_idx).reshape(bsz, Q_BLOCK, top_n * SEL_LEN, HEAD_DIM)
        tok = (top_idx[..., None] * SEL_LEN + jnp.arange(SEL_LEN)).reshape(bsz, Q_BLOCK, top_n * SEL_LEN)
        sel_ok = jnp.repeat(top_val > 0.5 * NEG_INF, SEL_LEN, axis=-1)
        mask_sel = sel_ok & (tok <= pos[None, :, None])
        s = jnp.einsum('bthd,btkd->bhtk', qr, ksel, preferred_element_type=jnp.float32)
        p = masked_softmax(s, mask_sel[:, None])
        o_slc = jnp.einsum('bhtk,btkd->bthd', p.astype(vsel.dtype), vsel)

        kw = lax.dynamic_slice_in_dim(kw_pad, t0, Q_BLOCK + WINDOW, axis=1)
        vw = lax.dynamic_slice_in_dim(vw_pad, t0, Q_BLOCK + WINDOW, axis=1)
        kpos = t0 - WINDOW + jnp.arange(Q_BLOCK + WINDOW)
        mask_win = ((kpos[None, :] >= 0) & (kpos[None, :] <= pos[:, None])
                    & (kpos[None, :] > pos[:, None] - WINDOW))
        s = jnp.einsum('bthd,bkd->bhtk', qr, kw, preferred_element_type=jnp.float32)
        p = masked_softmax(s, mask_win)
        o_win = jnp.einsum('bhtk,bkd->bthd', p.astype(vw.dtype), vw)

        return g[..., 0:1] * o_cmp + g[..., 1:2] * o_slc + g[..., 2:3] * o_win

    out = lax.map(query_block, jnp.arange(seq // Q_BLOCK))
    return out.transpose(1, 0, 2, 3, 4).reshape(bsz, seq, C_NSA)

def spatial_gating(z, ln_g, ln_b, w_s, b_s):
    z = jax.nn.gelu(z)
    u, v = jnp.split(z, 2, axis=-1)
    v = layer_norm(v, ln_g, ln_b)
    bsz, seq, c = v.shape
    vr = v.reshape(bsz, seq // SGU_CHUNK, SGU_CHUNK, SGU_GROUPS, c // SGU_GROUPS)
    causal = jnp.tril(jnp.ones((SGU_CHUNK, SGU_CHUNK), dtype=bool))
    ws = jnp.where(causal, w_s, 0.0).astype(v.dtype)
    f = jnp.einsum('gts,bcsgd->bctgd', ws, vr) + b_s.T[:, :, None]
    return u * f.reshape(bsz, seq, c)

def multiscale_pool(z, w_p, scale):
    bsz, seq, c = z.shape
    cg = c // len(POOL_WINDOWS)
    zf = z.astype(jnp.float32)
    cs = jnp.pad(jnp.cumsum(zf, axis=1), ((0, 0), (1, 0), (0, 0)))
    t = jnp.arange(seq)
    outs = []
    for gi, w in enumerate(POOL_WINDOWS):
        c_g = cs[..., gi * cg:(gi + 1) * cg]
        lag = jnp.pad(c_g[:, :seq + 1 - w], ((0, 0), (w - 1, 0), (0, 0)))
        cnt = jnp.minimum(t + 1, w).astype(jnp.float32)[:, None]
        outs.append((c_g[:, 1:] - lag) / cnt - zf[..., gi * cg:(gi + 1) * cg])
    pooled = jnp.stack(outs, axis=2).astype(z.dtype)
    y = jnp.einsum('bsgc,gcd->bsgd', pooled, w_p).reshape(bsz, seq, c)
    return y * scale

def conv_ffn(h, w_up, cw, cb, w_down):
    gu = causal_dwconv(h @ w_up, cw, cb)
    g, u = jnp.split(gu, 2, axis=-1)
    return (jax.nn.gelu(g, approximate=True) * u) @ w_down

def second_inputs(seed: int = 0) -> dict:
    key = jax.random.key(seed)
    ks = jax.random.split(key, 32)
    L = DEPTH
    hd = HEAD_DIM

    def nrm(k, shape, s):
        return jax.random.normal(k, shape, jnp.float32) * s

    def gain(k, shape):
        return 1.0 + nrm(k, shape, 0.05)

    return {
        'x': nrm(ks[0], (BATCH, SEQ, D_MODEL), 1.0),
        'norm_mix_pre': gain(ks[1], (L, D_MODEL)),
        'norm_mix_post': gain(ks[2], (L, D_MODEL)),
        'norm_ffn_pre': gain(ks[3], (L, D_MODEL)),
        'norm_ffn_post': gain(ks[4], (L, D_MODEL)),
        'w_in': nrm(ks[5], (L, D_MODEL, N_IN), D_MODEL ** -0.5),
        'w_out': nrm(ks[6], (L, D_MIX, D_MODEL), D_MIX ** -0.5),
        'conv_dw_w': nrm(ks[7], (L, CONV_K, C_CONV), CONV_K ** -0.5),
        'conv_dw_b': nrm(ks[8], (L, C_CONV), 0.02),
        'conv_ln_g': gain(ks[9], (L, C_CONV)),
        'conv_ln_b': nrm(ks[10], (L, C_CONV), 0.02),
        'nsa_pe_k': nrm(ks[11], (L, CMP_LEN, hd), 0.1),
        'nsa_pe_v': nrm(ks[12], (L, CMP_LEN, hd), 0.1),
        'nsa_ck_w1': nrm(ks[13], (L, CMP_LEN * hd, hd), (CMP_LEN * hd) ** -0.5),
        'nsa_ck_w2': nrm(ks[14], (L, hd, hd), hd ** -0.5),
        'nsa_cv_w1': nrm(ks[15], (L, CMP_LEN * hd, hd), (CMP_LEN * hd) ** -0.5),
        'nsa_cv_w2': nrm(ks[16], (L, hd, hd), hd ** -0.5),
        'sgu_ln_g': gain(ks[17], (L, C_SGU)),
        'sgu_ln_b': nrm(ks[18], (L, C_SGU), 0.02),
        'sgu_w': nrm(ks[19], (L, SGU_GROUPS, SGU_CHUNK, SGU_CHUNK), SGU_CHUNK ** -0.5),
        'sgu_b': 1.0 + nrm(ks[20], (L, SGU_GROUPS, SGU_CHUNK), 0.1),
        'pool_w': nrm(ks[21], (L, len(POOL_WINDOWS), C_POOL // 4, C_POOL // 4), (C_POOL // 4) ** -0.5),
        'pool_scale': gain(ks[22], (L, C_POOL)),
        'ffn_up': nrm(ks[23], (L, D_MODEL, 2 * FFN_DIM), D_MODEL ** -0.5),
        'ffn_conv_w': nrm(ks[24], (L, FFN_CONV_K, 2 * FFN_DIM), FFN_CONV_K ** -0.5),
        'ffn_conv_b': nrm(ks[25], (L, 2 * FFN_DIM), 0.02),
        'ffn_down': nrm(ks[26], (L, FFN_DIM, D_MODEL), FFN_DIM ** -0.5),
    }

def second_block(x, norm_mix_pre, norm_mix_post, norm_ffn_pre, norm_ffn_post, w_in, w_out,
              conv_dw_w, conv_dw_b, conv_ln_g, conv_ln_b,
              nsa_pe_k, nsa_pe_v, nsa_ck_w1, nsa_ck_w2, nsa_cv_w1, nsa_cv_w2,
              sgu_ln_g, sgu_ln_b, sgu_w, sgu_b, pool_w, pool_scale,
              ffn_up, ffn_conv_w, ffn_conv_b, ffn_down):
    bsz, seq, _ = x.shape
    cos, sin = rope_tables_2(seq)
    sizes = (2 * C_CONV, C_NSA, 6 * HEAD_DIM, 3 * NSA_HEADS, 2 * C_SGU, C_POOL)
    offsets = [int(o) for o in np.cumsum(sizes)[:-1]]
    for l in range(DEPTH):
        h = rms_norm_2(x, norm_mix_pre[l])
        z = h @ w_in[l]
        za, zq, zkv, zg, zc, zd = jnp.split(z, offsets, axis=-1)
        y_conv = conformer_conv(za, conv_dw_w[l], conv_dw_b[l], conv_ln_g[l], conv_ln_b[l])
        q = zq.reshape(bsz, seq, NSA_HEADS, HEAD_DIM)
        kv = zkv.reshape(bsz, seq, 6, HEAD_DIM)
        gates = jax.nn.sigmoid(zg).reshape(bsz, seq, NSA_HEADS, 3)
        y_nsa = nsa_attention(q, kv[:, :, 0], kv[:, :, 1], kv[:, :, 2], kv[:, :, 3], kv[:, :, 4], kv[:, :, 5],
                              gates, nsa_pe_k[l], nsa_pe_v[l], nsa_ck_w1[l], nsa_ck_w2[l],
                              nsa_cv_w1[l], nsa_cv_w2[l], cos, sin)
        y_sgu = spatial_gating(zc, sgu_ln_g[l], sgu_ln_b[l], sgu_w[l], sgu_b[l])
        y_pool = multiscale_pool(zd, pool_w[l], pool_scale[l])
        y = jnp.concatenate([y_conv, y_nsa, y_sgu, y_pool], axis=-1) @ w_out[l]
        x = x + rms_norm_2(y, norm_mix_post[l])
        h = rms_norm_2(x, norm_ffn_pre[l])
        y = conv_ffn(h, ffn_up[l], ffn_conv_w[l], ffn_conv_b[l], ffn_down[l])
        x = x + rms_norm_2(y, norm_ffn_post[l])
    return x


def setup_inputs(seed=0):
    out = dict(first_inputs(seed))
    for name, value in second_inputs(seed + 1).items():
        if name != "x":
            out[name + "_2"] = value
    return out


def reference(
    x, c, positions, mod_w, mod_b, norm_g, ffn_w_gate, ffn_w_up, ffn_w_down, fox_w_in, fox_b_f,
    fox_q_g, fox_k_g, fox_w_out, dil_w_in, dil_q_g, dil_k_g, dil_w_out, norm_mix_pre_2,
    norm_mix_post_2, norm_ffn_pre_2, norm_ffn_post_2, w_in_2, w_out_2, conv_dw_w_2, conv_dw_b_2,
    conv_ln_g_2, conv_ln_b_2, nsa_pe_k_2, nsa_pe_v_2, nsa_ck_w1_2, nsa_ck_w2_2, nsa_cv_w1_2,
    nsa_cv_w2_2, sgu_ln_g_2, sgu_ln_b_2, sgu_w_2, sgu_b_2, pool_w_2, pool_scale_2, ffn_up_2,
    ffn_conv_w_2, ffn_conv_b_2, ffn_down_2,
):
    x = first_block(
        x, c, positions, mod_w, mod_b, norm_g, ffn_w_gate, ffn_w_up, ffn_w_down, fox_w_in,
        fox_b_f, fox_q_g, fox_k_g, fox_w_out, dil_w_in, dil_q_g, dil_k_g, dil_w_out,
    )
    return second_block(
        x, norm_mix_pre_2, norm_mix_post_2, norm_ffn_pre_2, norm_ffn_post_2, w_in_2, w_out_2,
        conv_dw_w_2, conv_dw_b_2, conv_ln_g_2, conv_ln_b_2, nsa_pe_k_2, nsa_pe_v_2, nsa_ck_w1_2,
        nsa_ck_w2_2, nsa_cv_w1_2, nsa_cv_w2_2, sgu_ln_g_2, sgu_ln_b_2, sgu_w_2, sgu_b_2,
        pool_w_2, pool_scale_2, ffn_up_2, ffn_conv_w_2, ffn_conv_b_2, ffn_down_2,
    )


_drawn_inputs = setup_inputs


def setup_inputs(seed=0):
    import zlib

    import numpy as np

    out = dict(_drawn_inputs(seed))
    spreads = {}
    factors = {'mod_b': 3.858,
     'norm_g': 5.755,
     'fox_q_g': 8.0,
     'fox_k_g': 8.0,
     'dil_q_g': 8.0,
     'dil_k_g': 8.0,
     'conv_dw_b_2': 90.253,
     'conv_ln_b_2': 200.0,
     'nsa_pe_k_2': 64.0,
     'nsa_pe_v_2': 20.953,
     'sgu_ln_g_2': 24.744,
     'sgu_ln_b_2': 64.0,
     'norm_mix_pre_2': 5.233,
     'norm_mix_post_2': 6.956,
     'norm_ffn_pre_2': 4.793,
     'norm_ffn_post_2': 6.844,
     'conv_ln_g_2': 64.0,
     'nsa_ck_w1_2': 8.0,
     'nsa_ck_w2_2': 8.0,
     'nsa_cv_w1_2': 3.291,
     'sgu_b_2': 8.0,
     'pool_scale_2': 8.0,
     'ffn_conv_b_2': 8.0}
    for name, (base, spread) in spreads.items():
        noise = np.random.default_rng([zlib.crc32(name.encode()), seed]).standard_normal(out[name].shape)
        drawn = base * np.exp(spread * noise) if base else spread * noise
        out[name] = __import__('jax').numpy.asarray(drawn.astype(out[name].dtype))
    for name, factor in factors.items():
        out[name] = (out[name] * factor).astype(out[name].dtype)
    return out
```

```python
from contextlib import ExitStack

import numpy as np
import concourse.bass as bass
from concourse import mybir

F32 = mybir.dt.float32
I32 = mybir.dt.int32
ALU = mybir.AluOpType
ACT = mybir.ActivationFunctionType
AX = mybir.AxisListType

P = 128
T = 256
NT = T // P
D = 1024
KC = D // P
LAYERS = 2
HEADS, HD = 16, 64
PAIRS = HEADS // 2
FF = 2816
UPS = FF // 256
FC = FF // P
STEP = 4096
DOWNS = -(-FC // 4)
RING = 3
GROUPS = 3
MODQ = 18
EPS, LN_EPS = 1e-6, 1e-5
ROPE_HALF = 8
NH = 4
CMP_LEN, CMP_STRIDE = 32, 16
NCMP = (T - CMP_LEN) // CMP_STRIDE + 1
TAPS = 31
C2 = 256
POOLS = (2, 4, 8, 16)
FAR = 1.0e30
ROUND = 1.5 * 2.0 ** 23
TWO_PI = (6.28125, 1.93500518798828125e-3, 3.0199159819e-7)

PHASES = [("ffn0", UPS + DOWNS), ("fox", 6), ("fox_out", 2), ("ffn1", UPS + DOWNS),
          ("ffn2", UPS + DOWNS), ("dil", 6 * GROUPS), ("dil_out", 2), ("ffn3", UPS + DOWNS),
          ("mix0", 4), ("mix0_out", 2), ("ffn4", UPS + DOWNS),
          ("mix1", 4), ("mix1_out", 2), ("ffn5", UPS + DOWNS)]
BASE, STEPS = {}, 0
for _name, _n in PHASES:
    BASE[_name] = STEPS
    STEPS += _n

COLS, NCOLS = {}, 0
for _name, _n in [("mod_b", LAYERS * 72), ("norm_g", LAYERS * 24), ("mix_pre", LAYERS * 8), ("ffn_pre", LAYERS * 8),
                  ("conv_w", LAYERS * TAPS * 2), ("conv_b", LAYERS * 2), ("conv_g", LAYERS * 2), ("conv_lb", LAYERS * 2),
                  ("pool_s", LAYERS * 2), ("fc_w", LAYERS * 3 * 44), ("fc_b", LAYERS * 44), ("sgu_b", LAYERS * 4),
                  ("c", KC)]:
    COLS[_name] = NCOLS
    NCOLS += _n

ROWS, NROWS = {}, 0
for _name, _n in [("fox_q", HD), ("fox_k", HD), ("dil_q", GROUPS * HD), ("dil_k", GROUPS * HD), ("b_f", HEADS), ("inv_freq", ROPE_HALF)]:
    ROWS[_name] = NROWS
    NROWS += _n

KONST, NKONST = {}, 0
for _name, _n in [("ident", P), ("ones", P), ("ntri", T), ("eps", 1), ("ln_eps", 1), ("causal", T + P), ("dil", GROUPS * (T + P))]:
    KONST[_name] = NKONST
    NKONST += _n
KONST2, NKONST2 = {}, 0
for _name, _n in [("pool", 4 * (T + P)), ("nsa1", 2 * T), ("nsa0", 2 * P + 2 * NCMP), ("cos", 64), ("sin", 64),
                  ("mean", P), ("late", 1)]:
    KONST2[_name] = NKONST2
    NKONST2 += _n
NSA_W = 2 * CMP_LEN * HD + 2 * HD + 2 * CMP_LEN
MIX_W = 4 * P + 2 * HD + 2 * C2


class Tick:

    def __init__(self, eng, sem):
        self.eng, self.sem, self.n, self.it, self.per, self.start = eng, sem, 0, None, 0, 0

    def mark(self, ins):
        ins.then_inc(self.sem, 1)
        self.n += 1

    def settle(self, back=0):
        v = self.n - back
        self.eng.wait_ge(self.sem, v if self.it is None else self.it * self.per + v)

    def enter(self, it, per):
        self.it, self.per, self.start = it, per, self.n

    def leave(self, turns):
        assert self.n - self.start == self.per, (self.n - self.start, self.per)
        self.it, self.n = None, self.start + turns * self.per


def build(nc, a, out):
    ctx = ExitStack()
    with ctx:
        def sb(name, shape, dt=F32):
            return ctx.enter_context(nc.sbuf_tensor(name, shape, dt))

        def sem(name):
            return ctx.enter_context(nc.semaphore(name))

        ring = sb("ring", [P, RING, STEP])
        x = sb("x", [P, NT, D])
        xn = sb("xn", [P, NT, D])
        hT = sb("hT", [P, KC, T])
        hidT = sb("hidT", [P, FC * T])
        gate = sb("gate", [P, 3, D])
        wa, wb, wc = sb("wa", [P, 1024]), sb("wb", [P, 1024]), sb("wc", [P, 1024])
        arena = sb("arena", [P, 18432])
        cols = sb("cols", [P, NCOLS])
        rows = sb("rows", [P, NROWS])
        konst = sb("konst", [P, NKONST])
        wf = sb("wf", [P, KC, HEADS])
        pos = sb("pos", [P, NT], I32)
        cact = sb("cact", [P, KC])
        modcol = sb("modcol", [P, 3, 2, KC])
        ms, rms, rstd = sb("ms", [P, 4]), sb("rms", [P, 4]), sb("rstd", [P, 4])
        ss16, rs16 = sb("ss16", [P, 16]), sb("rs16", [P, 16])
        nmax, lsum, rsum = sb("nmax", [P, 2, 8]), sb("lsum", [P, 4, 8]), sb("rsum", [P, 2, 8])
        rope = sb("rope", [P, 2, NT, ROPE_HALF])
        rtmp = sb("rtmp", [P, 4, NT * ROPE_HALF])
        flog = sb("flog", [P, 4, NT * HEADS])
        ncum = sb("ncum", [HEADS, T])
        gt = sb("gt", [P, NT, 3 * NH])
        ps = ctx.enter_context(nc.psum_tensor("ps", [P, 8, 512], F32))
        psf = ps[:, :, :].rearrange("p b n -> p (b n)")

        ident = konst[:, KONST["ident"]:KONST["ident"] + P]
        ones = konst[:, KONST["ones"]:KONST["ones"] + P]
        ntri = konst[:, KONST["ntri"]:KONST["ntri"] + T]
        eps_col, ln_eps_col = [konst[:, KONST[n]:KONST[n] + 1] for n in ("eps", "ln_eps")]

        accs = arena[:, 0:MODQ * 512]
        mring = arena[:, 9216:9216 + STEP].rearrange("p (h n) -> p h n", h=2)
        sel = hidT[0:HEADS, 0:HEADS * P]
        fox_bufs = dict(qT=arena[:, 13312:15360], kT=arena[:, 15360:17408], v=hidT[:, 2048:4096], s=hidT[:, 4096:5632])
        dil_bufs = dict(qT=arena[:, 0:6144], kT=arena[:, 6144:12288], v=arena[:, 12288:18432], s=hidT[:, 0:4608])

        nsaw = arena[0:HD, 0:NSA_W]
        yT = arena[:, 4288:6336].rearrange("p (c t) -> p c t", c=KC)
        k2 = arena[:, 6336:6336 + NKONST2]
        a0 = 6336 + NKONST2
        mixw = arena[:, a0:a0 + MIX_W]
        a0 += MIX_W
        cq = arena[:, a0:a0 + 1024].rearrange("p (t n) -> p t n", t=NT)
        rot = arena[:, a0 + 1024:a0 + 1792].rearrange("p (t n) -> p t n", t=NT)
        qkT = arena[0:HD, a0 + 1792:a0 + 1792 + 12 * T]
        a0 += 1792 + 12 * T
        dv = arena[:, a0:a0 + 768].rearrange("p (t n) -> p t n", t=NT)
        blk = arena[0:HD, a0 + 768:a0 + 768 + 2 * CMP_LEN * NCMP].rearrange("p (w l n) -> p w l n", w=2, l=CMP_LEN)
        a0 += 768 + 2 * CMP_LEN * NCMP
        hid = arena[0:HD, a0:a0 + 32]
        kcT = arena[0:HD, a0 + 32:a0 + 32 + NCMP]
        vc = arena[0:NCMP, a0 + 64:a0 + 128]
        pT = arena[:, a0 + 128:a0 + 640]
        zg = wa[:, :].rearrange("p (t n) -> p t n", t=NT)
        vn = wb[:, 0:512].rearrange("p (t n) -> p t n", t=NT)
        bnst = arena[:, a0 + 640:a0 + 656]
        lnv = arena[:, a0 + 656:a0 + 664]
        assert a0 + 664 <= 18432, a0
        CVW = TAPS - 1 + T
        cv = hidT[:, 0:2 * CVW].rearrange("p (c t) -> p c t", c=2)
        cacc = hidT[:, 572:1084].rearrange("p (c t) -> p c t", c=2)
        cd = hidT[:, 1084:1596].rearrange("p (c t) -> p c t", c=2)
        csq = hidT[:, 1596:2108].rearrange("p (c t) -> p c t", c=2)
        NS1, NS0 = 2 * T, 2 * P + 2 * NCMP
        nsaS = hidT[:, 2108:2108 + NS1 + NS0]
        nsaP = [hidT[:, 2908 + i * 800:2908 + i * 800 + NS1 + NS0] for i in range(2)]
        nsaT = hidT[:, 4508:5532]
        ysg = wc[:, 512:1024].rearrange("p (t n) -> p t n", t=NT)
        ac = wc[:, 0:512].rearrange("p (t n) -> p t n", t=NT)
        osm = xn[:, 0, 0:512].rearrange("p (t n) -> p t n", t=NT)

        slot_full = [sem(f"slot_full{i}") for i in range(RING)]
        step_done = sem("step_done")
        konst_in, late_in, gate_in, mix_in = sem("konst_in"), sem("late_in"), sem("gate_in"), sem("mix_in")
        mod_in = [sem(f"mod_in{i}") for i in range(2)]
        half_done = sem("half_done")
        col_sum, col_ready = sem("col_sum"), sem("col_ready")
        gate_sum, gate_ready = sem("gate_sum"), sem("gate_ready")
        cact_ready = sem("cact_ready")
        dve_tick, act_tick = sem("dve_tick"), sem("act_tick")
        x_ready = sem("x_ready")
        ms_ready, xn_ready, norm_T, hT_dve, hT_act = sem("ms_ready"), sem("xn_ready"), sem("norm_T"), sem("hT_dve"), sem("hT_act")
        silu_ready, h_ready, tr_done, tr_copied = sem("silu_ready"), sem("h_ready"), sem("tr_done"), sem("tr_copied")
        gu_ready, fconv_ready, gelu_ready = sem("gu_ready"), sem("fconv_ready"), sem("gelu_ready")
        ang_ready, rope_ready = sem("ang_ready"), sem("rope_ready")
        f_sum, f_abs, f_ln, lf_ready, cum_sum, cum_ready = [sem(n) for n in ("f_sum", "f_abs", "f_ln", "lf_ready", "cum_sum", "cum_ready")]
        sq_ready, ss_ready, rs_ready, qk_read, qn_ready, qk_T, qk_copied, v_copied = [sem(n) for n in ("sq_ready", "ss_ready", "rs_ready", "qk_read", "qn_ready", "qk_T", "qk_copied", "v_copied")]
        s_done, max_ready, exp_ready, p_T, pT_dve, pT_act, o_sum, o_ready = [
            sem(n) for n in ("s_done", "max_ready", "exp_ready", "p_T", "pT_dve", "pT_act", "o_sum", "o_ready")]
        o_T, oT_dve, oT_act = sem("o_T"), sem("oT_dve"), sem("oT_act")
        a_sig, a_gated, a_T, cv_ready, c_copied, d_copied, b_gelu = [sem(n) for n in ("a_sig", "a_gated", "a_T", "cv_ready", "c_copied", "d_copied", "b_gelu")]
        rot_ready, conv_ready, q_T, qkT_ready, blk_ready = [sem(n) for n in ("rot_ready", "conv_ready", "q_T", "qkT_ready", "blk_ready")]
        hid_sum, hid_ready, kv_sum, kv_ready = [sem(n) for n in ("hid_sum", "hid_ready", "kv_sum", "kv_ready")]
        pool_sum, pool_copied, pool_mix, pool_out = [sem(n) for n in ("pool_sum", "pool_copied", "pool_mix", "pool_out")]
        vn_ready, sgu_sum, sgu_ready, sgu_T, sgu_out = [sem(n) for n in ("vn_ready", "sgu_sum", "sgu_ready", "sgu_T", "sgu_out")]
        ns_done, nmax_ready, nexp_ready, np_ready, np_T, npT_copied, no_sum, no_copied, no_T, no_out = [
            sem(n) for n in ("ns_done", "nmax_ready", "nexp_ready", "np_ready", "np_T", "npT_copied", "no_sum", "no_copied", "no_T", "no_out")]
        mu_sum, cd_ready, csq_ready, var_sum, cn_ready, conv_out = [sem(n) for n in ("mu_sum", "cd_ready", "csq_ready", "var_sum", "cn_ready", "conv_out")]
        yms_ready, zvar_ready, zstd_ready, cstd_ready = [sem(n) for n in ("yms_ready", "zvar_ready", "zstd_ready", "cstd_ready")]
        stored = sem("stored")

        def pair(n):
            return 2 * (n % RING)

        block = ctx.enter_context(nc.Block())

        @block.sync
        def _(sp):
            for n in range(RING):
                sp.dma_start(ring[:, n, :], a["stream"][n, :, :]).then_inc(slot_full[n], 16)
            whole = STEPS // RING
            with sp.Fori(1, whole) as i:
                for r in range(RING):
                    sp.wait_ge(step_done, i * RING + (r - RING + 1))
                    sp.dma_start(ring[:, r, :], a["stream"][i * RING + r, :, :]).then_inc(slot_full[r], 16)
            for n in range(whole * RING, STEPS):
                sp.wait_ge(step_done, n - RING + 1)
                sp.dma_start(ring[:, n % RING, :], a["stream"][n, :, :]).then_inc(slot_full[n % RING], 16)
            for tt in range(NT):
                sp.wait_ge(x_ready, 2 * 9 + tt + 1)
                sp.dma_start(out[tt * P:(tt + 1) * P, :], x[:, tt, :]).then_inc(stored, 16)
            sp.wait_ge(stored, 16 * NT)

        @block.gpsimd
        def _(pool):
            def wide(r, s, n):
                return pool.dma_start(gate[:, s:s + n, :].rearrange("p s n -> p (s n)"),
                                      a["wide"][r:r + n, :].rearrange("s n -> (s n)").partition_broadcast(P))

            pool.dma_start(cols[:, :], a["cols"]).then_inc(konst_in, 16)
            for h in range(2):
                pool.dma_start(mring[:, h, :], a["mod"][0, :, h * 2048:(h + 1) * 2048]).then_inc(mod_in[h], 16)
            pool.dma_start(konst[:, :], a["konst"]).then_inc(konst_in, 16)
            pool.dma_start(x[:, :, :], a["x"]).then_inc(konst_in, 16)
            pool.dma_start(rows[:, :], a["rows"].partition_broadcast(P)).then_inc(konst_in, 16)
            pool.dma_start(wf[:, :, :], a["wf"]).then_inc(konst_in, 16)
            pool.dma_start(pos[:, :], a["pos"]).then_inc(konst_in, 16)
            wide(0, 0, 3).then_inc(konst_in, 16)

            def mod_loads(first, end):
                with pool.Fori(first, end) as q:
                    for h in range(2):
                        pool.wait_ge(half_done, q * 2 + (h - 1))
                        pool.dma_start(mring[:, h, :], a["mod"][q, :, h * 2048:(h + 1) * 2048]).then_inc(mod_in[h], 16)

            mod_loads(1, MODQ + 1)
            pool.wait_ge(x_ready, 2)
            pool.dma_start(sel, a["sel"]).then_inc(late_in, 16)
            mod_loads(MODQ + 1, 2 * MODQ)
            pool.wait_ge(x_ready, 6)
            wide(3, 0, 3).then_inc(gate_in, 16)
            pool.wait_ge(x_ready, 10)
            pool.dma_start(k2, a["konst2"]).then_inc(mix_in, 16)
            pool.dma_start(nsaw, a["nsaw"][0, :, :]).then_inc(mix_in, 16)
            pool.dma_start(mixw, a["mixw"][0, :, :]).then_inc(mix_in, 16)
            pool.wait_ge(x_ready, 12)
            wide(6, 0, 3).then_inc(gate_in, 16)
            pool.wait_ge(x_ready, 14)
            wide(9, 0, 1).then_inc(gate_in, 16)
            pool.dma_start(nsaw, a["nsaw"][1, :, :]).then_inc(mix_in, 16)
            pool.dma_start(mixw, a["mixw"][1, :, :]).then_inc(mix_in, 16)

        def val(it, c):
            return c if it is None else it * RING + c

        PEEL, TURNS = UPS % RING, UPS // RING

        @block.tensor
        def _(pe):
            def take(n, it=None, turn=1):
                need = 16 * (n // RING + 1)
                pe.wait_ge(slot_full[n % RING], need if it is None else it * (16 * turn) + need)

            def up(n):
                for tt in range(NT):
                    for k in range(KC):
                        mm = nc.tensor.matmul(ps[:, pair(n) + tt, :], hT[:, k, tt * P:(tt + 1) * P],
                                              ring[:, n % RING, k * 512:(k + 1) * 512], start=(k == 0), stop=(k == KC - 1))
                mm.then_inc(step_done, 1)

            def down(n, lhs, first, last, count, bank):
                for kk in range(count):
                    for tt in range(NT):
                        for half in range(2):
                            mm = nc.tensor.matmul(ps[:, bank + 2 * tt + half, :], lhs(kk, tt),
                                                  ring[:, n % RING, kk * D + half * 512:kk * D + (half + 1) * 512],
                                                  start=(first and kk == 0), stop=(last and kk == count - 1))
                mm.then_inc(step_done, 1)

            def norm(m):
                if m in (0, 1, 3):
                    pe.wait_ge(col_ready, {0: 1, 1: 2, 3: 3}[m])
                for tt in range(NT):
                    pe.wait_ge(xn_ready, 2 * m + tt + 1)
                for b in range(4):
                    for cc in range(2):
                        for tt in range(NT):
                            c = 2 * b + cc
                            mm = nc.tensor.transpose(ps[:, 4 + b, cc * T + tt * P:cc * T + (tt + 1) * P],
                                                     xn[:, tt, c * P:(c + 1) * P], ident)
                    mm.then_inc(norm_T, 1)
                pe.wait_ge(hT_dve, m + 1)
                pe.wait_ge(hT_act, m + 1)

            def mod_cols(layer, subs):
                pe.wait_ge(half_done, 2 * (MODQ * layer + 6 * subs[-1] + 4))
                for s in subs:
                    for kind in range(2):
                        for c in range(KC):
                            o = (6 * s + 2 * kind) * 512 + c * P
                            at = (s * 2 + kind) * KC + c
                            mm = nc.tensor.matmul(ps[:, 7, at:at + 1], accs[:, o:o + P], ones[:, 0:1], start=True, stop=True)
                mm.then_inc(col_sum, 1)

            def gates(layer, subs):
                pe.wait_ge(half_done, 2 * (MODQ * layer + 6 * subs[-1] + 6))
                for s in subs:
                    for half in range(2):
                        g = 6 * layer + 2 * s + half
                        if g >= 2:
                            pe.wait_ge(gate_ready, g - 1)
                        o = (6 * s + 4 + half) * 512
                        nc.tensor.matmul(ps[:, 6 + half, :], ones, accs[:, o:o + 512], start=True, stop=True).then_inc(gate_sum, 1)

            def ffn(f, conv):
                n0 = BASE[f"ffn{f}"]
                v0 = UPS * (f - 4) if conv else UPS * f

                def turn_hidden(j, it):
                    u, v = UPS * f + j, v0 + j
                    pe.wait_ge(tr_copied, val(it, u))
                    if conv:
                        pe.wait_ge(gu_ready, val(it, v + 1))
                        for c in range(4):
                            for tt in range(NT):
                                o = (c % 2) * T + tt * P
                                mm = nc.tensor.transpose(ps[:, 6 + c // 2, o:o + P], wa[:, tt * 512 + c * P:tt * 512 + (c + 1) * P], ident)
                    else:
                        pe.wait_ge(h_ready, val(it, v + 1))
                        for c in range(2):
                            for tt in range(NT):
                                o = c * T + tt * P
                                mm = nc.tensor.transpose(ps[:, 6, o:o + P], wb[:, tt * C2 + c * P:tt * C2 + (c + 1) * P], ident)
                    mm.then_inc(tr_done, 1)

                def step(j, it):
                    n = n0 + j
                    take(n, it)
                    if v0 + j >= RING:
                        pe.wait_ge(gu_ready if conv else h_ready, val(it, v0 + j - RING + 1))
                    up(n)
                    if j > 0:
                        turn_hidden(j - 1, it)

                ahead = 1 if v0 == 0 else 0
                for j in range(PEEL + ahead * RING):
                    step(j, None)
                with pe.Fori(ahead, TURNS) as it:
                    for r in range(RING):
                        step(PEEL + r, it)
                turn_hidden(UPS - 1, None)
                pe.wait_ge(tr_copied, UPS * (f + 1))
                if f in (0, 2):
                    gates(f // 2, [0] if f == 0 else [0, 1, 2])
                for d in range(DOWNS):
                    n = n0 + UPS + d
                    take(n)
                    down(n, lambda kk, tt: hidT[:, (4 * d + kk) * T + tt * P:(4 * d + kk) * T + (tt + 1) * P],
                         d == 0, d == DOWNS - 1, min(4, FC - 4 * d), 0)

            def qkv(n0, z0, w0, turns, groups):
                def turn_qk(z, it):
                    pe.wait_ge(qn_ready, z + 1 if it is None else it * 4 + (z + 1))
                    pe.wait_ge(qk_copied, z if it is None else it * 4 + z)
                    for pr in range(4):
                        for tt in range(NT):
                            o = (pr % 2) * T + tt * P
                            mm = nc.tensor.transpose(ps[:, 6 + pr // 2, o:o + P], wb[:, tt * 512 + pr * P:tt * 512 + (pr + 1) * P], ident)
                    mm.then_inc(qk_T, 1)

                def group(it):
                    def at(c, per):
                        return c if it is None else it * per + c
                    for j in range(6):
                        take(n0 + j, it, 2)
                        if j in (0, 4, 5):
                            pe.wait_ge(qk_read, at(z0 + {0: 0, 4: 2, 5: 3}[j], 4))
                        elif j == 3:
                            pe.wait_ge(qk_read, at(z0 + 1, 4))
                        else:
                            pe.wait_ge(v_copied, at(w0, 2))
                        up(n0 + j)
                        if 1 <= j <= 4:
                            turn_qk(z0 + j - 1, it)

                if groups == 1:
                    group(None)
                else:
                    with pe.Fori(0, groups) as it:
                        group(it)

            def attention(G, a_0, qk_all, v_all, bufs, cum):
                SW = G * (T + P)
                prob = [bufs["s"][:, SW * (1 + i):SW * (2 + i)] for i in range(2)]
                probT = bufs["s"][:, 3 * SW:4 * SW]
                pe.wait_ge(qk_copied, qk_all)
                pe.wait_ge(v_copied, v_all)
                if cum:
                    pe.wait_ge(cum_ready, 1)
                    pe.wait_ge(late_in, 16)

                def scores(h):
                    q0 = (h % 2) * HD
                    if h > 0:
                        pe.wait_ge(max_ready, a_0 + h)
                    for tile, at, keys in ((1, 0, T), (0, 1024, P)):
                        for g in range(G):
                            o = at + g * keys
                            col = g * PAIRS * T + (h // 2) * T
                            mm = nc.tensor.matmul(psf[:, o:o + keys], bufs["qT"][q0:q0 + HD, col + tile * P:col + tile * P + P],
                                                  bufs["kT"][q0:q0 + HD, col:col + keys], start=True, stop=not cum)
                            if cum:
                                mm = nc.tensor.matmul(psf[:, o:o + keys], sel[:, h * P:(h + 1) * P], ncum[:, 0:keys],
                                                      start=False, stop=True)
                    mm.then_inc(s_done, 1)

                def turn_probs(h):
                    pe.wait_ge(exp_ready, a_0 + h + 1)
                    pe.wait_ge(pT_dve, a_0 + h)
                    if G > 1:
                        pe.wait_ge(pT_act, h)
                    for b in range(3 * G):
                        mm = nc.tensor.transpose(psf[:, 1536 + b * P:1536 + (b + 1) * P], prob[h % 2][:, b * P:(b + 1) * P], ident)
                    mm.then_inc(p_T, 1)

                def values(h):
                    pe.wait_ge(pT_dve, a_0 + h + 1)
                    if G > 1:
                        pe.wait_ge(pT_act, h + 1)
                    if h >= 2:
                        pe.wait_ge(o_ready, a_0 + h - 1)
                    o = (6 + h % 2) * 512

                    def v(g, tile):
                        return bufs["v"][:, g * 2048 + tile * D + h * HD:g * 2048 + tile * D + (h + 1) * HD]
                    for i in range(2 * G):
                        nc.tensor.matmul(psf[:, o + HD:o + 2 * HD], probT[:, i * P:(i + 1) * P], v(i // 2, i % 2),
                                         start=(i == 0), stop=(i == 2 * G - 1))
                    for i in range(G):
                        mm = nc.tensor.matmul(psf[:, o:o + HD], probT[:, (2 * G + i) * P:(2 * G + i + 1) * P], v(i, 0),
                                              start=(i == 0), stop=(i == G - 1))
                    mm.then_inc(o_sum, 1)

                for h in range(HEADS + 2):
                    if h < HEADS:
                        scores(h)
                    if 1 <= h <= HEADS:
                        turn_probs(h - 1)
                    if h >= 2:
                        values(h - 2)

            def attention_out(name, a_0, k):
                pe.wait_ge(o_ready, a_0 + HEADS)
                for b in range(4):
                    for cc in range(2):
                        for tt in range(NT):
                            c = 2 * b + cc
                            mm = nc.tensor.transpose(ps[:, b, cc * T + tt * P:cc * T + (tt + 1) * P], xn[:, tt, c * P:(c + 1) * P], ident)
                    mm.then_inc(o_T, 1)
                pe.wait_ge(oT_dve, k + 1)
                pe.wait_ge(oT_act, k + 1)
                for d in range(2):
                    n = BASE[name] + d
                    take(n)
                    down(n, lambda kk, tt: hT[:, 4 * d + kk, tt * P:(tt + 1) * P], d == 0, d == 1, 4, 4)

            def mixer(l):
                n0 = BASE[f"mix{l}"]
                bA, bC, bD = pair(n0), pair(n0 + 1), pair(n0 + 2)
                for j in range(3):
                    take(n0 + j)
                    up(n0 + j)
                pe.wait_ge(a_gated, l + 1)
                for c in range(2):
                    for tt in range(NT):
                        o = c * T + tt * P
                        mm = nc.tensor.transpose(ps[:, 6, o:o + P], ac[:, tt, c * P:(c + 1) * P], ident)
                mm.then_inc(a_T, 1)
                take(n0 + 3)
                up(n0 + 3)
                pe.wait_ge(rot_ready, l + 1)
                pe.wait_ge(c_copied, l + 1)
                pe.wait_ge(d_copied, l + 1)
                pe.wait_ge(cv_ready, l + 1)
                banks = [bC, bC + 1, bD, bD + 1, 6, 7]
                for b in range(12):
                    for tt in range(NT):
                        src = rot[:, tt, b * HD:(b + 1) * HD] if b < 6 else cq[:, tt, (384 + (b - 6) * HD if b < 8 else (b - 8) * HD):][:, 0:HD]
                        o = (b % 2) * T + tt * P
                        mm = nc.tensor.transpose(ps[0:HD, banks[b // 2], o:o + P], src, ident)
                mm.then_inc(q_T, 1)
                pe.wait_ge(mix_in, 48 + 32 * l)
                pe.wait_ge(blk_ready, l + 1)
                for w in range(2):
                    for e in range(CMP_LEN):
                        o = w * CMP_LEN * HD + e * HD
                        mm = nc.tensor.matmul(ps[0:HD, 6, w * 16:w * 16 + NCMP], nsaw[:, o:o + HD], blk[:, w, e, :],
                                              start=(e == 0), stop=(e == CMP_LEN - 1))
                mm.then_inc(hid_sum, 1)
                for g in range(4):
                    o = KONST2["pool"] + g * (T + P)
                    h0 = (g % 2) * HD
                    dst = ps[h0:h0 + HD, 7, (g // 2) * T:(g // 2) * T + T]
                    nc.tensor.matmul(dst, dv[:, 0, g * HD:(g + 1) * HD], k2[:, o:o + T], start=True, stop=False)
                    mm = nc.tensor.matmul(dst[:, P:T], dv[:, 1, g * HD:(g + 1) * HD], k2[:, o + T:o + T + P], start=False, stop=True)
                mm.then_inc(pool_sum, 1)
                pe.wait_ge(hid_ready, l + 1)
                o = 2 * CMP_LEN * HD
                nc.tensor.matmul(ps[0:HD, 6, 32:32 + NCMP], nsaw[:, o:o + HD], hid[:, 0:NCMP], start=True, stop=True)
                nc.tensor.matmul(ps[0:NCMP, 6, 64:64 + HD], hid[:, 16:16 + NCMP], nsaw[:, o + HD:o + 2 * HD], start=True, stop=True).then_inc(kv_sum, 1)
                pe.wait_ge(pool_copied, l + 1)
                for g in range(4):
                    h0 = (g % 2) * HD
                    mm = nc.tensor.matmul(ps[h0:h0 + HD, 7, (g // 2) * T:(g // 2) * T + T],
                                          mixw[h0:h0 + HD, 4 * P + (g // 2) * HD:4 * P + (g // 2 + 1) * HD],
                                          pT[h0:h0 + HD, (g // 2) * T:(g // 2) * T + T], start=True, stop=True)
                mm.then_inc(pool_mix, 1)
                pe.wait_ge(vn_ready, l + 1)
                pe.wait_ge(kv_ready, l + 1)
                for tt in range(NT):
                    for g in range(4):
                        mm = nc.tensor.matmul(ps[:, 6, tt * C2 + g * HD:tt * C2 + (g + 1) * HD], mixw[:, g * P:(g + 1) * P],
                                              vn[:, tt, g * HD:(g + 1) * HD], start=True, stop=True)
                mm.then_inc(sgu_sum, 1)

                def scores(h):
                    i = NH * l + h
                    if h > 0:
                        pe.wait_ge(nmax_ready, i)
                    qr, qc = h * T, (8 + h) * T
                    for tile, keys, b in ((1, T, bC), (0, P, bC + 1)):
                        for w in range(2):
                            nc.tensor.matmul(ps[:, b, w * keys:(w + 1) * keys], qkT[:, qr + tile * P:qr + (tile + 1) * P],
                                             qkT[:, (4 + w) * T:(4 + w) * T + keys], start=True, stop=True)
                    for tile in range(NT):
                        o = 2 * P + tile * NCMP
                        mm = nc.tensor.matmul(ps[:, bC + 1, o:o + NCMP], qkT[:, qc + tile * P:qc + (tile + 1) * P], kcT,
                                              start=True, stop=True)
                    mm.then_inc(ns_done, 1)

                def turn_probs(h):
                    i = NH * l + h
                    pe.wait_ge(np_ready, i + 1)
                    pe.wait_ge(npT_copied, i)
                    pr = nsaP[h % 2]
                    for b in range(6):
                        o = b * P
                        nc.tensor.transpose(ps[:, bD + b // 4, (b % 4) * P:(b % 4 + 1) * P], pr[:, o:o + P], ident)
                    for tile in range(NT):
                        o = NS1 + 2 * P + tile * NCMP
                        mm = nc.tensor.transpose(ps[0:NCMP, bD + 1, 2 * P + tile * P:2 * P + (tile + 1) * P], pr[:, o:o + NCMP], ident)
                    mm.then_inc(np_T, 1)

                def values(h):
                    i = NH * l + h
                    pe.wait_ge(npT_copied, i + 1)
                    if h == 0:
                        pe.wait_ge(pool_out, l + 1)
                    vs = lambda w, tile: dv[:, tile, C2 + w * HD:C2 + (w + 1) * HD]
                    for b in range(4):
                        nc.tensor.matmul(ps[:, 7, h * P + HD:h * P + 2 * HD], nsaT[:, b * P:(b + 1) * P], vs(b // 2, b % 2), start=(b == 0), stop=False)
                    nc.tensor.matmul(ps[:, 7, h * P + HD:h * P + 2 * HD], nsaT[0:NCMP, 7 * P:8 * P], vc, start=False, stop=True)
                    for w in range(2):
                        nc.tensor.matmul(ps[:, 7, h * P:h * P + HD], nsaT[:, (4 + w) * P:(5 + w) * P], vs(w, 0), start=(w == 0), stop=False)
                    nc.tensor.matmul(ps[:, 7, h * P:h * P + HD], nsaT[0:NCMP, 6 * P:7 * P], vc, start=False, stop=True).then_inc(no_sum, 1)

                for h in range(NH + 2):
                    if h < NH:
                        scores(h)
                    if 1 <= h <= NH:
                        turn_probs(h - 1)
                    if h >= 2:
                        values(h - 2)
                pe.wait_ge(conv_ready, l + 1)
                pe.wait_ge(b_gelu, l + 1)
                mean = k2[:, KONST2["mean"]:KONST2["mean"] + P]
                for c in range(2):
                    mm = nc.tensor.matmul(ps[:, bA, 0:T], mean, cacc[:, c, :], start=(c == 0), stop=(c == 1))
                mm.then_inc(mu_sum, 1)
                pe.wait_ge(csq_ready, l + 1)
                for c in range(2):
                    mm = nc.tensor.matmul(ps[:, bA + 1, 0:T], mean, csq[:, c, :], start=(c == 0), stop=(c == 1))
                mm.then_inc(var_sum, 1)
                pe.wait_ge(sgu_ready, l + 1)
                for c in range(2):
                    for tt in range(NT):
                        mm = nc.tensor.transpose(ps[:, 6, c * T + tt * P:c * T + (tt + 1) * P], ysg[:, tt, c * P:(c + 1) * P], ident)
                mm.then_inc(sgu_T, 1)
                pe.wait_ge(no_copied, l + 1)
                for c in range(2):
                    for tt in range(NT):
                        mm = nc.tensor.transpose(ps[:, 7, c * T + tt * P:c * T + (tt + 1) * P], osm[:, tt, c * P:(c + 1) * P], ident)
                mm.then_inc(no_T, 1)
                for s in (sgu_out, no_out, conv_out):
                    pe.wait_ge(s, l + 1)
                for d in range(2):
                    n = BASE[f"mix{l}_out"] + d
                    take(n)
                    down(n, lambda kk, tt: yT[:, 4 * d + kk, tt * P:(tt + 1) * P], d == 0, d == 1, 4, 4)

            pe.wait_ge(konst_in, 16 * 7)
            mod_cols(0, [0])
            norm(0)
            ffn(0, False)
            pe.wait_ge(gate_ready, 2)
            mod_cols(0, [1, 2])
            norm(1)
            gates(0, [1, 2])
            pe.wait_ge(gate_ready, 6)
            for tt in range(NT):
                for k in range(KC):
                    mm = nc.tensor.matmul(ps[:, 6, tt * HEADS:(tt + 1) * HEADS], hT[:, k, tt * P:(tt + 1) * P], wf[:, k, :],
                                          start=(k == 0), stop=(k == KC - 1))
            mm.then_inc(f_sum, 1)
            pe.wait_ge(lf_ready, 1)
            lf = flog[:, 3, :]
            nc.tensor.matmul(ps[0:HEADS, 7, 0:T], lf[:, 0:HEADS], ntri, start=True, stop=False)
            nc.tensor.matmul(ps[0:HEADS, 7, P:T], lf[:, HEADS:2 * HEADS], ntri[:, 0:P], start=False, stop=True).then_inc(cum_sum, 1)
            pe.wait_ge(cum_ready, 1)
            qkv(BASE["fox"], 0, 0, 1, 1)
            attention(1, 0, 4, 2, fox_bufs, True)
            attention_out("fox_out", 0, 0)
            norm(2)
            ffn(1, False)
            mod_cols(1, [0, 1, 2])
            norm(3)
            ffn(2, False)
            norm(4)
            qkv(BASE["dil"], 4, 2, 2, GROUPS)
            attention(GROUPS, HEADS, 4 + 4 * GROUPS, 2 + 2 * GROUPS, dil_bufs, False)
            attention_out("dil_out", HEADS, 1)
            norm(5)
            ffn(3, False)
            for l in range(LAYERS):
                norm(6 + 2 * l)
                mixer(l)
                norm(7 + 2 * l)
                ffn(4 + l, True)

        @block.scalar
        def _(act):
            tick = Tick(act, act_tick)

            def norm(m):
                for tt in range(NT):
                    if m > 0:
                        act.wait_ge(x_ready, 2 * (m - 1) + tt + 1)
                    tick.mark(nc.scalar.activation(xn[:, tt, :], x[:, tt, :], ACT.Square, scale=D ** -0.5, accum_out=ms[:, tt:tt + 1]))
                    tick.settle()
                    nc.scalar.activation(rms[:, tt:tt + 1], ms[:, tt:tt + 1], ACT.Sqrt, bias=eps_col).then_inc(ms_ready, 1)
                if m in (0, 1, 3):
                    act.wait_ge(col_ready, {0: 1, 1: 2, 3: 3}[m])
                for b in (1, 3):
                    act.wait_ge(norm_T, 4 * m + b + 1)
                    for cc in range(2):
                        c = 2 * b + cc
                        src = ps[:, 4 + b, cc * T:(cc + 1) * T]
                        if m < 6:
                            ins = nc.scalar.activation(hT[:, c, :], src, ACT.Identity, bias=modcol[:, m % 3, 0, c:c + 1],
                                                       scale=modcol[:, m % 3, 1, c:c + 1])
                        else:
                            g = (COLS["mix_pre"] if m % 2 == 0 else COLS["ffn_pre"]) + 8 * ((m - 6) // 2) + c
                            ins = nc.scalar.activation(hT[:, c, :], src, ACT.Copy, scale=cols[:, g:g + 1])
                ins.then_inc(hT_act, 1)

            def ffn(f):
                n0 = BASE[f"ffn{f}"]

                def step(j, it):
                    u = UPS * f + j
                    act.wait_ge(step_done, val(it, n0 + j + 1))
                    act.wait_ge(h_ready, val(it, u))
                    nc.scalar.activation(wa[:, 0:512].rearrange("p (t n) -> p t n", t=NT), ps[:, pair(n0 + j):pair(n0 + j) + 2, 0:C2],
                                         ACT.Silu).then_inc(silu_ready, 1)
                for j in range(PEEL):
                    step(j, None)
                with act.Fori(0, TURNS) as it:
                    for r in range(RING):
                        step(PEEL + r, it)

            def ffn_conv(f):
                n0, v0 = BASE[f"ffn{f}"], UPS * (f - 4)

                def gelu(j, it):
                    v = v0 + j
                    act.wait_ge(fconv_ready, val(it, v + 1))
                    nc.scalar.activation(wc[:, 0:512], wb[:, 0:512], ACT.Gelu_apprx_tanh).then_inc(gelu_ready, 1)

                def step(j, it):
                    u = UPS * f + j
                    act.wait_ge(step_done, val(it, n0 + j + 1))
                    act.wait_ge(tr_done, val(it, u))
                    nc.scalar.activation(wa[:, :], psf[:, pair(n0 + j) * 512:(pair(n0 + j) + 2) * 512], ACT.Copy).then_inc(gu_ready, 1)
                    if j > 0:
                        gelu(j - 1, it)
                for j in range(PEEL):
                    step(j, None)
                with act.Fori(0, TURNS) as it:
                    for r in range(RING):
                        step(PEEL + r, it)
                gelu(UPS - 1, None)

            def qkv(n0, z0, w0, bufs, groups):
                def group(it):
                    def at(c, per):
                        return c if it is None else it * per + c

                    def copy_qk(z, j):
                        act.wait_ge(qk_T, at(z + 1, 4))
                        buf = bufs["qT"] if j < 2 else bufs["kT"]
                        o = at((j % 2) * 1024, PAIRS * T)
                        nc.scalar.activation(buf[:, bass.ds(o, 1024)], psf[:, 6 * 512:8 * 512], ACT.Copy).then_inc(qk_copied, 1)

                    for j in range(6):
                        act.wait_ge(step_done, at(n0 + j + 1, 6))
                        b = pair(n0 + j)
                        if j < 4:
                            act.wait_ge(qk_read, at(z0 + j, 4))
                            nc.scalar.activation(wa[:, :], psf[:, b * 512:(b + 2) * 512], ACT.Square, scale=HD ** -0.5).then_inc(sq_ready, 1)
                            act.wait_ge(ss_ready, at(z0 + j + 1, 4))
                            nc.scalar.activation(rs16[:, :], ss16[:, :], ACT.Sqrt, bias=eps_col).then_inc(rs_ready, 1)
                        else:
                            for tt in range(NT):
                                o = at(tt * D + (j - 4) * 512, 2048)
                                ins = nc.scalar.activation(bufs["v"][:, bass.ds(o, 512)], ps[:, b + tt, :], ACT.Copy)
                            ins.then_inc(v_copied, 1)
                        if 1 <= j <= 4:
                            copy_qk(z0 + j - 1, j - 1)
                if groups == 1:
                    group(None)
                else:
                    with act.Fori(0, groups) as it:
                        group(it)

            def attention(G, a_0, bufs):
                SW, S1 = G * (T + P), G * T
                s = bufs["s"]
                prob = [s[:, SW * (1 + i):SW * (2 + i)] for i in range(2)]
                probT = s[:, 3 * SW:4 * SW]
                for h in range(HEADS + 1):
                    if h < HEADS:
                        act.wait_ge(max_ready, a_0 + h + 1)
                        if h >= 2:
                            act.wait_ge(p_T, a_0 + h - 1)
                        for i, (lo, hi) in enumerate(((0, S1), (S1, SW))):
                            ins = nc.scalar.activation(prob[h % 2][:, lo:hi], s[:, lo:hi], ACT.Exp, scale=-1.0,
                                                       bias=nmax[:, h % 2, i:i + 1], accum_out=lsum[:, h % 4, i:i + 1])
                        ins.then_inc(exp_ready, 1)
                    if h >= 1:
                        act.wait_ge(p_T, a_0 + h)
                        if h >= 2:
                            act.wait_ge(o_sum, a_0 + h - 1)
                        if G > 1:
                            nc.scalar.activation(probT[:, 512:1024], psf[:, 2048:2560], ACT.Copy).then_inc(pT_act, 1)

            def attention_out(k):
                for b in (1, 3):
                    act.wait_ge(o_T, 4 * k + b + 1)
                    ins = nc.scalar.activation(hT[:, 2 * b:2 * b + 2, :].rearrange("p c t -> p (c t)"), ps[:, b, :], ACT.Copy)
                ins.then_inc(oT_act, 1)

            def mixer(l):
                n0 = BASE[f"mix{l}"]
                bA, bC, bD = pair(n0), pair(n0 + 1), pair(n0 + 2)
                act.wait_ge(step_done, n0 + 1)
                nc.scalar.activation(wb[:, 0:512].rearrange("p (t n) -> p t n", t=NT), ps[:, bA:bA + 2, C2:2 * C2], ACT.Sigmoid).then_inc(a_sig, 1)
                act.wait_ge(step_done, n0 + 2)
                nc.scalar.activation(cq[:, :, 0:C2], ps[:, bC:bC + 2, 0:C2], ACT.Copy, scale=HD ** -0.5)
                nc.scalar.activation(cq[:, :, C2:512], ps[:, bC:bC + 2, C2:512], ACT.Copy).then_inc(c_copied, 1)
                act.wait_ge(step_done, n0 + 3)
                nc.scalar.activation(gt[:, :, :], ps[:, bD:bD + 2, 384:396], ACT.Sigmoid)
                nc.scalar.activation(dv[:, :, :], ps[:, bD:bD + 2, 0:384], ACT.Copy).then_inc(d_copied, 1)
                act.wait_ge(a_T, l + 1)
                nc.scalar.activation(cv[:, :, TAPS - 1:CVW], ps[:, 6, :].rearrange("p (c t) -> p c t", c=2), ACT.Copy).then_inc(cv_ready, 1)
                act.wait_ge(step_done, n0 + 4)
                act.wait_ge(rot_ready, l + 1)
                nc.scalar.activation(zg[:, :, :], ps[:, bA:bA + 2, :], ACT.Gelu_apprx_tanh).then_inc(b_gelu, 1)
                act.wait_ge(q_T, l + 1)
                for i, b in enumerate((bC, bD, 6)):
                    ins = nc.scalar.activation(qkT[:, i * 1024:(i + 1) * 1024], psf[0:HD, b * 512:(b + 2) * 512], ACT.Copy)
                ins.then_inc(qkT_ready, 1)
                act.wait_ge(hid_sum, l + 1)
                nc.scalar.activation(hid.rearrange("p (w n) -> p w n", w=2)[:, :, 0:NCMP],
                                     ps[0:HD, 6, 0:32].rearrange("p (w n) -> p w n", w=2)[:, :, 0:NCMP], ACT.Gelu_apprx_tanh).then_inc(hid_ready, 1)
                act.wait_ge(zvar_ready, l + 1)
                nc.scalar.activation(lnv[:, 4:6], lnv[:, 0:4].rearrange("p (t w) -> p t w", t=NT)[:, :, 1], ACT.Sqrt, bias=ln_eps_col).then_inc(zstd_ready, 1)
                act.wait_ge(pool_sum, l + 1)
                nc.scalar.activation(pT, ps[:, 7, :], ACT.Copy).then_inc(pool_copied, 1)
                act.wait_ge(pool_mix, l + 1)
                for c in range(2):
                    o = COLS["pool_s"] + 2 * l + c
                    ins = nc.scalar.activation(yT[:, 6 + c, :], ps[:, 7, c * T:(c + 1) * T], ACT.Copy, scale=cols[:, o:o + 1])
                ins.then_inc(pool_out, 1)
                segs = [(0, T), (T, 2 * T), (NS1, NS1 + P), (NS1 + P, NS1 + 2 * P),
                        (NS1 + 2 * P, NS1 + 2 * P + NCMP), (NS1 + 2 * P + NCMP, NS1 + NS0)]
                for h in range(NH + 1):
                    i = NH * l + h
                    if h < NH:
                        act.wait_ge(nmax_ready, i + 1)
                        if h >= 2:
                            act.wait_ge(np_T, i - 1)
                        for k, (lo, hi) in enumerate(segs):
                            ins = nc.scalar.activation(nsaP[h % 2][:, lo:hi], nsaS[:, lo:hi], ACT.Exp, scale=-1.0,
                                                       bias=nmax[:, h % 2, k:k + 1], accum_out=lsum[:, h % 4, k:k + 1])
                        ins.then_inc(nexp_ready, 1)
                    if h >= 1:
                        act.wait_ge(np_T, i)
                        if h >= 2:
                            act.wait_ge(no_sum, i - 1)
                        nc.scalar.activation(nsaT[:, 0:768], psf[:, bD * 512:bD * 512 + 768], ACT.Copy)
                        nc.scalar.activation(nsaT[0:NCMP, 768:1024], ps[0:NCMP, bD + 1, C2:512], ACT.Copy).then_inc(npT_copied, 1)
                act.wait_ge(cd_ready, l + 1)
                nc.scalar.activation(csq[:, :, :], cd[:, :, :], ACT.Square).then_inc(csq_ready, 1)
                act.wait_ge(var_sum, l + 1)
                nc.scalar.activation(wb[:, 0:T], ps[:, bA + 1, 0:T], ACT.Sqrt, bias=ln_eps_col).then_inc(cstd_ready, 1)
                act.wait_ge(sgu_T, l + 1)
                nc.scalar.activation(yT[:, 4:6, :].rearrange("p c t -> p (c t)"), ps[:, 6, :], ACT.Copy).then_inc(sgu_out, 1)
                act.wait_ge(no_T, l + 1)
                nc.scalar.activation(yT[:, 2:4, :].rearrange("p c t -> p (c t)"), ps[:, 7, :], ACT.Copy).then_inc(no_out, 1)
                act.wait_ge(cn_ready, l + 1)
                for c in range(2):
                    g, b = COLS["conv_g"] + 2 * l + c, COLS["conv_lb"] + 2 * l + c
                    ins = nc.scalar.activation(yT[:, c, :], cd[:, c, :], ACT.Silu, scale=cols[:, g:g + 1], bias=cols[:, b:b + 1])
                ins.then_inc(conv_out, 1)

            def post_norm(end, k, bank):
                act.wait_ge(step_done, end)
                for tt in range(NT):
                    o = (bank + 2 * tt) * 512
                    tick.mark(nc.scalar.activation(xn[:, tt, :], psf[:, o:o + D], ACT.Square, scale=D ** -0.5, accum_out=ms[:, 2 + tt:3 + tt]))
                    tick.settle()
                    nc.scalar.activation(rms[:, 2 + tt:3 + tt], ms[:, 2 + tt:3 + tt], ACT.Sqrt, bias=eps_col).then_inc(yms_ready, 1)

            act.wait_ge(konst_in, 16 * 7)
            nc.scalar.activation(cact[:, :], cols[:, COLS["c"]:COLS["c"] + KC], ACT.Silu).then_inc(cact_ready, 1)
            act.wait_ge(ang_ready, 1)
            nc.scalar.activation(rope[:, :, :, :].rearrange("p w t n -> p (w t n)"),
                                 rtmp[:, 0:2, :].rearrange("p w n -> p (w n)"), ACT.Sin).then_inc(rope_ready, 1)
            norm(0)
            ffn(0)
            norm(1)
            act.wait_ge(f_abs, 1)
            tick.mark(nc.scalar.activation(flog[:, 2, :], flog[:, 1, :], ACT.Exp, scale=-1.0))
            tick.settle()
            nc.scalar.activation(flog[:, 3, :], flog[:, 2, :], ACT.Ln, bias=1.0).then_inc(f_ln, 1)
            qkv(BASE["fox"], 0, 0, fox_bufs, 1)
            attention(1, 0, fox_bufs)
            attention_out(0)
            norm(2)
            ffn(1)
            norm(3)
            ffn(2)
            norm(4)
            qkv(BASE["dil"], 4, 2, dil_bufs, GROUPS)
            attention(GROUPS, HEADS, dil_bufs)
            attention_out(1)
            norm(5)
            ffn(3)
            for l in range(LAYERS):
                norm(6 + 2 * l)
                mixer(l)
                post_norm(BASE[f"mix{l}_out"] + 2, 2 * l, 4)
                norm(7 + 2 * l)
                ffn_conv(4 + l)
                post_norm(BASE[f"ffn{4 + l}"] + UPS + DOWNS, 2 * l + 1, 0)

        @block.vector
        def _(dve):
            v = nc.vector
            tick = Tick(dve, dve_tick)

            def col(name, i):
                return cols[:, COLS[name] + i:COLS[name] + i + 1]

            def norm(m):
                for tt in range(NT):
                    dve.wait_ge(ms_ready, 2 * m + tt + 1)
                    tick.mark(v.reciprocal(rstd[:, tt:tt + 1], rms[:, tt:tt + 1]))
                    tick.settle()
                    v.tensor_scalar(xn[:, tt, :], x[:, tt, :], rstd[:, tt:tt + 1], None, ALU.mult).then_inc(xn_ready, 1)
                for b in (0, 2):
                    dve.wait_ge(norm_T, 4 * m + b + 1)
                    for cc in range(2):
                        c = 2 * b + cc
                        src = ps[:, 4 + b, cc * T:(cc + 1) * T]
                        if m < 6:
                            ins = v.tensor_scalar(hT[:, c, :], src, modcol[:, m % 3, 1, c:c + 1], modcol[:, m % 3, 0, c:c + 1], ALU.mult, ALU.add)
                        else:
                            ins = v.tensor_scalar(hT[:, c, :], src, col("mix_pre" if m % 2 == 0 else "ffn_pre", 8 * ((m - 6) // 2) + c), None, ALU.mult)
                ins.then_inc(hT_dve, 1)

            def mod_step(q, big):
                tmp = wc[:, 0:512]
                for h in range(2):
                    dve.wait_ge(mod_in[h], big * 16 + 16)
                    for k in range(4):
                        src, c = mring[:, h, k * 512:(k + 1) * 512], cact[:, 4 * h + k:4 * h + k + 1]
                        if h == 0 and k == 0:
                            tick.mark(v.tensor_scalar(tmp, src, c, None, ALU.mult))
                            continue
                        if h == 1 and k == 0:
                            dve.wait_ge(half_done, big * 2 + 1)
                        else:
                            tick.settle()
                        dst = accs[:, bass.ds(q * 512, 512)] if h == 1 and k == 3 else tmp
                        ins = v.scalar_tensor_tensor(out=dst, in0=src, scalar=c, in1=tmp, op0=ALU.mult, op1=ALU.add)
                        if k == 3:
                            ins.then_inc(half_done, 1)
                        else:
                            tick.mark(ins)
                dve.wait_ge(half_done, big * 2 + 2)

            def mod_loop(layer, first, end):
                with dve.Fori(first, end) as q:
                    tick.enter(q - first, 6)
                    mod_step(q, q + MODQ * layer)
                tick.leave(end - first)

            def mod_cols(layer, subs, k):
                dve.wait_ge(col_sum, k)
                for s in subs:
                    b = COLS["mod_b"] + layer * 72 + s * 24
                    tick.mark(v.tensor_tensor(modcol[:, s, :, :].rearrange("p w c -> p (w c)"), ps[:, 7, s * 16:s * 16 + 16],
                                              cols[:, b:b + 16], ALU.add))
                tick.settle()
                for s in subs:
                    g = COLS["norm_g"] + layer * 24 + s * 8
                    ins = v.scalar_tensor_tensor(out=modcol[:, s, 1, :], in0=modcol[:, s, 1, :], scalar=1.0, in1=cols[:, g:g + 8],
                                                 op0=ALU.add, op1=ALU.mult)
                ins.then_inc(col_ready, 1)
                dve.wait_ge(col_ready, k)

            def gates(layer, subs):
                for s in subs:
                    for half in range(2):
                        dve.wait_ge(gate_sum, 6 * layer + 2 * s + half + 1)
                        g = gate[:, s, half * 512:(half + 1) * 512]
                        v.tensor_tensor(g, ps[:, 6 + half, :], g, ALU.add).then_inc(gate_ready, 1)

            def update(end, s, weight, bank):
                dve.wait_ge(step_done, end)
                w = (wa, wb)
                for tt in range(NT):
                    o = (bank + 2 * tt) * 512
                    tick.mark(v.scalar_tensor_tensor(out=w[tt][:, :], in0=psf[:, o:o + D], scalar=weight, in1=gate[:, s, :],
                                                     op0=ALU.mult, op1=ALU.mult))
                for tt in range(NT):
                    tick.settle(1 - tt)
                    v.tensor_tensor(x[:, tt, :], x[:, tt, :], w[tt][:, :], ALU.add).then_inc(x_ready, 1)

            def update_normed(k, s, bank):
                w = (wa, wb)
                for tt in range(NT):
                    dve.wait_ge(yms_ready, 2 * k + tt + 1)
                    tick.mark(v.reciprocal(rstd[:, 2 + tt:3 + tt], rms[:, 2 + tt:3 + tt]))
                for tt in range(NT):
                    o = (bank + 2 * tt) * 512
                    tick.settle(1)
                    tick.mark(v.scalar_tensor_tensor(out=w[tt][:, :], in0=psf[:, o:o + D], scalar=rstd[:, 2 + tt:3 + tt],
                                                     in1=gate[:, s, :], op0=ALU.mult, op1=ALU.mult))
                for tt in range(NT):
                    tick.settle(1 - tt)
                    v.tensor_tensor(x[:, tt, :], x[:, tt, :], w[tt][:, :], ALU.add).then_inc(x_ready, 1)

            def ffn(f):
                n0 = BASE[f"ffn{f}"]
                q0 = {0: 4, 1: 0}.get(f)

                def keep(j, it):
                    u = UPS * f + j
                    dve.wait_ge(tr_done, val(it, u + 1))
                    o = j * 512 if it is None else it * (RING * 512) + j * 512
                    v.tensor_copy(hidT[:, bass.ds(o, 512)], ps[:, 6, :]).then_inc(tr_copied, 1)

                def step(j, it):
                    u, n = UPS * f + j, n0 + j
                    dve.wait_ge(silu_ready, val(it, u + 1))
                    dve.wait_ge(tr_done, val(it, u))
                    v.tensor_tensor(wb[:, 0:512].rearrange("p (t n) -> p t n", t=NT), ps[:, pair(n):pair(n) + 2, C2:512],
                                    wa[:, 0:512].rearrange("p (t n) -> p t n", t=NT), ALU.mult).then_inc(h_ready, 1)
                    if j > 0:
                        keep(j - 1, it)
                    if q0 is not None:
                        q = val(it, q0 + j)
                        mod_step(q, q + MODQ * f)

                for j in range(PEEL):
                    step(j, None)
                with dve.Fori(0, TURNS) as it:
                    tick.enter(it, 6 * RING if q0 is not None else 0)
                    for r in range(RING):
                        step(PEEL + r, it)
                tick.leave(TURNS)
                keep(UPS - 1, None)
                if f in (0, 2):
                    if f == 2:
                        dve.wait_ge(gate_in, 16)
                    gates(f // 2, [0] if f == 0 else [0, 1, 2])
                if q0 is not None:
                    mod_loop(f, q0 + UPS, MODQ)
                if f in (0, 2):
                    dve.wait_ge(gate_ready, 2 if f == 0 else 12)
                update(n0 + UPS + DOWNS, 0 if f in (0, 2) else 2, 0.5, 0)

            def ffn_conv(f):
                n0, v0, l = BASE[f"ffn{f}"], UPS * (f - 4), f - 4
                acc = wb[:, :].rearrange("p (c t) -> p c t", c=4)

                def conv(j, it):
                    u, y = UPS * f + j, v0 + j
                    dve.wait_ge(tr_done, val(it, u + 1))

                    def at(name, c):
                        o = COLS[name] + (c // 2) * FC + (c % 2) + 2 * j
                        return cols[:, o:o + 1] if it is None else cols[:, bass.ds(it * (2 * RING) + o, 1)]

                    def src(c, lag):
                        return ps[:, 6 + c // 2, (c % 2) * T:(c % 2) * T + T - lag]
                    fw = COLS["fc_w"]
                    for c in range(4):
                        o = (c // 2) * FC + (c % 2) + 2 * j
                        w = [cols[:, bass.ds(val2(it, COLS["fc_w"] + (l * 3 + k) * 44 + o), 1)] for k in range(3)]
                        b = cols[:, bass.ds(val2(it, COLS["fc_b"] + l * 44 + o), 1)]
                        tick.mark(v.tensor_scalar(acc[:, c, :], src(c, 0), w[2], b, ALU.mult, ALU.add))
                    for lag in (1, 2):
                        for c in range(4):
                            o = (c // 2) * FC + (c % 2) + 2 * j
                            w = cols[:, bass.ds(val2(it, COLS["fc_w"] + (l * 3 + 2 - lag) * 44 + o), 1)]
                            tick.settle(3)
                            ins = v.scalar_tensor_tensor(out=acc[:, c, lag:T], in0=src(c, lag), scalar=w, in1=acc[:, c, lag:T],
                                                         op0=ALU.mult, op1=ALU.add)
                            if lag == 2 and c == 3:
                                ins.then_inc(fconv_ready, 1)
                            else:
                                tick.mark(ins)

                def val2(it, c):
                    return c if it is None else it * (2 * RING) + c

                def join(j, it):
                    y = v0 + j
                    dve.wait_ge(gelu_ready, val(it, y + 1))
                    o = j * 512 if it is None else it * (RING * 512) + j * 512
                    v.tensor_tensor(hidT[:, bass.ds(o, 512)], wc[:, 0:512], wb[:, 512:1024], ALU.mult).then_inc(tr_copied, 1)

                def step(j, it):
                    if j > 0:
                        conv(j - 1, it)
                        join(j - 1, it)

                for j in range(PEEL):
                    step(j, None)
                with dve.Fori(0, TURNS) as it:
                    tick.enter(it, 11 * RING)
                    for r in range(RING):
                        step(PEEL + r, it)
                tick.leave(TURNS)
                step(UPS, None)

            def angles():
                posf = rtmp[:, 3, 0:NT]
                freq = rows[:, ROWS["inv_freq"]:ROWS["inv_freq"] + ROPE_HALF]
                tick.mark(v.tensor_copy(posf, pos[:, :]))
                tick.settle()
                ang = rtmp[:, 2, :]
                for tt in range(NT):
                    tick.mark(v.tensor_scalar(ang[:, tt * ROPE_HALF:(tt + 1) * ROPE_HALF], freq, posf[:, tt:tt + 1], None, ALU.mult))
                for w, turn in ((0, 0.25), (1, 0.0)):
                    r, n = rtmp[:, w, :], rtmp[:, 3, :]
                    tick.settle()
                    tick.mark(v.tensor_scalar(n, ang, 1.0 / (2.0 * np.pi), turn, ALU.mult, ALU.add))
                    tick.settle()
                    tick.mark(v.tensor_scalar(n, n, ROUND, -ROUND, ALU.add, ALU.add))
                    for i, part in enumerate(TWO_PI):
                        tick.settle()
                        tick.mark(v.scalar_tensor_tensor(out=r, in0=n, scalar=-part, in1=(ang if i == 0 else r), op0=ALU.mult, op1=ALU.add))
                    tick.settle()
                    tick.mark(v.tensor_scalar(r, r, turn * 2.0 * np.pi, 3.1415925, ALU.add, ALU.min))
                    tick.settle()
                    ins = v.tensor_scalar(r, r, -3.1415925, None, ALU.max)
                    tick.mark(ins)
                tick.settle()
                v.tensor_copy(rtmp[:, 3, 0:1], rtmp[:, 0, 0:1]).then_inc(ang_ready, 1)

            def forget():
                bf = rows[:, ROWS["b_f"]:ROWS["b_f"] + HEADS].unsqueeze(1).broadcast_to([P, NT, HEADS])
                dve.wait_ge(f_sum, 1)
                tick.mark(v.tensor_tensor(flog[:, 0, :].rearrange("p (t h) -> p t h", t=NT),
                                          ps[:, 6, 0:NT * HEADS].rearrange("p (t h) -> p t h", t=NT), bf, ALU.add))
                tick.settle()
                v.scalar_tensor_tensor(out=flog[:, 1, :], in0=flog[:, 0, :], scalar=-1.0, in1=flog[:, 0, :], op0=ALU.mult, op1=ALU.max).then_inc(f_abs, 1)
                dve.wait_ge(f_abs, 1)
                tick.mark(v.tensor_scalar(flog[:, 0, :], flog[:, 0, :], 0.0, None, ALU.min))
                tick.settle()
                dve.wait_ge(f_ln, 1)
                v.tensor_tensor(flog[:, 3, :], flog[:, 0, :], flog[:, 3, :], ALU.subtract).then_inc(lf_ready, 1)
                dve.wait_ge(cum_sum, 1)
                v.tensor_copy(ncum[:, :], ps[0:HEADS, 7, 0:T]).then_inc(cum_ready, 1)

            def qk(n0, z0, groups):
                def group(it):
                    def at(c, per):
                        return c if it is None else it * per + c
                    for j in range(4):
                        z, b = z0 + j, pair(n0 + j)
                        heads = psf[:, b * 512:(b + 2) * 512].rearrange("p (h d) -> p h d", d=HD)
                        qn = wb[:, :].rearrange("p (h d) -> p h d", d=HD)
                        dve.wait_ge(sq_ready, at(z + 1, 4))
                        v.tensor_reduce(ss16[:, :], wa[:, :].rearrange("p (h d) -> p h d", d=HD), AX.X, ALU.add).then_inc(ss_ready, 1)
                        dve.wait_ge(rs_ready, at(z + 1, 4))
                        tick.mark(v.reciprocal(rs16[:, :], rs16[:, :]))
                        tick.settle()
                        dve.wait_ge(qk_T, at(z, 4))
                        v.tensor_tensor(qn, heads, rs16[:, :].unsqueeze(2).broadcast_to([P, 16, HD]), ALU.mult).then_inc(qk_read, 1)
                        dve.wait_ge(qk_read, at(z + 1, 4))
                        name = ("fox_" if groups == 1 else "dil_") + ("q" if j < 2 else "k")
                        gain = rows[:, bass.ds(at(ROWS[name], HD), HD)].unsqueeze(1).broadcast_to([P, 16, HD])
                        ins = v.scalar_tensor_tensor(out=qn, in0=qn, scalar=HD ** -0.5 if j < 2 else 1.0, in1=gain, op0=ALU.mult, op1=ALU.mult)
                        if groups == 1:
                            ins.then_inc(qn_ready, 1)
                            continue
                        tick.mark(ins)
                        tick.settle()
                        qv = wb[:, :].rearrange("p (t h d) -> p t h d", t=NT, d=HD)
                        x1, x2 = qv[:, :, :, 0:ROPE_HALF], qv[:, :, :, ROPE_HALF:2 * ROPE_HALF]
                        c, s = [rope[:, w, :, :].unsqueeze(2).broadcast_to([P, NT, 8, ROPE_HALF]) for w in range(2)]
                        t = [wc[:, i * P:(i + 1) * P].rearrange("p (t h d) -> p t h d", t=NT, d=ROPE_HALF) for i in range(4)]
                        for dst, xx, cs in ((t[0], x1, c), (t[1], x2, s), (t[2], x2, c), (t[3], x1, s)):
                            tick.mark(v.tensor_tensor(dst, xx, cs, ALU.mult))
                        tick.settle()
                        v.tensor_tensor(x1, t[0], t[1], ALU.subtract)
                        v.tensor_tensor(x2, t[2], t[3], ALU.add).then_inc(qn_ready, 1)
                if groups == 1:
                    group(None)
                else:
                    with dve.Fori(0, groups) as it:
                        tick.enter(it, 24)
                        group(it)
                    tick.leave(groups)

            def attention(G, a_0, bufs, mask):
                SW, S1 = G * (T + P), G * T
                s = bufs["s"]
                probT = s[:, 3 * SW:4 * SW]

                def out_head(h):
                    dve.wait_ge(o_sum, a_0 + h + 1)
                    tick.mark(v.reciprocal(rsum[:, h % 2, 0:2], lsum[:, h % 4, 0:2]))
                    tick.settle()
                    o = (6 + h % 2) * 512
                    v.tensor_scalar(xn[:, 1, h * HD:(h + 1) * HD], psf[:, o + HD:o + 2 * HD], rsum[:, h % 2, 0:1], None, ALU.mult)
                    v.tensor_scalar(xn[:, 0, h * HD:(h + 1) * HD], psf[:, o:o + HD], rsum[:, h % 2, 1:2], None, ALU.mult).then_inc(o_ready, 1)

                for h in range(HEADS + 2):
                    if h < HEADS:
                        dve.wait_ge(s_done, a_0 + h + 1)
                        if h > 0:
                            dve.wait_ge(exp_ready, a_0 + h)
                        for i, (lo, hi, at) in enumerate(((0, S1, 0), (S1, SW, 1024))):
                            ins = v.tensor_tensor_reduce(out=s[:, lo:hi], in0=psf[:, at:at + hi - lo], in1=mask[:, lo:hi], scale=-1.0,
                                                         scalar=3.0e38, op0=ALU.add, op1=ALU.min, accum_out=nmax[:, h % 2, i:i + 1])
                        ins.then_inc(max_ready, 1)
                    if 1 <= h <= HEADS:
                        dve.wait_ge(p_T, a_0 + h)
                        if h >= 2:
                            dve.wait_ge(o_sum, a_0 + h - 1)
                        if G == 1:
                            ins = v.tensor_copy(probT[:, 0:SW], psf[:, 1536:1536 + SW])
                        else:
                            v.tensor_copy(probT[:, 0:512], psf[:, 1536:2048])
                            ins = v.tensor_copy(probT[:, 1024:SW], psf[:, 2560:1536 + SW])
                        ins.then_inc(pT_dve, 1)
                    if h >= 2:
                        out_head(h - 2)

            def attention_out(k):
                for b in (0, 2):
                    dve.wait_ge(o_T, 4 * k + b + 1)
                    ins = v.tensor_copy(hT[:, 2 * b:2 * b + 2, :].rearrange("p c t -> p (c t)"), ps[:, b, :])
                ins.then_inc(oT_dve, 1)

            def mixer(l):
                n0 = BASE[f"mix{l}"]
                bA, bC = pair(n0), pair(n0 + 1)
                dve.wait_ge(mix_in, 48 + 32 * l)
                tick.mark(v.memset(cv[:, :, 0:TAPS - 1], 0.0))
                tri = ntri[:, 0:P].unsqueeze(1).broadcast_to([P, 4, P])
                ws = mixw[:, 0:4 * P].rearrange("p (g t) -> p g t", g=4)
                tick.mark(v.scalar_tensor_tensor(out=ws, in0=ws, scalar=-1.0, in1=tri, op0=ALU.mult, op1=ALU.mult))
                dve.wait_ge(a_sig, l + 1)
                v.tensor_tensor(ac, ps[:, bA:bA + 2, 0:C2], wb[:, 0:512].rearrange("p (t n) -> p t n", t=NT), ALU.mult).then_inc(a_gated, 1)
                dve.wait_ge(c_copied, l + 1)
                qv = cq[:, :, 0:384].rearrange("p t (h d) -> p t h d", d=HD)
                ov = rot[:, :, :].rearrange("p t (h d) -> p t h d", d=HD)
                x1, x2 = qv[:, :, :, 0:32], qv[:, :, :, 32:64]
                c, s = [k2[:, KONST2[n]:KONST2[n] + 64].rearrange("p (t d) -> p t d", t=NT).unsqueeze(2).broadcast_to([P, NT, 6, 32]) for n in ("cos", "sin")]
                t = [w.rearrange("p (t h d) -> p t h d", t=NT, d=32) for w in (wa[:, 0:384], wa[:, 512:896], wb[:, 512:896], wc[:, 512:896])]
                for dst, xx, cs in ((t[0], x1, c), (t[1], x2, s), (t[2], x2, c), (t[3], x1, s)):
                    tick.mark(v.tensor_tensor(dst, xx, cs, ALU.mult))
                tick.settle()
                v.tensor_tensor(ov[:, :, :, 0:32], t[0], t[1], ALU.subtract)
                v.tensor_tensor(ov[:, :, :, 32:64], t[2], t[3], ALU.add).then_inc(rot_ready, 1)
                dve.wait_ge(cv_ready, l + 1)
                tick.settle()
                for c in range(2):
                    tick.mark(v.tensor_scalar(cacc[:, c, :], cv[:, c, 0:T], col("conv_w", l * TAPS * 2 + c), col("conv_b", 2 * l + c), ALU.mult, ALU.add))
                for k in range(1, TAPS):
                    for c in range(2):
                        tick.settle(1)
                        tick.mark(v.scalar_tensor_tensor(out=cacc[:, c, :], in0=cv[:, c, k:k + T], scalar=col("conv_w", (l * TAPS + k) * 2 + c),
                                                         in1=cacc[:, c, :], op0=ALU.mult, op1=ALU.add))
                tick.settle()
                v.tensor_copy(lnv[:, 6:7], cacc[:, 1, 0:1]).then_inc(conv_ready, 1)
                dve.wait_ge(qkT_ready, l + 1)
                for w in range(2):
                    src = qkT[:, (6 + w) * T:(7 + w) * T].rearrange("p (n i) -> p i n", i=CMP_STRIDE)
                    o = 2 * CMP_LEN * HD + 2 * HD + w * CMP_LEN
                    for part in range(2):
                        pe_col = nsaw[:, o + part * 16:o + part * 16 + 16].unsqueeze(2).broadcast_to([HD, 16, NCMP])
                        ins = v.tensor_tensor(blk[:, w, part * 16:part * 16 + 16, :], src[:, :, part:part + NCMP], pe_col, ALU.add)
                ins.then_inc(blk_ready, 1)
                dve.wait_ge(b_gelu, l + 1)
                for tt in range(NT):
                    tick.mark(v.bn_stats(bnst[:, tt * 6:tt * 6 + 6], zg[:, tt, C2:512]))
                tick.settle()
                for tt in range(NT):
                    ins = v.bn_aggr(lnv[:, 2 * tt:2 * tt + 2], bnst[:, tt * 6:tt * 6 + 6])
                ins.then_inc(zvar_ready, 1)
                dve.wait_ge(zstd_ready, l + 1)
                tick.mark(v.reciprocal(lnv[:, 4:6], lnv[:, 4:6]))
                tick.settle()
                for tt in range(NT):
                    tick.mark(v.tensor_scalar(vn[:, tt, :], zg[:, tt, C2:512], lnv[:, 2 * tt:2 * tt + 1], lnv[:, 4 + tt:5 + tt], ALU.subtract, ALU.mult))
                tick.settle()
                ln = [mixw[:, 4 * P + 2 * HD + i * C2:4 * P + 2 * HD + (i + 1) * C2].unsqueeze(1).broadcast_to([P, NT, C2]) for i in range(2)]
                tick.mark(v.tensor_tensor(vn, vn, ln[0], ALU.mult))
                tick.settle()
                v.tensor_tensor(vn, vn, ln[1], ALU.add).then_inc(vn_ready, 1)
                dve.wait_ge(kv_sum, l + 1)
                v.tensor_copy(kcT, ps[0:HD, 6, 32:32 + NCMP])
                v.tensor_copy(vc, ps[0:NCMP, 6, 64:64 + HD]).then_inc(kv_ready, 1)
                dve.wait_ge(sgu_sum, l + 1)
                fv = ps[:, 6, :].rearrange("p (t n) -> p t n", t=NT)
                for g in range(4):
                    gs = slice(g * HD, (g + 1) * HD)
                    ins = v.scalar_tensor_tensor(out=ysg[:, :, gs], in0=fv[:, :, gs], scalar=col("sgu_b", 4 * l + g), in1=zg[:, :, gs], op0=ALU.add, op1=ALU.mult)
                ins.then_inc(sgu_ready, 1)
                segs = [(0, T, bC, 0), (T, 2 * T, bC, T), (NS1, NS1 + P, bC + 1, 0), (NS1 + P, NS1 + 2 * P, bC + 1, P),
                        (NS1 + 2 * P, NS1 + 2 * P + NCMP, bC + 1, 2 * P), (NS1 + 2 * P + NCMP, NS1 + NS0, bC + 1, 2 * P + NCMP)]
                branch = [(1, 1), (1, 2), (0, 1), (0, 2), (0, 0), (1, 0)]

                def weigh(h):
                    i = NH * l + h
                    dve.wait_ge(nexp_ready, i + 1)
                    tick.mark(v.reciprocal(rsum[:, h % 2, 0:6], lsum[:, h % 4, 0:6]))
                    tick.settle()
                    for k, (tt, b) in enumerate(branch):
                        tick.mark(v.tensor_tensor(rsum[:, h % 2, k:k + 1], rsum[:, h % 2, k:k + 1], gt[:, tt, 3 * h + b:3 * h + b + 1], ALU.mult))
                    tick.settle()
                    tick.mark(v.tensor_tensor(rsum[:, h % 2, 4:5], rsum[:, h % 2, 4:5], k2[:, KONST2["late"]:KONST2["late"] + 1], ALU.mult))
                    tick.settle()
                    for k, (lo, hi, _, _) in enumerate(segs):
                        pr = nsaP[h % 2][:, lo:hi]
                        ins = v.tensor_scalar(pr, pr, rsum[:, h % 2, k:k + 1], None, ALU.mult)
                    ins.then_inc(np_ready, 1)

                for h in range(NH + 1):
                    i = NH * l + h
                    if h < NH:
                        dve.wait_ge(ns_done, i + 1)
                        if h > 0:
                            dve.wait_ge(nexp_ready, i)
                        for k, (lo, hi, b, o) in enumerate(segs):
                            m = KONST2["nsa1"] + lo if lo < NS1 else KONST2["nsa0"] + lo - NS1
                            ins = v.tensor_tensor_reduce(out=nsaS[:, lo:hi], in0=ps[:, b, o:o + hi - lo], in1=k2[:, m:m + hi - lo], scale=-1.0,
                                                         scalar=3.0e38, op0=ALU.add, op1=ALU.min, accum_out=nmax[:, h % 2, k:k + 1])
                        ins.then_inc(nmax_ready, 1)
                    if h >= 1:
                        weigh(h - 1)
                dve.wait_ge(mu_sum, l + 1)
                v.tensor_tensor(cd, cacc, ps[:, bA, 0:T].unsqueeze(1).broadcast_to([P, 2, T]), ALU.subtract).then_inc(cd_ready, 1)
                dve.wait_ge(no_sum, NH * (l + 1))
                tick.settle()
                ov = ps[:, 7, :].rearrange("p (h t d) -> p t h d", h=NH, t=NT)
                v.tensor_copy(osm[:, 0, :].rearrange("p (h d) -> p h d", d=HD), ov[:, 0, :, :])
                v.tensor_copy(osm[:, 1, :].rearrange("p (h d) -> p h d", d=HD), ov[:, 1, :, :]).then_inc(no_copied, 1)
                dve.wait_ge(cstd_ready, l + 1)
                tick.mark(v.reciprocal(wb[:, 0:T], wb[:, 0:T]))
                tick.settle()
                dve.wait_ge(cd_ready, l + 1)
                v.tensor_tensor(cd, cd, wb[:, 0:T].unsqueeze(1).broadcast_to([P, 2, T]), ALU.mult).then_inc(cn_ready, 1)

            dve.wait_ge(konst_in, 16 * 7)
            angles()
            dve.wait_ge(cact_ready, 1)
            mod_loop(0, 0, 4)
            mod_cols(0, [0], 1)
            norm(0)
            ffn(0)
            mod_cols(0, [1, 2], 2)
            norm(1)
            gates(0, [1, 2])
            forget()
            qk(BASE["fox"], 0, 1)
            attention(1, 0, fox_bufs, konst[:, KONST["causal"]:KONST["causal"] + T + P])
            attention_out(0)
            update(BASE["fox_out"] + 2, 1, 1.0, 4)
            norm(2)
            ffn(1)
            mod_cols(1, [0, 1, 2], 3)
            norm(3)
            ffn(2)
            norm(4)
            qk(BASE["dil"], 4, GROUPS)
            attention(GROUPS, HEADS, dil_bufs, konst[:, KONST["dil"]:KONST["dil"] + GROUPS * (T + P)])
            attention_out(1)
            update(BASE["dil_out"] + 2, 1, 1.0, 4)
            norm(5)
            ffn(3)
            dve.wait_ge(gate_in, 32)
            for l in range(LAYERS):
                norm(6 + 2 * l)
                mixer(l)
                update_normed(2 * l, 2 * l, 4)
                norm(7 + 2 * l)
                ffn_conv(4 + l)
                if l == 1:
                    dve.wait_ge(gate_in, 48)
                update_normed(2 * l + 1, (2 * l + 1) % 3, 0)


def _steps(w):
    n = w.shape[1] // 512
    return w.reshape(KC, P, n, 512).transpose(2, 1, 0, 3).reshape(n, P, STEP)


def _down(w):
    n = -(-w.shape[0] // 512)
    full = np.zeros((n * 512, D), w.dtype)
    full[:w.shape[0]] = w
    return full.reshape(n, 4, P, D).transpose(0, 2, 1, 3).reshape(n, P, STEP)


def _gate_up(g, u):
    return _steps(np.stack([g.reshape(D, UPS, C2), u.reshape(D, UPS, C2)], axis=2).reshape(D, 2 * FF))


def _columns(v):
    return v.reshape(-1, P).T


def _constants():
    t = np.arange(T)
    q, k = t[:, None], t[None, :]

    def tiles(seen):
        far = np.where(seen, np.float32(0), np.float32(-FAR)).astype(np.float32)
        return far[P:, :], far[:P, :P]
    causal = k <= q
    c1, c0 = tiles(causal)
    dil = [tiles(causal & ((q - k) % d == 0) & (q - k <= w)) for w, d in ((128, 1), (512, 4), (2048, 16))]
    eye = np.eye(P, dtype=np.float32)
    one = np.ones((P, P), np.float32)
    ntri = np.concatenate([-np.triu(one), -one], axis=1)
    first = [eye, one, ntri, one[:, :1] * np.float32(EPS), one[:, :1] * np.float32(LN_EPS), c1, c0] + [d[0] for d in dil] + [d[1] for d in dil]

    pool = []
    for w in POOLS:
        cnt = np.minimum(t + 1, w).astype(np.float32)[:, None]
        m = (np.where(causal & (q - k < w), np.float32(1), np.float32(0)) / cnt - np.eye(T, dtype=np.float32)).T.astype(np.float32)
        pool += [m[:P, :], m[P:, P:]]
    ends = np.arange(NCMP) * CMP_STRIDE + CMP_LEN - 1
    cmp_far = np.where(ends[None, :] <= q, np.float32(0), np.float32(-FAR)).astype(np.float32)
    inv = (np.float32(10000.0) ** (-np.arange(32, dtype=np.float32) * np.float32(2.0) / np.float32(HD))).astype(np.float32)
    ang = (t.astype(np.float32)[:, None] * inv[None, :]).astype(np.float32)

    def by_tile(v):
        return v.reshape(NT, P, -1).transpose(1, 0, 2).reshape(P, -1)
    late = (np.arange(P) >= CMP_LEN - 1).astype(np.float32)[:, None]
    second = pool + [c1, c1, c0, c0, cmp_far[:P], cmp_far[P:], by_tile(np.cos(ang)), by_tile(np.sin(ang)),
                     np.full((P, P), 1.0 / C2, np.float32), late]
    sel = np.repeat(np.eye(HEADS, dtype=np.float32), P, axis=1)
    cat = lambda parts: np.ascontiguousarray(np.concatenate(parts, axis=1), np.float32)
    return cat(first), cat(second), sel


def kernel(x, c, positions, mod_w, mod_b, norm_g, ffn_w_gate, ffn_w_up, ffn_w_down, fox_w_in, fox_b_f,
           fox_q_g, fox_k_g, fox_w_out, dil_w_in, dil_q_g, dil_k_g, dil_w_out, norm_mix_pre_2,
           norm_mix_post_2, norm_ffn_pre_2, norm_ffn_post_2, w_in_2, w_out_2, conv_dw_w_2, conv_dw_b_2,
           conv_ln_g_2, conv_ln_b_2, nsa_pe_k_2, nsa_pe_v_2, nsa_ck_w1_2, nsa_ck_w2_2, nsa_cv_w1_2,
           nsa_cv_w2_2, sgu_ln_g_2, sgu_ln_b_2, sgu_w_2, sgu_b_2, pool_w_2, pool_scale_2, ffn_up_2,
           ffn_conv_w_2, ffn_conv_b_2, ffn_down_2):
    import concourse.bacc as bacc
    from concourse.bass_utils import run_bass_kernel_spmd as run

    qkv = HEADS * HD
    parts = []
    for i in range(LAYERS):
        for j in range(2):
            ffn = [_gate_up(np.asarray(ffn_w_gate)[i, j], np.asarray(ffn_w_up)[i, j]), _down(np.asarray(ffn_w_down)[i, j])]
            if j == 1:
                parts += [_steps(np.asarray(fox_w_in)[0][:, :3 * qkv]), _down(np.asarray(fox_w_out)[0])] if i == 0 else \
                         [_steps(np.asarray(dil_w_in)[0]), _down(np.asarray(dil_w_out)[0])]
            parts += ffn
    at = [0, 256, 512, 768, 1152, 1164, 1420, 1676, 1932]
    for l in range(LAYERS):
        w = np.asarray(w_in_2)[l]
        kv = [w[:, 768 + HD * i:768 + HD * (i + 1)] for i in range(6)]
        order = [w[:, 0:512], w[:, 512:768], kv[2], kv[4], kv[0], kv[1], w[:, 1676:1932], kv[3], kv[5], w[:, 1152:1164],
                 np.zeros((D, 512 - 396), w.dtype), w[:, 1164:1676]]
        up = np.asarray(ffn_up_2)[l]
        parts += [_steps(np.concatenate(order, axis=1)), _down(np.asarray(w_out_2)[l]),
                  _gate_up(up[:, :FF], up[:, FF:]), _down(np.asarray(ffn_down_2)[l])]
    konst, konst2, sel = _constants()
    inv_freq = np.float32(500000.0) ** (-(np.arange(ROPE_HALF, dtype=np.float32) * np.float32(2.0) / np.float32(2 * ROPE_HALF)))
    as_np = np.asarray
    cols = np.concatenate([_columns(as_np(v)) for v in (
        mod_b, norm_g, norm_mix_pre_2, norm_ffn_pre_2, conv_dw_w_2, conv_dw_b_2, conv_ln_g_2, conv_ln_b_2,
        pool_scale_2, ffn_conv_w_2, ffn_conv_b_2, sgu_b_2, c)], axis=1)
    rows = np.concatenate([as_np(v).reshape(-1) for v in (fox_q_g, fox_k_g, dil_q_g, dil_k_g, fox_b_f)] + [inv_freq.astype(np.float32)])
    mb = as_np(mod_b).reshape(LAYERS, 3, 3, D)
    post = [as_np(norm_mix_post_2), as_np(norm_ffn_post_2)]
    wide = np.concatenate([mb[0, :, 2], mb[1, :, 2]] + [post[k][l:l + 1] for l in range(LAYERS) for k in range(2)], axis=0)
    w1 = [as_np(v).reshape(LAYERS, CMP_LEN, HD, HD).transpose(0, 2, 1, 3).reshape(LAYERS, HD, CMP_LEN * HD) for v in (nsa_ck_w1_2, nsa_cv_w1_2)]
    nsaw = np.concatenate(w1 + [as_np(nsa_ck_w2_2), as_np(nsa_cv_w2_2), as_np(nsa_pe_k_2).transpose(0, 2, 1), as_np(nsa_pe_v_2).transpose(0, 2, 1)], axis=2)
    mixw = np.concatenate(
        [as_np(sgu_w_2).transpose(0, 3, 1, 2).reshape(LAYERS, P, 4 * P),
         as_np(pool_w_2).reshape(LAYERS, 2, 2, HD, HD).transpose(0, 2, 3, 1, 4).reshape(LAYERS, P, 2 * HD)] +
        [np.broadcast_to(as_np(v)[:, None, :], (LAYERS, P, C2)) for v in (sgu_ln_g_2, sgu_ln_b_2)], axis=2)
    arrays = {
        "stream": np.concatenate(parts, axis=0),
        "mod": np.concatenate([_steps(as_np(mod_w)[i]) for i in range(LAYERS)], axis=0),
        "cols": cols, "rows": rows, "wide": wide, "konst": konst, "konst2": konst2, "sel": sel,
        "wf": as_np(fox_w_in)[0][:, 3 * qkv:].reshape(KC, P, HEADS).transpose(1, 0, 2),
        "x": as_np(x)[0].reshape(NT, P, D).transpose(1, 0, 2),
        "pos": as_np(positions)[0].reshape(NT, P).T,
        "nsaw": nsaw, "mixw": mixw,
    }
    arrays = {f"in_{k}": np.ascontiguousarray(v) for k, v in arrays.items()}
    assert arrays["in_stream"].shape == (STEPS, P, STEP) and arrays["in_cols"].shape == (P, NCOLS)
    assert arrays["in_rows"].shape == (NROWS,) and arrays["in_konst"].shape == (P, NKONST) and arrays["in_konst2"].shape == (P, NKONST2)
    assert arrays["in_nsaw"].shape == (LAYERS, HD, NSA_W) and arrays["in_mixw"].shape == (LAYERS, P, MIX_W)
    nc = bacc.Bacc("TRN2", target_bir_lowering=False, num_devices=1)
    a = {k[3:]: nc.dram_tensor(k, v.shape, mybir.dt.from_np(v.dtype), kind="ExternalInput").ap() for k, v in arrays.items()}
    out = nc.dram_tensor("out", (T, D), F32, kind="ExternalOutput").ap()
    build(nc, a, out)
    r = run(nc, [arrays], core_ids=[0])
    return r.results[0]["out"].reshape(1, T, D)
```

```python
from contextlib import ExitStack

import numpy as np
import concourse.bass as bass
from concourse import mybir

F32 = mybir.dt.float32
F32R = mybir.dt.float32r
I32 = mybir.dt.int32
ALU = mybir.AluOpType
ACT = mybir.ActivationFunctionType
AX = mybir.AxisListType

P = 128
T = 256
NT = T // P
D = 1024
KC = D // P
LAYERS = 2
HEADS, HD = 16, 64
PAIRS = HEADS // 2
FF = 2816
UPS = FF // 256
FC = FF // P
STEP = 4096
HALF, QUARTER = STEP // 2, STEP // 4
SLOTS = 4
SPLITS = 4
LEAD = 3
RING = 2
UPQ, DOWNQ = 4 * UPS, FC
GROUPS = 3
MODQ = 18
EPS, LN_EPS = 1e-6, 1e-5
ROPE_HALF = 8
NH = 4
CMP_LEN, CMP_STRIDE = 32, 16
NCMP = (T - CMP_LEN) // CMP_STRIDE + 1
TAPS = 31
C2 = 256
POOLS = (2, 4, 8, 16)
FAR = 1.0e30
ROUND = 1.5 * 2.0 ** 23
TWO_PI = (6.28125, 1.93500518798828125e-3, 3.0199159819e-7)

PHASES = [("ffn0", UPQ + DOWNQ), ("fox", 4 * 6), ("fox_out", 8), ("ffn1", UPQ + DOWNQ),
          ("ffn2", UPQ + DOWNQ), ("dil", 4 * 6 * GROUPS), ("dil_out", 8), ("ffn3", UPQ + DOWNQ),
          ("mix0", 16), ("mix0_out", 8), ("ffn4", UPQ + DOWNQ),
          ("mix1", 16), ("mix1_out", 8), ("ffn5", UPQ + DOWNQ)]
BASE, QUARTERS = {}, 0
for _name, _n in PHASES:
    BASE[_name] = QUARTERS
    QUARTERS += _n
HALVES = QUARTERS // 2
POOL_Q = [BASE[_f] + 4 * _j + 3 for _f in ("ffn4", "ffn5") for _j in range(UPS)]
UP_BANKS = (0, 2)
MIX_BANKS = (0, 2, 4, 0)
DOWN_BANK = 2

COLS, NCOLS = {}, 0
for _name, _n in [("mod_b", LAYERS * 72), ("norm_g", LAYERS * 24), ("mix_pre", LAYERS * 8), ("ffn_pre", LAYERS * 8),
                  ("conv_w", LAYERS * TAPS * 2), ("conv_b", LAYERS * 2), ("conv_g", LAYERS * 2), ("conv_lb", LAYERS * 2),
                  ("pool_s", LAYERS * 2), ("fc_w", LAYERS * 3 * 44), ("fc_b", LAYERS * 44), ("sgu_b", LAYERS * 4),
                  ("c", KC)]:
    COLS[_name] = NCOLS
    NCOLS += _n

ROWS, NROWS = {}, 0
for _name, _n in [("fox_q", HD), ("fox_k", HD), ("dil_q", GROUPS * HD), ("dil_k", GROUPS * HD), ("b_f", HEADS), ("inv_freq", ROPE_HALF)]:
    ROWS[_name] = NROWS
    NROWS += _n

KONST, NKONST = {}, 0
for _name, _n in [("ident", P), ("ones", P), ("ntri", T), ("eps", 1), ("ln_eps", 1), ("causal", T + P), ("dil", GROUPS * P)]:
    KONST[_name] = NKONST
    NKONST += _n
KONST2, NKONST2 = {}, 0
for _name, _n in [("pool", 4 * (T + P)), ("nsa1", 2 * T), ("nsa0", 2 * P + 2 * NCMP), ("cos", 64), ("sin", 64),
                  ("mean", P), ("late", 1)]:
    KONST2[_name] = NKONST2
    NKONST2 += _n
NSA_W = 2 * CMP_LEN * HD + 2 * HD + 2 * CMP_LEN
MIX_W = 4 * P + 2 * HD + 2 * C2


class Tick:

    def __init__(self, eng, sem):
        self.eng, self.sem, self.n, self.it, self.per, self.start = eng, sem, 0, None, 0, 0

    def mark(self, ins):
        ins.then_inc(self.sem, 1)
        self.n += 1

    def settle(self, back=0):
        v = self.n - back
        self.eng.wait_ge(self.sem, v if self.it is None else self.it * self.per + v)

    def enter(self, it, per):
        self.it, self.per, self.start = it, per, self.n

    def leave(self, turns):
        assert self.n - self.start == self.per, (self.n - self.start, self.per)
        self.it, self.n = None, self.start + turns * self.per


def build(nc, a, out):
    ctx = ExitStack()
    with ctx:
        def sb(name, shape, dt=F32):
            return ctx.enter_context(nc.sbuf_tensor(name, shape, dt))

        def sem(name):
            return ctx.enter_context(nc.semaphore(name))

        ARENA = 23040
        WF = KC * HEADS
        sizes = [("ring", SLOTS * HALF), ("w_hi", SPLITS * QUARTER), ("hT", KC * T), ("h_hi", KC * T), ("arena", ARENA),
                 ("wf", WF), ("wf_hi", WF)]
        slab_at, slab_n = {}, 0
        for n_, w_ in sizes:
            slab_at[n_] = slab_n
            slab_n += w_
        sb("slab", [P, slab_n])
        slab_base = nc.sbuf_base - 4 * slab_n

        def over(name, at, shape, dt=F32):
            return nc.alloc_sbuf_tensor_at(name, shape, dt, offset=slab_base + 4 * at)

        ring = over("ring", slab_at["ring"], [P, SLOTS, HALF])
        ring_lo = over("ring_lo", slab_at["ring"], [P, SLOTS, HALF], F32R)
        w_hi = over("w_hi", slab_at["w_hi"], [P, SPLITS, QUARTER], F32R)
        hT = over("hT", slab_at["hT"], [P, KC, T])
        h_lo = over("h_lo", slab_at["hT"], [P, KC, T], F32R)
        h_hi = over("h_hi", slab_at["h_hi"], [P, KC, T], F32R)
        arena = over("arena", slab_at["arena"], [P, ARENA])
        hid_hi = over("hid_hi", slab_at["arena"], [P, FC * T], F32R)
        hid_lo = over("hid_lo", slab_at["arena"] + FC * T, [P, FC * T], F32R)
        hid_whole = over("hid_whole", slab_at["arena"] + FC * T, [P, FC * T])
        wf = over("wf", slab_at["wf"], [P, KC, HEADS])
        wf_lo = over("wf_lo", slab_at["wf"], [P, KC, HEADS], F32R)
        wf_hi = over("wf_hi", slab_at["wf_hi"], [P, KC, HEADS], F32R)
        x = sb("x", [P, NT, D])
        xn = sb("xn", [P, NT, D])
        gate = sb("gate", [P, 3, D])
        wa, wb, wc = sb("wa", [P, 1024]), sb("wb", [P, 1024]), sb("wc", [P, 1024])
        cols = sb("cols", [P, NCOLS])
        rows = sb("rows", [P, NROWS])
        konst = sb("konst", [P, NKONST])
        pos = sb("pos", [P, NT], I32)
        cact = sb("cact", [P, KC])
        modcol = sb("modcol", [P, 3, 2, KC])
        ms, rms, rstd = sb("ms", [P, 4]), sb("rms", [P, 4]), sb("rstd", [P, 4])
        ss16, rs16 = sb("ss16", [P, 16]), sb("rs16", [P, 16])
        nmax, lsum, rsum = sb("nmax", [P, 2, 8]), sb("lsum", [P, 4, 8]), sb("rsum", [P, 2, 8])
        rope = sb("rope", [P, 2, NT, ROPE_HALF])
        rtmp = sb("rtmp", [P, 4, NT * ROPE_HALF])
        flog = sb("flog", [P, 4, NT * HEADS])
        ncum = sb("ncum", [HEADS, T])
        gt = sb("gt", [P, NT, 3 * NH])
        ps = ctx.enter_context(nc.psum_tensor("ps", [P, 8, 512], F32))
        psf = ps[:, :, :].rearrange("p b n -> p (b n)")

        ident = konst[:, KONST["ident"]:KONST["ident"] + P]
        ones = konst[:, KONST["ones"]:KONST["ones"] + P]
        ntri = konst[:, KONST["ntri"]:KONST["ntri"] + T]
        eps_col, ln_eps_col = [konst[:, KONST[n]:KONST[n] + 1] for n in ("eps", "ln_eps")]

        A0 = 2 * FC * T
        accs = arena[:, A0:A0 + MODQ * 512]
        mring = arena[:, A0 + MODQ * 512:A0 + MODQ * 512 + 2 * QUARTER].rearrange("p (h n) -> p h n", h=2)
        fox_bufs = dict(qT=arena[:, 0:2048], kT=arena[:, 2048:4096], v=arena[:, 4096:6144], s=arena[:, 6144:7680])
        sel = arena[0:HEADS, 7680:7680 + HEADS * P]
        dil_bufs = dict(qT=arena[:, 0:6144], kT=arena[:, 6144:12288], v=arena[:, 12288:18432], s=arena[:, 18432:23040])
        mod_first = [[arena[:, 0:STEP]], [arena[:, STEP:2 * STEP]], [arena[:, A0 + 2048:A0 + 2048 + STEP]],
                     [arena[:, A0 + 2048 + STEP:A0 + MODQ * 512], wa[:, :]]]
        FIRST = len(mod_first)

        a0 = 5632
        cq = arena[:, a0:a0 + 1024].rearrange("p (t n) -> p t n", t=NT)
        rot = arena[:, a0 + 1024:a0 + 1792].rearrange("p (t n) -> p t n", t=NT)
        qkT = arena[0:HD, a0 + 1792:a0 + 1792 + 12 * T]
        a0 += 1792 + 12 * T
        dv = arena[:, a0:a0 + 768].rearrange("p (t n) -> p t n", t=NT)
        blk = arena[0:HD, a0 + 768:a0 + 768 + 2 * CMP_LEN * NCMP].rearrange("p (w l n) -> p w l n", w=2, l=CMP_LEN)
        a0 += 768 + 2 * CMP_LEN * NCMP
        hid = arena[0:HD, a0:a0 + 32]
        kcT = arena[0:HD, a0 + 32:a0 + 32 + NCMP]
        vc = arena[0:NCMP, a0 + 64:a0 + 128]
        pT = arena[:, a0 + 128:a0 + 640]
        bnst = arena[:, a0 + 640:a0 + 656]
        lnv = arena[:, a0 + 656:a0 + 664]
        a0 = max(a0 + 664, A0)
        nsaw = arena[0:HD, a0:a0 + NSA_W]
        k2 = arena[:, a0 + NSA_W:a0 + NSA_W + NKONST2]
        a0 += NSA_W + NKONST2
        mixw = arena[:, a0:a0 + MIX_W]
        assert a0 + MIX_W + 2 * T + 2 * P + 2 * NCMP <= ARENA, a0
        hidT = arena
        zg = wa[:, :].rearrange("p (t n) -> p t n", t=NT)
        vn = wb[:, 0:512].rearrange("p (t n) -> p t n", t=NT)
        CVW = TAPS - 1 + T
        cv = hidT[:, 0:2 * CVW].rearrange("p (c t) -> p c t", c=2)
        cacc = hidT[:, 572:1084].rearrange("p (c t) -> p c t", c=2)
        cd = hidT[:, 1084:1596].rearrange("p (c t) -> p c t", c=2)
        csq = hidT[:, 1596:2108].rearrange("p (c t) -> p c t", c=2)
        NS1, NS0 = 2 * T, 2 * P + 2 * NCMP
        nsaS = [hidT[:, 2108:2108 + NS1 + NS0], arena[:, a0 + MIX_W:a0 + MIX_W + NS1 + NS0]]
        nsaP = [hidT[:, 2908 + i * 800:2908 + i * 800 + NS1 + NS0] for i in range(2)]
        nsaT = hidT[:, 4508:5532]
        ysg = wc[:, 512:1024].rearrange("p (t n) -> p t n", t=NT)
        ac = wc[:, 0:512].rearrange("p (t n) -> p t n", t=NT)
        osm = xn[:, 0, 0:512].rearrange("p (t n) -> p t n", t=NT)

        slot_full = [sem(f"slot_full{i}") for i in range(SLOTS)]
        w_hi_ready, w_lo_ready, w_lo_pool = sem("w_hi_ready"), sem("w_lo_ready"), sem("w_lo_pool")
        tile_done = sem("tile_done")
        quarter_done = sem("quarter_done")
        cols_in, x_in, konst_in, late_in, gate_in, mix_in = [sem(n) for n in ("cols_in", "x_in", "konst_in", "late_in", "gate_in", "mix_in")]
        first_in = [sem(f"first_in{i}") for i in range(FIRST)]
        first_done = sem("first_done")
        mod_in = [sem(f"mod_in{i}") for i in range(2)]
        mod_used = sem("mod_used")
        col_sum, col_ready = sem("col_sum"), sem("col_ready")
        gate_sum, gate_ready = sem("gate_sum"), sem("gate_ready")
        cact_ready = sem("cact_ready")
        dve_tick, act_tick, pool_tick = sem("dve_tick"), sem("act_tick"), sem("pool_tick")
        x_ready = sem("x_ready")
        ms_ready, xn_ready, norm_T, norm_hi, norm_lo = sem("ms_ready"), sem("xn_ready"), sem("norm_T"), sem("norm_hi"), sem("norm_lo")
        silu_ready, h_ready, tr_done, tr_copied = sem("silu_ready"), sem("h_ready"), sem("tr_done"), sem("tr_copied")
        gu_ready, fconv_ready, gelu_ready = sem("gu_ready"), sem("fconv_ready"), sem("gelu_ready")
        ang_ready, rope_ready = sem("ang_ready"), sem("rope_ready")
        f_sum, f_abs, f_ln, lf_ready, cum_sum, cum_ready = [sem(n) for n in ("f_sum", "f_abs", "f_ln", "lf_ready", "cum_sum", "cum_ready")]
        sq_ready, ss_ready, rs_ready, qk_read, qn_ready, qk_T, qk_copied, v_copied = [sem(n) for n in ("sq_ready", "ss_ready", "rs_ready", "qk_read", "qn_ready", "qk_T", "qk_copied", "v_copied")]
        s_done, max_ready, exp_ready, p_T, pT_dve, pT_act, o_sum, o_ready = [
            sem(n) for n in ("s_done", "max_ready", "exp_ready", "p_T", "pT_dve", "pT_act", "o_sum", "o_ready")]
        o_T, oT_hi, oT_lo = sem("o_T"), sem("oT_hi"), sem("oT_lo")
        hid_hi_ready, wf_hi_ready, wf_ready = sem("hid_hi_ready"), sem("wf_hi_ready"), sem("wf_ready")
        a_sig, a_gated, a_T, cv_ready, c_copied, d_copied, b_gelu = [sem(n) for n in ("a_sig", "a_gated", "a_T", "cv_ready", "c_copied", "d_copied", "b_gelu")]
        rot_ready, conv_ready, q_T, qkT_ready, blk_ready = [sem(n) for n in ("rot_ready", "conv_ready", "q_T", "qkT_ready", "blk_ready")]
        hid_sum, hid_ready, kv_sum, kv_ready = [sem(n) for n in ("hid_sum", "hid_ready", "kv_sum", "kv_ready")]
        pool_sum, pool_copied, pool_mix, pool_hi, pool_out = [sem(n) for n in ("pool_sum", "pool_copied", "pool_mix", "pool_hi", "pool_out")]
        vn_ready, sgu_sum, sgu_ready, sgu_T, sgu_hi, sgu_out = [sem(n) for n in ("vn_ready", "sgu_sum", "sgu_ready", "sgu_T", "sgu_hi", "sgu_out")]
        ns_done, nmax_ready, nexp_ready, nw_ready, np_ready, np_T, npT_copied, no_sum, no_copied, no_T, no_hi, no_out = [
            sem(n) for n in ("ns_done", "nmax_ready", "nexp_ready", "nw_ready", "np_ready", "np_T", "npT_copied", "no_sum", "no_copied", "no_T", "no_hi", "no_out")]
        mu_sum, cd_ready, csq_ready, var_sum, cn_ready, conv_hi, conv_out = [sem(n) for n in ("mu_sum", "cd_ready", "csq_ready", "var_sum", "cn_ready", "conv_hi", "conv_out")]
        yms_ready, zvar_ready, zstd_ready, cstd_ready = [sem(n) for n in ("yms_ready", "zvar_ready", "zstd_ready", "cstd_ready")]
        stored = sem("stored")

        block = ctx.enter_context(nc.Block())

        def val(it, c, per=RING):
            return c if it is None else it * per + c

        TURNQ = 4 * RING
        PEEL, TURNS = UPS % RING, UPS // RING

        @block.sync
        def _(sp):
            for q in range(FIRST):
                at = 0
                for part in mod_first[q]:
                    w = min(part.shape[1], STEP - at)
                    sp.dma_start(part[:, 0:w], a["mod"][q, :, at:at + w]).then_inc(first_in[q], 16)
                    at += w
            for h in range(SLOTS):
                sp.dma_start(ring[:, h, :], a["stream"][h, :, :]).then_inc(slot_full[h], 16)
            whole = HALVES // SLOTS
            with sp.Fori(1, whole) as i:
                for r in range(SLOTS):
                    sp.wait_ge(quarter_done, i * (2 * SLOTS) + 2 * (r - SLOTS + 1))
                    sp.dma_start(ring[:, r, :], a["stream"][i * SLOTS + r, :, :]).then_inc(slot_full[r], 16)
            for h in range(whole * SLOTS, HALVES):
                sp.wait_ge(quarter_done, 2 * (h - SLOTS + 1))
                sp.dma_start(ring[:, h % SLOTS, :], a["stream"][h, :, :]).then_inc(slot_full[h % SLOTS], 16)
            for tt in range(NT):
                sp.wait_ge(x_ready, 2 * 9 + tt + 1)
                sp.dma_start(out[tt * P:(tt + 1) * P, :], x[:, tt, :]).then_inc(stored, 16)
            sp.wait_ge(stored, 16 * NT)

        @block.gpsimd
        def _(pool):
            def wide(r, s, n):
                return pool.dma_start(gate[:, s:s + n, :].rearrange("p s n -> p (s n)"),
                                      a["wide"][r:r + n, :].rearrange("s n -> (s n)").partition_broadcast(P))

            pool.dma_start(rows[:, :], a["rows"].partition_broadcast(P)).then_inc(konst_in, 16)
            pool.dma_start(wf[:, :, :], a["wf"]).then_inc(konst_in, 16)
            pool.dma_start(pos[:, :], a["pos"]).then_inc(konst_in, 16)
            tick = Tick(pool, pool_tick)

            def split(f):
                q0 = BASE[f"ffn{f}"] + LEAD

                def step(j, it):
                    q = q0 + 4 * j
                    pool.wait_ge(w_hi_ready, val(it, q + 1, TURNQ))
                    slot, cs = (q // 2) % SLOTS, slice((q % 2) * QUARTER, (q % 2 + 1) * QUARTER)
                    nc.gpsimd.tensor_tensor(ring_lo[:, slot, cs], ring[:, slot, cs], w_hi[:, q % SPLITS, :], ALU.subtract).then_inc(w_lo_pool, 1)
                for j in range(PEEL):
                    step(j, None)
                with pool.Fori(0, TURNS) as it:
                    for r in range(RING):
                        step(PEEL + r, it)

            def convolution(l):
                def wide_col(o):
                    return cols[:, o:o + 2].unsqueeze(2).broadcast_to([P, 2, T])
                pool.wait_ge(cv_ready, l + 1)
                tick.mark(nc.gpsimd.tensor_tensor(cacc, cv[:, :, 0:T], wide_col(COLS["conv_w"] + l * TAPS * 2), ALU.mult))
                for k in range(1, TAPS):
                    tap = (cd, csq)[k % 2]
                    tick.mark(nc.gpsimd.tensor_tensor(tap, cv[:, :, k:k + T], wide_col(COLS["conv_w"] + (l * TAPS + k) * 2), ALU.mult))
                    tick.settle()
                    tick.mark(nc.gpsimd.tensor_tensor(cacc, cacc, tap, ALU.add))
                tick.settle()
                nc.gpsimd.tensor_tensor(cacc, cacc, wide_col(COLS["conv_b"] + 2 * l), ALU.add).then_inc(conv_ready, 1)

            def mod_load(q, r):
                pool.dma_start(mring[:, r % 2, :], a["mod"][q, :, r * QUARTER:(r + 1) * QUARTER]).then_inc(mod_in[r % 2], 16)

            def mod_loads(first, end):
                with pool.Fori(first, end) as q:
                    for r in range(4):
                        pool.wait_ge(mod_used, q * 4 + (r - 1 - 4 * FIRST))
                        mod_load(q, r)

            for r in range(4):
                if r >= 2:
                    pool.wait_ge(mod_used, r - 1)
                mod_load(FIRST, r)
            wide(0, 0, 3).then_inc(gate_in, 16)
            mod_loads(FIRST + 1, MODQ)
            for r in range(4):
                if r == 2:
                    pool.wait_ge(x_ready, 2)
                    pool.dma_start(sel, a["sel"]).then_inc(late_in, 16)
                pool.wait_ge(mod_used, 4 * (MODQ - FIRST) + r - 1)
                mod_load(MODQ, r)
            mod_loads(MODQ + 1, 2 * MODQ)
            pool.wait_ge(x_ready, 6)
            wide(3, 0, 3).then_inc(gate_in, 16)
            pool.wait_ge(x_ready, 8)
            pool.dma_start(gate[:, 0, 0:GROUPS * T], a["dil_mask"]).then_inc(late_in, 16)
            pool.wait_ge(x_ready, 10)
            pool.dma_start(k2, a["konst2"]).then_inc(mix_in, 16)
            pool.dma_start(nsaw, a["nsaw"][0, :, :]).then_inc(mix_in, 16)
            pool.dma_start(mixw, a["mixw"][0, :, :]).then_inc(mix_in, 16)
            pool.wait_ge(x_ready, 12)
            wide(6, 0, 3).then_inc(gate_in, 16)
            convolution(0)
            pool.wait_ge(x_ready, 14)
            wide(9, 0, 1).then_inc(gate_in, 16)
            pool.dma_start(nsaw, a["nsaw"][1, :, :]).then_inc(mix_in, 16)
            pool.dma_start(mixw, a["mixw"][1, :, :]).then_inc(mix_in, 16)
            split(4)
            convolution(1)
            split(5)

        @block.tensor
        def _(pe):
            def quarter(q, it, per, lhs, out_of, first, last, ends=False):
                before = sum(p < q for p in POOL_Q)
                mine = sum(q <= p < q + per for p in POOL_Q)
                if q in POOL_Q:
                    pe.wait_ge(w_lo_pool, val(it, before + 1, mine))
                else:
                    pe.wait_ge(w_lo_ready, val(it, q + 1 - before, per - mine))
                slot, half, buf = (q // 2) % SLOTS, (q % 2) * QUARTER, q % SPLITS
                order = [(i, tt) for tt in range(NT) for i in range(2)] if ends else [(i, tt) for i in range(2) for tt in range(NT)]
                for n, (i, tt) in enumerate(order):
                    hi = w_hi[:, buf, i * 512:(i + 1) * 512]
                    lo = ring_lo[:, slot, half + i * 512:half + (i + 1) * 512]
                    x_hi, x_lo = lhs(i, tt)
                    dst = out_of(i, tt)
                    nc.tensor.matmul(dst, x_lo, hi, start=first(i), stop=False)
                    nc.tensor.matmul(dst, x_hi, lo, start=False, stop=False)
                    mm = nc.tensor.matmul(dst, x_hi, hi, start=False, stop=last(i))
                    if ends and n == 1:
                        mm.then_inc(tile_done, 1)
                mm.then_inc(quarter_done, 1)

            def up(q, bank, it=None, per=0, fresh=None):
                for r in range(4):
                    if fresh is not None:
                        pe.wait_ge(fresh[0], fresh[1] + r + 1)

                    def lhs(i, tt):
                        ts = slice(tt * P, (tt + 1) * P)
                        return h_hi[:, 2 * r + i, ts], h_lo[:, 2 * r + i, ts]
                    quarter(q + r, it, per, lhs, lambda i, tt: ps[:, bank + tt, :],
                            lambda i: r == 0 and i == 0, lambda i: r == 3 and i == 1)

            def down(q, kk, count, parts, bank):
                def lhs(i, tt):
                    return parts(kk, tt)
                quarter(q + kk, None, 0, lhs, lambda i, tt: ps[:, bank + 2 * tt + i, :], lambda i: kk == 0, lambda i: kk == count - 1, kk == count - 1)

            def h_parts(kk, tt):
                return h_hi[:, kk, tt * P:(tt + 1) * P], h_lo[:, kk, tt * P:(tt + 1) * P]

            def hid_parts(kk, tt):
                o = kk * T + tt * P
                return hid_hi[:, o:o + P], hid_lo[:, o:o + P]

            def norm(m):
                for tt in range(NT):
                    pe.wait_ge(xn_ready, 2 * m + tt + 1)
                for b in range(4):
                    for cc in range(2):
                        for tt in range(NT):
                            c = 2 * b + cc
                            mm = nc.tensor.transpose(ps[:, 4 + b, cc * T + tt * P:cc * T + (tt + 1) * P],
                                                     xn[:, tt, c * P:(c + 1) * P], ident)
                    mm.then_inc(norm_T, 1)

            def mod_cols(layer, subs):
                if layer == 0 and subs == [0]:
                    pe.wait_ge(first_done, FIRST)
                else:
                    pe.wait_ge(mod_used, 4 * (MODQ * layer + 6 * subs[-1] + 4 - FIRST))
                for s in subs:
                    for kind in range(2):
                        for c in range(KC):
                            o = (6 * s + 2 * kind) * 512 + c * P
                            at = (s * 2 + kind) * KC + c
                            mm = nc.tensor.matmul(ps[:, 0, at:at + 1], accs[:, o:o + P], ones[:, 0:1], start=True, stop=True)
                mm.then_inc(col_sum, 1)

            def gates(layer, subs, bank=6):
                pe.wait_ge(mod_used, 4 * (MODQ * layer + 6 * subs[-1] + 6 - FIRST))
                for s in subs:
                    for half in range(2):
                        g = 6 * layer + 2 * s + half
                        if g >= 2:
                            pe.wait_ge(gate_ready, g - 1)
                        o = (6 * s + 4 + half) * 512
                        nc.tensor.matmul(ps[:, bank + half, :], ones, accs[:, o:o + 512], start=True, stop=True).then_inc(gate_sum, 1)

            def ffn(f, conv, m):
                q0 = BASE[f"ffn{f}"]
                v0 = UPS * (f - 4) if conv else UPS * f

                def turn_hidden(j, it):
                    u, v = UPS * f + j, v0 + j
                    pe.wait_ge(tr_copied, val(it, u))
                    if conv:
                        pe.wait_ge(gu_ready, val(it, v + 1))
                        for c in range(4):
                            for tt in range(NT):
                                o = (c % 2) * T + tt * P
                                mm = nc.tensor.transpose(ps[:, 6 + c // 2, o:o + P], wa[:, tt * 512 + c * P:tt * 512 + (c + 1) * P], ident)
                    else:
                        pe.wait_ge(h_ready, val(it, v + 1))
                        for c in range(2):
                            for tt in range(NT):
                                o = c * T + tt * P
                                mm = nc.tensor.transpose(ps[:, 6, o:o + P], wb[:, tt * C2 + c * P:tt * C2 + (c + 1) * P], ident)
                    mm.then_inc(tr_done, 1)

                def step(j, it):
                    if f == 1 and j == 1:
                        pe.wait_ge(gate_ready, 6)
                    if v0 + j >= RING or it is not None:
                        pe.wait_ge(gu_ready if conv else h_ready, val(it, v0 + j - RING + 1))
                    up(q0 + 4 * j, UP_BANKS[j % 2], it, TURNQ, (norm_lo, 4 * m) if j == 0 else None)
                    if j > 0:
                        turn_hidden(j - 1, it)

                ahead = 1 if v0 == 0 else 0
                for j in range(PEEL + ahead * RING):
                    step(j, None)
                with pe.Fori(ahead, TURNS) as it:
                    for r in range(RING):
                        step(PEEL + r, it)
                early = DOWNQ // 2 - 1
                for kk in range(early):
                    down(q0 + UPQ, kk, DOWNQ, hid_parts, DOWN_BANK)
                turn_hidden(UPS - 1, None)
                for kk in range(early, DOWNQ):
                    if kk == DOWNQ - 2:
                        pe.wait_ge(tr_copied, UPS * (f + 1))
                        if f in (0, 2):
                            gates(f // 2, [0] if f == 0 else [0, 1, 2])
                    down(q0 + UPQ, kk, DOWNQ, hid_parts, DOWN_BANK)

            def qkv(q0, z0, w0, groups, m):
                def turn_qk(z, it):
                    pe.wait_ge(qn_ready, val(it, z + 1, 4))
                    pe.wait_ge(qk_copied, val(it, z, 4))
                    for pr in range(4):
                        for tt in range(NT):
                            o = (pr % 2) * T + tt * P
                            mm = nc.tensor.transpose(ps[:, 6 + pr // 2, o:o + P], wb[:, tt * 512 + pr * P:tt * 512 + (pr + 1) * P], ident)
                    mm.then_inc(qk_T, 1)

                def running_sums():
                    pe.wait_ge(lf_ready, 1)
                    lf = flog[:, 3, :]
                    nc.tensor.matmul(ps[0:HEADS, 5, 0:T], lf[:, 0:HEADS], ntri, start=True, stop=False)
                    nc.tensor.matmul(ps[0:HEADS, 5, P:T], lf[:, HEADS:2 * HEADS], ntri[:, 0:P], start=False, stop=True).then_inc(cum_sum, 1)

                def group(it):
                    for j in range(6):
                        if groups == 1 and j == 3:
                            running_sums()
                        if j >= 2:
                            pe.wait_ge(qk_read, val(it, z0 + j - 1, 4))
                        elif groups > 1:
                            pe.wait_ge(v_copied, val(it, w0 + j - 1, 2))
                        up(q0 + 4 * j, UP_BANKS[j % 2], it, 24, (norm_lo, 4 * m) if j == 0 else None)
                        if 1 <= j <= 4:
                            turn_qk(z0 + j - 1, it)

                if groups == 1:
                    group(None)
                else:
                    with pe.Fori(0, groups) as it:
                        group(it)

            def attention(G, a_0, qk_all, v_all, bufs, cum):
                SW = G * (T + P)
                prob = [bufs["s"][:, SW * (1 + i):SW * (2 + i)] for i in range(2)]
                probT = bufs["s"][:, 3 * SW:4 * SW]
                pe.wait_ge(qk_copied, qk_all)
                pe.wait_ge(v_copied, v_all)
                if cum:
                    pe.wait_ge(cum_ready, 1)
                    pe.wait_ge(late_in, 16)

                def scores(h):
                    q0 = (h % 2) * HD
                    if h > 0:
                        pe.wait_ge(max_ready, a_0 + h)
                    for tile, at, keys in ((1, 0, T), (0, 1024, P)):
                        for g in range(G):
                            o = at + g * keys
                            col = g * PAIRS * T + (h // 2) * T
                            mm = nc.tensor.matmul(psf[:, o:o + keys], bufs["qT"][q0:q0 + HD, col + tile * P:col + tile * P + P],
                                                  bufs["kT"][q0:q0 + HD, col:col + keys], start=True, stop=not cum)
                            if cum:
                                mm = nc.tensor.matmul(psf[:, o:o + keys], sel[:, h * P:(h + 1) * P], ncum[:, 0:keys],
                                                      start=False, stop=True)
                    mm.then_inc(s_done, 1)

                def turn_probs(h):
                    pe.wait_ge(exp_ready, a_0 + h + 1)
                    pe.wait_ge(pT_dve, a_0 + h)
                    if G > 1:
                        pe.wait_ge(pT_act, h)
                    for b in range(3 * G):
                        mm = nc.tensor.transpose(psf[:, 1536 + b * P:1536 + (b + 1) * P], prob[h % 2][:, b * P:(b + 1) * P], ident)
                    mm.then_inc(p_T, 1)

                def values(h):
                    pe.wait_ge(pT_dve, a_0 + h + 1)
                    if G > 1:
                        pe.wait_ge(pT_act, h + 1)
                    if h >= 2:
                        pe.wait_ge(o_ready, a_0 + h - 1)
                    o = (6 + h % 2) * 512

                    def v(g, tile):
                        return bufs["v"][:, g * 2048 + tile * D + h * HD:g * 2048 + tile * D + (h + 1) * HD]
                    for i in range(2 * G):
                        nc.tensor.matmul(psf[:, o + HD:o + 2 * HD], probT[:, i * P:(i + 1) * P], v(i // 2, i % 2),
                                         start=(i == 0), stop=(i == 2 * G - 1))
                    for i in range(G):
                        mm = nc.tensor.matmul(psf[:, o:o + HD], probT[:, (2 * G + i) * P:(2 * G + i + 1) * P], v(i, 0),
                                              start=(i == 0), stop=(i == G - 1))
                    mm.then_inc(o_sum, 1)

                for h in range(HEADS + 2):
                    if h < HEADS:
                        scores(h)
                    if 1 <= h <= HEADS:
                        turn_probs(h - 1)
                    if h >= 2:
                        values(h - 2)

            def attention_out(name, a_0, k):
                pe.wait_ge(o_ready, a_0 + HEADS)
                for b in range(4):
                    for cc in range(2):
                        for tt in range(NT):
                            c = 2 * b + cc
                            mm = nc.tensor.transpose(ps[:, b, cc * T + tt * P:cc * T + (tt + 1) * P], xn[:, tt, c * P:(c + 1) * P], ident)
                    mm.then_inc(o_T, 1)
                for kk in range(KC):
                    if kk % 2 == 0:
                        pe.wait_ge(oT_lo, 4 * k + kk // 2 + 1)
                    down(BASE[name], kk, KC, h_parts, 4)

            def mixer(l):
                q0 = BASE[f"mix{l}"]
                bA, bC, bD = MIX_BANKS[0:3]
                for j in range(3):
                    up(q0 + 4 * j, MIX_BANKS[j], None, 0, (norm_lo, 4 * (6 + 2 * l)) if j == 0 else None)
                pe.wait_ge(a_gated, l + 1)
                for c in range(2):
                    for tt in range(NT):
                        o = c * T + tt * P
                        mm = nc.tensor.transpose(ps[:, 6, o:o + P], ac[:, tt, c * P:(c + 1) * P], ident)
                mm.then_inc(a_T, 1)
                up(q0 + 12, MIX_BANKS[3])
                pe.wait_ge(rot_ready, l + 1)
                pe.wait_ge(c_copied, l + 1)
                pe.wait_ge(d_copied, l + 1)
                pe.wait_ge(cv_ready, l + 1)
                banks = [bC, bC + 1, bD, bD + 1, 6, 7]
                for b in range(12):
                    for tt in range(NT):
                        src = rot[:, tt, b * HD:(b + 1) * HD] if b < 6 else cq[:, tt, (384 + (b - 6) * HD if b < 8 else (b - 8) * HD):][:, 0:HD]
                        o = (b % 2) * T + tt * P
                        mm = nc.tensor.transpose(ps[0:HD, banks[b // 2], o:o + P], src, ident)
                mm.then_inc(q_T, 1)
                pe.wait_ge(mix_in, 48 + 32 * l)
                pe.wait_ge(blk_ready, l + 1)
                for w in range(2):
                    for e in range(CMP_LEN):
                        o = w * CMP_LEN * HD + e * HD
                        mm = nc.tensor.matmul(ps[0:HD, 6, w * 16:w * 16 + NCMP], nsaw[:, o:o + HD], blk[:, w, e, :],
                                              start=(e == 0), stop=(e == CMP_LEN - 1))
                mm.then_inc(hid_sum, 1)
                for g in range(4):
                    o = KONST2["pool"] + g * (T + P)
                    h0 = (g % 2) * HD
                    dst = ps[h0:h0 + HD, 7, (g // 2) * T:(g // 2) * T + T]
                    nc.tensor.matmul(dst, dv[:, 0, g * HD:(g + 1) * HD], k2[:, o:o + T], start=True, stop=False)
                    mm = nc.tensor.matmul(dst[:, P:T], dv[:, 1, g * HD:(g + 1) * HD], k2[:, o + T:o + T + P], start=False, stop=True)
                mm.then_inc(pool_sum, 1)
                pe.wait_ge(hid_ready, l + 1)
                o = 2 * CMP_LEN * HD
                nc.tensor.matmul(ps[0:HD, 6, 32:32 + NCMP], nsaw[:, o:o + HD], hid[:, 0:NCMP], start=True, stop=True)
                nc.tensor.matmul(ps[0:NCMP, 6, 64:64 + HD], hid[:, 16:16 + NCMP], nsaw[:, o + HD:o + 2 * HD], start=True, stop=True).then_inc(kv_sum, 1)
                pe.wait_ge(pool_copied, l + 1)
                for g in range(4):
                    h0 = (g % 2) * HD
                    mm = nc.tensor.matmul(ps[h0:h0 + HD, 7, (g // 2) * T:(g // 2) * T + T],
                                          mixw[h0:h0 + HD, 4 * P + (g // 2) * HD:4 * P + (g // 2 + 1) * HD],
                                          pT[h0:h0 + HD, (g // 2) * T:(g // 2) * T + T], start=True, stop=True)
                mm.then_inc(pool_mix, 1)
                pe.wait_ge(vn_ready, l + 1)
                pe.wait_ge(kv_ready, l + 1)
                for tt in range(NT):
                    for g in range(4):
                        mm = nc.tensor.matmul(ps[:, 6, tt * C2 + g * HD:tt * C2 + (g + 1) * HD], mixw[:, g * P:(g + 1) * P],
                                              vn[:, tt, g * HD:(g + 1) * HD], start=True, stop=True)
                mm.then_inc(sgu_sum, 1)

                def scores(h):
                    i = NH * l + h
                    if h >= 2:
                        pe.wait_ge(nmax_ready, i - 1)
                    bS = (bC, bA)[h % 2]
                    qr, qc = h * T, (8 + h) * T
                    for tile, keys, b in ((1, T, bS), (0, P, bS + 1)):
                        for w in range(2):
                            nc.tensor.matmul(ps[:, b, w * keys:(w + 1) * keys], qkT[:, qr + tile * P:qr + (tile + 1) * P],
                                             qkT[:, (4 + w) * T:(4 + w) * T + keys], start=True, stop=True)
                    for tile in range(NT):
                        o = 2 * P + tile * NCMP
                        mm = nc.tensor.matmul(ps[:, bS + 1, o:o + NCMP], qkT[:, qc + tile * P:qc + (tile + 1) * P], kcT,
                                              start=True, stop=True)
                    mm.then_inc(ns_done, 1)

                def turn_probs(h):
                    i = NH * l + h
                    pe.wait_ge(np_ready, i + 1)
                    pe.wait_ge(npT_copied, i)
                    pr = nsaP[h % 2]
                    for b in range(6):
                        o = b * P
                        nc.tensor.transpose(ps[:, bD + b // 4, (b % 4) * P:(b % 4 + 1) * P], pr[:, o:o + P], ident)
                    for tile in range(NT):
                        o = NS1 + 2 * P + tile * NCMP
                        mm = nc.tensor.transpose(ps[0:NCMP, bD + 1, 2 * P + tile * P:2 * P + (tile + 1) * P], pr[:, o:o + NCMP], ident)
                    mm.then_inc(np_T, 1)

                def values(h):
                    i = NH * l + h
                    pe.wait_ge(npT_copied, i + 1)
                    if h == 0:
                        pe.wait_ge(pool_out, l + 1)
                    vs = lambda w, tile: dv[:, tile, C2 + w * HD:C2 + (w + 1) * HD]
                    for b in range(4):
                        nc.tensor.matmul(ps[:, 7, h * P + HD:h * P + 2 * HD], nsaT[:, b * P:(b + 1) * P], vs(b // 2, b % 2), start=(b == 0), stop=False)
                    nc.tensor.matmul(ps[:, 7, h * P + HD:h * P + 2 * HD], nsaT[0:NCMP, 7 * P:8 * P], vc, start=False, stop=True)
                    for w in range(2):
                        nc.tensor.matmul(ps[:, 7, h * P:h * P + HD], nsaT[:, (4 + w) * P:(5 + w) * P], vs(w, 0), start=(w == 0), stop=False)
                    nc.tensor.matmul(ps[:, 7, h * P:h * P + HD], nsaT[0:NCMP, 6 * P:7 * P], vc, start=False, stop=True).then_inc(no_sum, 1)

                pe.wait_ge(b_gelu, l + 1)
                scores(0)
                scores(1)
                for h in range(NH + 1):
                    if h < NH:
                        turn_probs(h)
                    if h + 2 < NH:
                        scores(h + 2)
                    if h >= 1:
                        values(h - 1)
                pe.wait_ge(conv_ready, l + 1)
                mean = k2[:, KONST2["mean"]:KONST2["mean"] + P]
                for c in range(2):
                    mm = nc.tensor.matmul(ps[:, bA, 0:T], mean, cacc[:, c, :], start=(c == 0), stop=(c == 1))
                mm.then_inc(mu_sum, 1)
                pe.wait_ge(csq_ready, l + 1)
                for c in range(2):
                    mm = nc.tensor.matmul(ps[:, bA + 1, 0:T], mean, csq[:, c, :], start=(c == 0), stop=(c == 1))
                mm.then_inc(var_sum, 1)
                pe.wait_ge(sgu_ready, l + 1)
                for c in range(2):
                    for tt in range(NT):
                        mm = nc.tensor.transpose(ps[:, 6, c * T + tt * P:c * T + (tt + 1) * P], ysg[:, tt, c * P:(c + 1) * P], ident)
                mm.then_inc(sgu_T, 1)
                pe.wait_ge(no_copied, l + 1)
                for c in range(2):
                    for tt in range(NT):
                        mm = nc.tensor.transpose(ps[:, 7, c * T + tt * P:c * T + (tt + 1) * P], osm[:, tt, c * P:(c + 1) * P], ident)
                mm.then_inc(no_T, 1)
                for s in (sgu_out, no_out, conv_out):
                    pe.wait_ge(s, l + 1)
                for kk in range(KC):
                    down(BASE[f"mix{l}_out"], kk, KC, h_parts, 4)

            pe.wait_ge(x_in, 16 * 2)
            pe.wait_ge(konst_in, 16 * 3)
            norm(0)
            mod_cols(0, [0])
            ffn(0, False, 0)
            mod_cols(0, [1])
            norm(1)
            pe.wait_ge(norm_lo, 4 * 2)
            pe.wait_ge(wf_ready, 1)
            for tt in range(NT):
                for k in range(KC):
                    dst = ps[:, 4, tt * HEADS:(tt + 1) * HEADS]
                    x_hi, x_lo = h_parts(k, tt)
                    nc.tensor.matmul(dst, x_lo, wf_hi[:, k, :], start=(k == 0), stop=False)
                    nc.tensor.matmul(dst, x_hi, wf_lo[:, k, :], start=False, stop=False)
                    mm = nc.tensor.matmul(dst, x_hi, wf_hi[:, k, :], start=False, stop=(k == KC - 1))
            mm.then_inc(f_sum, 1)
            qkv(BASE["fox"], 0, 0, 1, 1)
            pe.wait_ge(qk_copied, 4)
            gates(0, [1])
            pe.wait_ge(gate_ready, 4)
            attention(1, 0, 4, 2, fox_bufs, True)
            attention_out("fox_out", 0, 0)
            mod_cols(0, [2])
            gates(0, [2], 2)
            norm(2)
            ffn(1, False, 2)
            mod_cols(1, [0, 1, 2])
            norm(3)
            ffn(2, False, 3)
            norm(4)
            qkv(BASE["dil"], 4, 2, GROUPS, 4)
            attention(GROUPS, HEADS, 4 + 4 * GROUPS, 2 + 2 * GROUPS, dil_bufs, False)
            attention_out("dil_out", HEADS, 1)
            norm(5)
            ffn(3, False, 5)
            for l in range(LAYERS):
                norm(6 + 2 * l)
                mixer(l)
                norm(7 + 2 * l)
                ffn(4 + l, True, 7 + 2 * l)

        @block.scalar
        def _(act):
            tick = Tick(act, act_tick)

            def split(first, end, it=None, per=0):
                for q in range(first, min(end, QUARTERS)):
                    half = q // 2
                    if q % 2 == 0 or q == first:
                        act.wait_ge(slot_full[half % SLOTS], val(it, 16 * (half // SLOTS + 1), 16 * (per // (2 * SLOTS))))
                    if q >= SPLITS:
                        act.wait_ge(quarter_done, val(it, q - SPLITS + 1, per))
                    nc.scalar.activation(w_hi[:, q % SPLITS, :], ring[:, half % SLOTS, (q % 2) * QUARTER:(q % 2 + 1) * QUARTER],
                                         ACT.Copy).then_inc(w_hi_ready, 1)

            def split_step(q, it=None, per=0):
                split(q + LEAD, q + LEAD + 4, it, per)

            def norm(m):
                for tt in range(NT):
                    if m > 0:
                        act.wait_ge(x_ready, 2 * (m - 1) + tt + 1)
                    tick.mark(nc.scalar.activation(xn[:, tt, :], x[:, tt, :], ACT.Square, scale=D ** -0.5, accum_out=ms[:, tt:tt + 1]))
                    tick.settle()
                    nc.scalar.activation(rms[:, tt:tt + 1], ms[:, tt:tt + 1], ACT.Sqrt, bias=eps_col).then_inc(ms_ready, 1)

            def norm_parts(m):
                if m <= 3:
                    act.wait_ge(col_ready, m + 1)
                for b in range(4):
                    act.wait_ge(norm_T, 4 * m + b + 1)
                    for c in (2 * b, 2 * b + 1):
                        src = ps[:, 4 + b, (c % 2) * T:(c % 2 + 1) * T]
                        if m < 6:
                            ins = nc.scalar.activation(h_hi[:, c, :], src, ACT.Identity, bias=modcol[:, m % 3, 0, c:c + 1],
                                                       scale=modcol[:, m % 3, 1, c:c + 1])
                        else:
                            g = (COLS["mix_pre"] if m % 2 == 0 else COLS["ffn_pre"]) + 8 * ((m - 6) // 2) + c
                            ins = nc.scalar.activation(h_hi[:, c, :], src, ACT.Copy, scale=cols[:, g:g + 1])
                    ins.then_inc(norm_hi, 1)

            def down_split(f):
                q0 = BASE[f"ffn{f}"] + UPQ
                turned = q0 + DOWNQ // 2 - 1 + SPLITS
                split(q0 + LEAD, turned)
                keep_hi(f, UPS - 1, None)
                split(turned, q0 + DOWNQ + LEAD)

            def keep_hi(f, j, it):
                act.wait_ge(tr_done, val(it, UPS * f + j + 1))
                o = val(it, j * 512, RING * 512)
                nc.scalar.activation(hid_hi[:, bass.ds(o, 512)], ps[:, 6, :], ACT.Copy).then_inc(hid_hi_ready, 1)

            def ffn(f):
                q0 = BASE[f"ffn{f}"]

                def step(j, it):
                    u, b = UPS * f + j, UP_BANKS[j % 2]
                    split_step(q0 + 4 * j, it, TURNQ)
                    act.wait_ge(quarter_done, val(it, q0 + 4 * j + 4, TURNQ))
                    act.wait_ge(h_ready, val(it, u))
                    nc.scalar.activation(wa[:, 0:512].rearrange("p (t n) -> p t n", t=NT), ps[:, b:b + 2, 0:C2],
                                         ACT.Silu).then_inc(silu_ready, 1)
                    if j > 0:
                        keep_hi(f, j - 1, it)
                for j in range(PEEL):
                    step(j, None)
                with act.Fori(0, TURNS) as it:
                    for r in range(RING):
                        step(PEEL + r, it)
                down_split(f)

            def ffn_conv(f):
                q0, v0 = BASE[f"ffn{f}"], UPS * (f - 4)

                def gelu(j, it):
                    v = v0 + j
                    act.wait_ge(fconv_ready, val(it, v + 1))
                    nc.scalar.activation(wc[:, 0:512], wb[:, 0:512], ACT.Gelu_apprx_tanh).then_inc(gelu_ready, 1)

                def step(j, it):
                    u, b = UPS * f + j, UP_BANKS[j % 2]
                    split_step(q0 + 4 * j, it, TURNQ)
                    act.wait_ge(quarter_done, val(it, q0 + 4 * j + 4, TURNQ))
                    act.wait_ge(tr_done, val(it, u))
                    nc.scalar.activation(wa[:, :], psf[:, b * 512:(b + 2) * 512], ACT.Copy).then_inc(gu_ready, 1)
                    if j > 0:
                        gelu(j - 1, it)
                for j in range(PEEL):
                    step(j, None)
                with act.Fori(0, TURNS) as it:
                    for r in range(RING):
                        step(PEEL + r, it)
                turned = q0 + UPQ + DOWNQ // 2 - 1 + SPLITS
                split(q0 + UPQ + LEAD, turned)
                gelu(UPS - 1, None)
                split(turned, q0 + UPQ + DOWNQ + LEAD)

            def qkv(q0, z0, w0, bufs, groups):
                def group(it):
                    def at(c, per):
                        return c if it is None else it * per + c

                    def copy_qk(z, j):
                        act.wait_ge(qk_T, at(z + 1, 4))
                        buf = bufs["qT"] if j < 2 else bufs["kT"]
                        o = at((j % 2) * 1024, PAIRS * T)
                        nc.scalar.activation(buf[:, bass.ds(o, 1024)], psf[:, 6 * 512:8 * 512], ACT.Copy).then_inc(qk_copied, 1)

                    for j in range(6):
                        split_step(q0 + 4 * j, it, 24)
                        act.wait_ge(quarter_done, at(q0 + 4 * j + 4, 24))
                        b = UP_BANKS[j % 2]
                        if j < 4:
                            act.wait_ge(qk_read, at(z0 + j, 4))
                            nc.scalar.activation(wa[:, :], psf[:, b * 512:(b + 2) * 512], ACT.Square, scale=HD ** -0.5).then_inc(sq_ready, 1)
                            act.wait_ge(ss_ready, at(z0 + j + 1, 4))
                            nc.scalar.activation(rs16[:, :], ss16[:, :], ACT.Sqrt, bias=eps_col).then_inc(rs_ready, 1)
                        else:
                            for tt in range(NT):
                                o = at(tt * D + (j - 4) * 512, 2048)
                                ins = nc.scalar.activation(bufs["v"][:, bass.ds(o, 512)], ps[:, b + tt, :], ACT.Copy)
                            ins.then_inc(v_copied, 1)
                        if 1 <= j <= 4:
                            copy_qk(z0 + j - 1, j - 1)
                if groups == 1:
                    group(None)
                else:
                    with act.Fori(0, groups) as it:
                        group(it)

            def attention(G, a_0, bufs):
                SW, S1 = G * (T + P), G * T
                s = bufs["s"]
                prob = [s[:, SW * (1 + i):SW * (2 + i)] for i in range(2)]
                probT = s[:, 3 * SW:4 * SW]
                for h in range(HEADS + 1):
                    if h < HEADS:
                        act.wait_ge(max_ready, a_0 + h + 1)
                        if h >= 2:
                            act.wait_ge(p_T, a_0 + h - 1)
                        for i, (lo, hi) in enumerate(((0, S1), (S1, SW))):
                            ins = nc.scalar.activation(prob[h % 2][:, lo:hi], s[:, lo:hi], ACT.Exp, scale=-1.0,
                                                       bias=nmax[:, h % 2, i:i + 1], accum_out=lsum[:, h % 4, i:i + 1])
                        ins.then_inc(exp_ready, 1)
                    if h >= 1:
                        act.wait_ge(p_T, a_0 + h)
                        if h >= 2:
                            act.wait_ge(o_sum, a_0 + h - 1)
                        if G > 1:
                            nc.scalar.activation(probT[:, 512:1024], psf[:, 2048:2560], ACT.Copy).then_inc(pT_act, 1)

            def attention_out(k, name):
                for b in range(4):
                    act.wait_ge(o_T, 4 * k + b + 1)
                    nc.scalar.activation(h_hi[:, 2 * b:2 * b + 2, :].rearrange("p c t -> p (c t)"), ps[:, b, :], ACT.Copy).then_inc(oT_hi, 1)
                split(BASE[name] + 4, BASE[name] + 8 + LEAD)

            def mixer(l):
                q0 = BASE[f"mix{l}"]
                bA, bC, bD = MIX_BANKS[0:3]
                split_step(q0)
                act.wait_ge(quarter_done, q0 + 4)
                nc.scalar.activation(wb[:, 0:512].rearrange("p (t n) -> p t n", t=NT), ps[:, bA:bA + 2, C2:2 * C2], ACT.Sigmoid).then_inc(a_sig, 1)
                split_step(q0 + 4)
                act.wait_ge(quarter_done, q0 + 8)
                nc.scalar.activation(cq[:, :, 0:C2], ps[:, bC:bC + 2, 0:C2], ACT.Copy, scale=HD ** -0.5)
                nc.scalar.activation(cq[:, :, C2:512], ps[:, bC:bC + 2, C2:512], ACT.Copy).then_inc(c_copied, 1)
                split_step(q0 + 8)
                act.wait_ge(quarter_done, q0 + 12)
                nc.scalar.activation(gt[:, :, :], ps[:, bD:bD + 2, 384:396], ACT.Sigmoid)
                nc.scalar.activation(dv[:, :, :], ps[:, bD:bD + 2, 0:384], ACT.Copy).then_inc(d_copied, 1)
                act.wait_ge(a_T, l + 1)
                nc.scalar.activation(cv[:, :, TAPS - 1:CVW], ps[:, 6, :].rearrange("p (c t) -> p c t", c=2), ACT.Copy).then_inc(cv_ready, 1)
                split(q0 + 15, q0 + 20)
                act.wait_ge(quarter_done, q0 + 16)
                act.wait_ge(rot_ready, l + 1)
                nc.scalar.activation(zg[:, :, :], ps[:, bA:bA + 2, :], ACT.Gelu_apprx_tanh).then_inc(b_gelu, 1)
                act.wait_ge(q_T, l + 1)
                for i, b in enumerate((bC, bD, 6)):
                    ins = nc.scalar.activation(qkT[:, i * 1024:(i + 1) * 1024], psf[0:HD, b * 512:(b + 2) * 512], ACT.Copy)
                ins.then_inc(qkT_ready, 1)
                act.wait_ge(hid_sum, l + 1)
                nc.scalar.activation(hid.rearrange("p (w n) -> p w n", w=2)[:, :, 0:NCMP],
                                     ps[0:HD, 6, 0:32].rearrange("p (w n) -> p w n", w=2)[:, :, 0:NCMP], ACT.Gelu_apprx_tanh).then_inc(hid_ready, 1)
                act.wait_ge(zvar_ready, l + 1)
                nc.scalar.activation(lnv[:, 4:6], lnv[:, 0:4].rearrange("p (t w) -> p t w", t=NT)[:, :, 1], ACT.Sqrt, bias=ln_eps_col).then_inc(zstd_ready, 1)
                act.wait_ge(pool_sum, l + 1)
                nc.scalar.activation(pT, ps[:, 7, :], ACT.Copy).then_inc(pool_copied, 1)
                act.wait_ge(pool_mix, l + 1)
                for c in range(2):
                    o = COLS["pool_s"] + 2 * l + c
                    ins = nc.scalar.activation(h_hi[:, 6 + c, :], ps[:, 7, c * T:(c + 1) * T], ACT.Copy, scale=cols[:, o:o + 1])
                ins.then_inc(pool_hi, 1)
                segs = [(0, T), (T, 2 * T), (NS1, NS1 + P), (NS1 + P, NS1 + 2 * P),
                        (NS1 + 2 * P, NS1 + 2 * P + NCMP), (NS1 + 2 * P + NCMP, NS1 + NS0)]
                for h in range(NH + 1):
                    i = NH * l + h
                    if h < NH:
                        act.wait_ge(nmax_ready, i + 1)
                        if h >= 2:
                            act.wait_ge(np_T, i - 1)
                        for k, (lo, hi) in enumerate(segs):
                            ins = nc.scalar.activation(nsaP[h % 2][:, lo:hi], nsaS[h % 2][:, lo:hi], ACT.Exp, scale=-1.0,
                                                       bias=nmax[:, h % 2, k:k + 1], accum_out=lsum[:, h % 4, k:k + 1])
                        ins.then_inc(nexp_ready, 1)
                    if h >= 1:
                        act.wait_ge(nexp_ready, i)
                        act.wait_ge(nw_ready, i)
                        for k, (lo, hi) in enumerate(segs):
                            pr = nsaP[(h - 1) % 2][:, lo:hi]
                            ins = nc.scalar.activation(pr, pr, ACT.Copy, scale=rsum[:, (h - 1) % 2, k:k + 1])
                        ins.then_inc(np_ready, 1)
                act.wait_ge(cd_ready, l + 1)
                nc.scalar.activation(csq[:, :, :], cd[:, :, :], ACT.Square).then_inc(csq_ready, 1)
                act.wait_ge(var_sum, l + 1)
                nc.scalar.activation(wb[:, 0:T], ps[:, bA + 1, 0:T], ACT.Sqrt, bias=ln_eps_col).then_inc(cstd_ready, 1)
                act.wait_ge(sgu_T, l + 1)
                nc.scalar.activation(h_hi[:, 4:6, :].rearrange("p c t -> p (c t)"), ps[:, 6, :], ACT.Copy).then_inc(sgu_hi, 1)
                act.wait_ge(no_T, l + 1)
                nc.scalar.activation(h_hi[:, 2:4, :].rearrange("p c t -> p (c t)"), ps[:, 7, :], ACT.Copy).then_inc(no_hi, 1)
                act.wait_ge(cn_ready, l + 1)
                for c in range(2):
                    g, b = COLS["conv_g"] + 2 * l + c, COLS["conv_lb"] + 2 * l + c
                    tick.mark(nc.scalar.activation(hT[:, c, :], cd[:, c, :], ACT.Silu, scale=cols[:, g:g + 1], bias=cols[:, b:b + 1]))
                tick.settle()
                nc.scalar.activation(h_hi[:, 0:2, :], hT[:, 0:2, :], ACT.Copy).then_inc(conv_hi, 1)
                split(q0 + 20, q0 + 24 + LEAD)

            def post_norm(end, k, bank):
                for tt in range(NT):
                    if tt == 0:
                        act.wait_ge(tile_done, 6 + k + 1)
                    else:
                        act.wait_ge(quarter_done, end)
                    o = (bank + 2 * tt) * 512
                    tick.mark(nc.scalar.activation(xn[:, tt, :], psf[:, o:o + D], ACT.Square, scale=D ** -0.5, accum_out=ms[:, 2 + tt:3 + tt]))
                    tick.settle()
                    nc.scalar.activation(rms[:, 2 + tt:3 + tt], ms[:, 2 + tt:3 + tt], ACT.Sqrt, bias=eps_col).then_inc(yms_ready, 1)

            act.dma_start(cols[:, :], a["cols"]).then_inc(cols_in, 16)
            act.dma_start(x[:, :, :], a["x"]).then_inc(x_in, 16)
            act.dma_start(konst[:, :], a["konst"]).then_inc(x_in, 16)
            act.wait_ge(cols_in, 16)
            nc.scalar.activation(cact[:, :], cols[:, COLS["c"]:COLS["c"] + KC], ACT.Silu).then_inc(cact_ready, 1)
            act.wait_ge(x_in, 16 * 2)
            act.wait_ge(konst_in, 16 * 3)
            norm(0)
            nc.scalar.activation(wf_hi[:, :, :], wf[:, :, :], ACT.Copy).then_inc(wf_hi_ready, 1)
            split(0, LEAD)
            norm_parts(0)
            ffn(0)
            norm(1)
            norm_parts(1)
            act.wait_ge(f_abs, 1)
            tick.mark(nc.scalar.activation(flog[:, 2, :], flog[:, 1, :], ACT.Exp, scale=-1.0))
            tick.settle()
            nc.scalar.activation(flog[:, 3, :], flog[:, 2, :], ACT.Ln, bias=1.0).then_inc(f_ln, 1)
            qkv(BASE["fox"], 0, 0, fox_bufs, 1)
            act.wait_ge(ang_ready, 1)
            nc.scalar.activation(rope[:, :, :, :].rearrange("p w t n -> p (w t n)"),
                                 rtmp[:, 0:2, :].rearrange("p w n -> p (w n)"), ACT.Sin).then_inc(rope_ready, 1)
            split(BASE["fox_out"] + LEAD, BASE["fox_out"] + 4)
            attention(1, 0, fox_bufs)
            attention_out(0, "fox_out")
            norm(2)
            norm_parts(2)
            ffn(1)
            norm(3)
            norm_parts(3)
            ffn(2)
            norm(4)
            norm_parts(4)
            qkv(BASE["dil"], 4, 2, dil_bufs, GROUPS)
            split(BASE["dil_out"] + LEAD, BASE["dil_out"] + 4)
            attention(GROUPS, HEADS, dil_bufs)
            attention_out(1, "dil_out")
            norm(5)
            norm_parts(5)
            ffn(3)
            for l in range(LAYERS):
                norm(6 + 2 * l)
                norm_parts(6 + 2 * l)
                mixer(l)
                post_norm(BASE[f"mix{l}_out"] + 8, 2 * l, 4)
                norm(7 + 2 * l)
                norm_parts(7 + 2 * l)
                ffn_conv(4 + l)
                post_norm(BASE[f"ffn{4 + l}"] + UPQ + DOWNQ, 2 * l + 1, DOWN_BANK)

        @block.vector
        def _(dve):
            v = nc.vector
            tick = Tick(dve, dve_tick)

            def col(name, i):
                return cols[:, COLS[name] + i:COLS[name] + i + 1]

            def split(first, end, it=None, per=0):
                for q in range(first, min(end, QUARTERS)):
                    if q in POOL_Q:
                        continue
                    dve.wait_ge(w_hi_ready, val(it, q + 1, per))
                    slot, cs = (q // 2) % SLOTS, slice((q % 2) * QUARTER, (q % 2 + 1) * QUARTER)
                    v.tensor_tensor(ring_lo[:, slot, cs], ring[:, slot, cs], w_hi[:, q % SPLITS, :], ALU.subtract).then_inc(w_lo_ready, 1)

            def split_step(q, it=None, per=0):
                split(q + LEAD, q + LEAD + 4, it, per)

            def norm(m):
                for tt in range(NT):
                    dve.wait_ge(ms_ready, 2 * m + tt + 1)
                    tick.mark(v.reciprocal(rstd[:, tt:tt + 1], rms[:, tt:tt + 1]))
                    tick.settle()
                    v.tensor_scalar(xn[:, tt, :], x[:, tt, :], rstd[:, tt:tt + 1], None, ALU.mult).then_inc(xn_ready, 1)

            def norm_parts(m):
                for b in range(4):
                    dve.wait_ge(norm_hi, 4 * m + b + 1)
                    for c in (2 * b, 2 * b + 1):
                        src = ps[:, 4 + b, (c % 2) * T:(c % 2 + 1) * T]
                        if m < 6:
                            tick.mark(v.tensor_scalar(hT[:, c, :], src, modcol[:, m % 3, 1, c:c + 1], modcol[:, m % 3, 0, c:c + 1], ALU.mult, ALU.add))
                        else:
                            g = col("mix_pre" if m % 2 == 0 else "ffn_pre", 8 * ((m - 6) // 2) + c)
                            ins = v.scalar_tensor_tensor(out=h_lo[:, c, :], in0=src, scalar=g, in1=h_hi[:, c, :], op0=ALU.mult, op1=ALU.subtract)
                    if m < 6:
                        tick.settle()
                        two = slice(2 * b, 2 * b + 2)
                        ins = v.tensor_tensor(h_lo[:, two, :], hT[:, two, :], h_hi[:, two, :], ALU.subtract)
                    ins.then_inc(norm_lo, 1)

            def mod_begin(first, end):
                for q in range(first, end):
                    dve.wait_ge(first_in[q], 16 * len(mod_first[q]))
                    dst = accs[:, q * 512:(q + 1) * 512]
                    for k in range(KC):
                        at, part = k * 512, mod_first[q][0]
                        if at >= part.shape[1]:
                            at, part = at - part.shape[1], mod_first[q][1]
                        src, c = part[:, at:at + 512], cact[:, k:k + 1]
                        if k == 0:
                            tick.mark(v.tensor_scalar(dst, src, c, None, ALU.mult))
                            continue
                        tick.settle()
                        ins = v.scalar_tensor_tensor(out=dst, in0=src, scalar=c, in1=dst, op0=ALU.mult, op1=ALU.add)
                        if k < KC - 1:
                            tick.mark(ins)
                    ins.then_inc(first_done, 1)

            def mod_quarter(q, big, r):
                tmp = wc[:, 0:512]
                dve.wait_ge(mod_in[r % 2], big * 32 + 16 * (r // 2 + 1))
                for i in range(2):
                    src, c = mring[:, r % 2, i * 512:(i + 1) * 512], cact[:, 2 * r + i:2 * r + i + 1]
                    if i == 1:
                        tick.settle()
                    elif r > 0 or not (isinstance(big, int) and big == 0):
                        dve.wait_ge(mod_used, big * 4 + r)
                    if r == 0 and i == 0:
                        tick.mark(v.tensor_scalar(tmp, src, c, None, ALU.mult))
                        continue
                    dst = accs[:, bass.ds(q * 512, 512)] if r == 3 and i == 1 else tmp
                    ins = v.scalar_tensor_tensor(out=dst, in0=src, scalar=c, in1=tmp, op0=ALU.mult, op1=ALU.add)
                    if i == 1:
                        ins.then_inc(mod_used, 1)
                    else:
                        tick.mark(ins)

            def mod_cols(layer, subs, k):
                dve.wait_ge(col_sum, k)
                for s in subs:
                    b = COLS["mod_b"] + layer * 72 + s * 24
                    tick.mark(v.tensor_tensor(modcol[:, s, :, :].rearrange("p w c -> p (w c)"), ps[:, 0, s * 16:s * 16 + 16],
                                              cols[:, b:b + 16], ALU.add))
                tick.settle()
                for s in subs:
                    g = COLS["norm_g"] + layer * 24 + s * 8
                    ins = v.scalar_tensor_tensor(out=modcol[:, s, 1, :], in0=modcol[:, s, 1, :], scalar=1.0, in1=cols[:, g:g + 8],
                                                 op0=ALU.add, op1=ALU.mult)
                ins.then_inc(col_ready, 1)
                dve.wait_ge(col_ready, k)

            def gates(layer, subs, bank=6):
                for s in subs:
                    for half in range(2):
                        dve.wait_ge(gate_sum, 6 * layer + 2 * s + half + 1)
                        g = gate[:, s, half * 512:(half + 1) * 512]
                        v.tensor_tensor(g, ps[:, bank + half, :], g, ALU.add).then_inc(gate_ready, 1)

            def update(u, end, s, weight, bank):
                w = (wa, wb)
                for tt in range(NT):
                    if tt == 0:
                        dve.wait_ge(tile_done, u + 1)
                    else:
                        dve.wait_ge(quarter_done, end)
                    o = (bank + 2 * tt) * 512
                    tick.mark(v.scalar_tensor_tensor(out=w[tt][:, :], in0=psf[:, o:o + D], scalar=weight, in1=gate[:, s, :],
                                                     op0=ALU.mult, op1=ALU.mult))
                    tick.settle()
                    v.tensor_tensor(x[:, tt, :], x[:, tt, :], w[tt][:, :], ALU.add).then_inc(x_ready, 1)

            def update_normed(k, s, bank):
                w = (wa, wb)
                for tt in range(NT):
                    dve.wait_ge(yms_ready, 2 * k + tt + 1)
                    tick.mark(v.reciprocal(rstd[:, 2 + tt:3 + tt], rms[:, 2 + tt:3 + tt]))
                    o = (bank + 2 * tt) * 512
                    tick.settle()
                    tick.mark(v.scalar_tensor_tensor(out=w[tt][:, :], in0=psf[:, o:o + D], scalar=rstd[:, 2 + tt:3 + tt],
                                                     in1=gate[:, s, :], op0=ALU.mult, op1=ALU.mult))
                    tick.settle()
                    v.tensor_tensor(x[:, tt, :], x[:, tt, :], w[tt][:, :], ALU.add).then_inc(x_ready, 1)

            def ffn(f):
                q0 = BASE[f"ffn{f}"]
                m0 = FIRST if f in (0, 1) else None

                def keep(j, it):
                    dve.wait_ge(hid_hi_ready, val(it, UPS * f + j + 1))
                    o = val(it, j * 512, RING * 512)
                    v.tensor_tensor(hid_lo[:, bass.ds(o, 512)], ps[:, 6, :], hid_hi[:, bass.ds(o, 512)], ALU.subtract).then_inc(tr_copied, 1)

                def step(j, it):
                    u, b = UPS * f + j, UP_BANKS[j % 2]
                    for r in range(4):
                        split(q0 + 4 * j + LEAD + r, q0 + 4 * j + LEAD + r + 1, it, TURNQ)
                        if m0 is not None:
                            q = val(it, m0 + j)
                            mod_quarter(q, q + (MODQ * f - FIRST), r)
                    dve.wait_ge(silu_ready, val(it, u + 1))
                    dve.wait_ge(tr_done, val(it, u))
                    v.tensor_tensor(wb[:, 0:512].rearrange("p (t n) -> p t n", t=NT), ps[:, b:b + 2, C2:512],
                                    wa[:, 0:512].rearrange("p (t n) -> p t n", t=NT), ALU.mult).then_inc(h_ready, 1)
                    if j > 0:
                        keep(j - 1, it)

                for j in range(PEEL):
                    step(j, None)
                with dve.Fori(0, TURNS) as it:
                    tick.enter(it, 4 * RING if m0 is not None else 0)
                    for r in range(RING):
                        step(PEEL + r, it)
                tick.leave(TURNS)
                d0 = q0 + UPQ
                turned = d0 + DOWNQ // 2 - 1 + SPLITS
                rest = [(q, r) for q in range(m0 + UPS, MODQ) for r in range(4)] if m0 is not None else []
                for q in range(d0 + LEAD, d0 + DOWNQ + LEAD):
                    if q == turned:
                        keep(UPS - 1, None)
                    if q == d0 + DOWNQ - 2 and f in (0, 2):
                        dve.wait_ge(gate_in, 16 if f == 0 else 32)
                        gates(f // 2, [0] if f == 0 else [0, 1, 2])
                    split(q, q + 1)
                    if rest:
                        mq, r = rest.pop(0)
                        mod_quarter(mq, mq + MODQ * f - FIRST, r)
                assert not rest
                if f in (0, 2):
                    dve.wait_ge(gate_ready, 2 if f == 0 else 12)
                update((0, 2, 3, 5)[f], d0 + DOWNQ, 0 if f in (0, 2) else 2, 0.5, DOWN_BANK)

            def ffn_conv(f):
                q0, v0, l = BASE[f"ffn{f}"], UPS * (f - 4), f - 4
                acc = wb[:, :].rearrange("p (c t) -> p c t", c=4)

                def conv(j, it):
                    u, y = UPS * f + j, v0 + j
                    dve.wait_ge(tr_done, val(it, u + 1))

                    def src(c, lag):
                        return ps[:, 6 + c // 2, (c % 2) * T:(c % 2) * T + T - lag]
                    fw = COLS["fc_w"]
                    for c in range(4):
                        o = (c // 2) * FC + (c % 2) + 2 * j
                        w = [cols[:, bass.ds(val2(it, COLS["fc_w"] + (l * 3 + k) * 44 + o), 1)] for k in range(3)]
                        b = cols[:, bass.ds(val2(it, COLS["fc_b"] + l * 44 + o), 1)]
                        tick.mark(v.tensor_scalar(acc[:, c, :], src(c, 0), w[2], b, ALU.mult, ALU.add))
                    for lag in (1, 2):
                        for c in range(4):
                            o = (c // 2) * FC + (c % 2) + 2 * j
                            w = cols[:, bass.ds(val2(it, COLS["fc_w"] + (l * 3 + 2 - lag) * 44 + o), 1)]
                            tick.settle(3)
                            ins = v.scalar_tensor_tensor(out=acc[:, c, lag:T], in0=src(c, lag), scalar=w, in1=acc[:, c, lag:T],
                                                         op0=ALU.mult, op1=ALU.add)
                            if lag == 2 and c == 3:
                                ins.then_inc(fconv_ready, 1)
                            else:
                                tick.mark(ins)

                def val2(it, c):
                    return c if it is None else it * (2 * RING) + c

                def join(j, it):
                    y = v0 + j
                    dve.wait_ge(gelu_ready, val(it, y + 1))
                    o = bass.ds(val(it, j * 512, RING * 512), 512)
                    tick.mark(v.tensor_tensor(hid_whole[:, o], wc[:, 0:512], wb[:, 512:1024], ALU.mult))
                    tick.mark(v.tensor_tensor(hid_hi[:, o], wc[:, 0:512], wb[:, 512:1024], ALU.mult))
                    tick.settle()
                    v.tensor_tensor(hid_lo[:, o], hid_whole[:, o], hid_hi[:, o], ALU.subtract).then_inc(tr_copied, 1)

                def step(j, it):
                    split_step(q0 + 4 * j, it, TURNQ)
                    if j > 0:
                        conv(j - 1, it)
                        join(j - 1, it)

                for j in range(PEEL):
                    step(j, None)
                with dve.Fori(0, TURNS) as it:
                    tick.enter(it, 13 * RING)
                    for r in range(RING):
                        step(PEEL + r, it)
                tick.leave(TURNS)
                d0 = q0 + UPQ
                turned = d0 + DOWNQ // 2 - 1 + SPLITS
                split(d0 + LEAD, turned)
                conv(UPS - 1, None)
                join(UPS - 1, None)
                split(turned, d0 + DOWNQ + LEAD)

            def angles():
                posf = rtmp[:, 3, 0:NT]
                freq = rows[:, ROWS["inv_freq"]:ROWS["inv_freq"] + ROPE_HALF]
                tick.mark(v.tensor_copy(posf, pos[:, :]))
                tick.settle()
                ang = rtmp[:, 2, :]
                for tt in range(NT):
                    tick.mark(v.tensor_scalar(ang[:, tt * ROPE_HALF:(tt + 1) * ROPE_HALF], freq, posf[:, tt:tt + 1], None, ALU.mult))
                for w, turn in ((0, 0.25), (1, 0.0)):
                    r, n = rtmp[:, w, :], rtmp[:, 3, :]
                    tick.settle()
                    tick.mark(v.tensor_scalar(n, ang, 1.0 / (2.0 * np.pi), turn, ALU.mult, ALU.add))
                    tick.settle()
                    tick.mark(v.tensor_scalar(n, n, ROUND, -ROUND, ALU.add, ALU.add))
                    for i, part in enumerate(TWO_PI):
                        tick.settle()
                        tick.mark(v.scalar_tensor_tensor(out=r, in0=n, scalar=-part, in1=(ang if i == 0 else r), op0=ALU.mult, op1=ALU.add))
                    tick.settle()
                    tick.mark(v.tensor_scalar(r, r, turn * 2.0 * np.pi, 3.1415925, ALU.add, ALU.min))
                    tick.settle()
                    ins = v.tensor_scalar(r, r, -3.1415925, None, ALU.max)
                    tick.mark(ins)
                tick.settle()
                v.tensor_copy(rtmp[:, 3, 0:1], rtmp[:, 0, 0:1]).then_inc(ang_ready, 1)

            def forget_logit():
                bf = rows[:, ROWS["b_f"]:ROWS["b_f"] + HEADS].unsqueeze(1).broadcast_to([P, NT, HEADS])
                dve.wait_ge(f_sum, 1)
                tick.mark(v.tensor_tensor(flog[:, 0, :].rearrange("p (t h) -> p t h", t=NT),
                                          ps[:, 4, 0:NT * HEADS].rearrange("p (t h) -> p t h", t=NT), bf, ALU.add))
                tick.settle()
                v.scalar_tensor_tensor(out=flog[:, 1, :], in0=flog[:, 0, :], scalar=-1.0, in1=flog[:, 0, :], op0=ALU.mult, op1=ALU.max).then_inc(f_abs, 1)
                dve.wait_ge(f_abs, 1)
                tick.mark(v.tensor_scalar(flog[:, 0, :], flog[:, 0, :], 0.0, None, ALU.min))

            def forget_log():
                tick.settle()
                dve.wait_ge(f_ln, 1)
                v.tensor_tensor(flog[:, 3, :], flog[:, 0, :], flog[:, 3, :], ALU.subtract).then_inc(lf_ready, 1)

            def forget_sums():
                dve.wait_ge(cum_sum, 1)
                v.tensor_copy(ncum[:, :], ps[0:HEADS, 5, 0:T]).then_inc(cum_ready, 1)

            def qk(q0, z0, groups):
                def group(it):
                    def at(c, per):
                        return c if it is None else it * per + c
                    for j in range(4):
                        z, b = z0 + j, UP_BANKS[j % 2]
                        split_step(q0 + 4 * j, it, 24)
                        if groups == 1 and j == 1:
                            forget_log()
                        heads = psf[:, b * 512:(b + 2) * 512].rearrange("p (h d) -> p h d", d=HD)
                        qn = wb[:, :].rearrange("p (h d) -> p h d", d=HD)
                        dve.wait_ge(sq_ready, at(z + 1, 4))
                        v.tensor_reduce(ss16[:, :], wa[:, :].rearrange("p (h d) -> p h d", d=HD), AX.X, ALU.add).then_inc(ss_ready, 1)
                        dve.wait_ge(rs_ready, at(z + 1, 4))
                        tick.mark(v.reciprocal(rs16[:, :], rs16[:, :]))
                        tick.settle()
                        dve.wait_ge(qk_T, at(z, 4))
                        v.tensor_tensor(qn, heads, rs16[:, :].unsqueeze(2).broadcast_to([P, 16, HD]), ALU.mult).then_inc(qk_read, 1)
                        dve.wait_ge(qk_read, at(z + 1, 4))
                        name = ("fox_" if groups == 1 else "dil_") + ("q" if j < 2 else "k")
                        gain = rows[:, bass.ds(at(ROWS[name], HD), HD)].unsqueeze(1).broadcast_to([P, 16, HD])
                        ins = v.scalar_tensor_tensor(out=qn, in0=qn, scalar=HD ** -0.5 if j < 2 else 1.0, in1=gain, op0=ALU.mult, op1=ALU.mult)
                        if groups == 1:
                            ins.then_inc(qn_ready, 1)
                            continue
                        tick.mark(ins)
                        tick.settle()
                        qv = wb[:, :].rearrange("p (t h d) -> p t h d", t=NT, d=HD)
                        x1, x2 = qv[:, :, :, 0:ROPE_HALF], qv[:, :, :, ROPE_HALF:2 * ROPE_HALF]
                        c, s = [rope[:, w, :, :].unsqueeze(2).broadcast_to([P, NT, 8, ROPE_HALF]) for w in range(2)]
                        t = [wc[:, i * P:(i + 1) * P].rearrange("p (t h d) -> p t h d", t=NT, d=ROPE_HALF) for i in range(4)]
                        for dst, xx, cs in ((t[0], x1, c), (t[1], x2, s), (t[2], x2, c), (t[3], x1, s)):
                            tick.mark(v.tensor_tensor(dst, xx, cs, ALU.mult))
                        tick.settle()
                        v.tensor_tensor(x1, t[0], t[1], ALU.subtract)
                        v.tensor_tensor(x2, t[2], t[3], ALU.add).then_inc(qn_ready, 1)
                    for j in (4, 5):
                        split_step(q0 + 4 * j, it, 24)
                    if groups == 1:
                        forget_sums()
                if groups == 1:
                    group(None)
                else:
                    with dve.Fori(0, groups) as it:
                        tick.enter(it, 24)
                        group(it)
                    tick.leave(groups)

            def attention(G, a_0, bufs, masks, beside=()):
                beside = list(beside)
                share = -(-len(beside) // HEADS)
                SW, S1 = G * (T + P), G * T
                s = bufs["s"]
                probT = s[:, 3 * SW:4 * SW]

                def out_head(h):
                    dve.wait_ge(o_sum, a_0 + h + 1)
                    tick.mark(v.reciprocal(rsum[:, h % 2, 0:2], lsum[:, h % 4, 0:2]))
                    tick.settle()
                    o = (6 + h % 2) * 512
                    v.tensor_scalar(xn[:, 1, h * HD:(h + 1) * HD], psf[:, o + HD:o + 2 * HD], rsum[:, h % 2, 0:1], None, ALU.mult)
                    v.tensor_scalar(xn[:, 0, h * HD:(h + 1) * HD], psf[:, o:o + HD], rsum[:, h % 2, 1:2], None, ALU.mult).then_inc(o_ready, 1)

                for h in range(HEADS + 2):
                    if h < HEADS:
                        dve.wait_ge(s_done, a_0 + h + 1)
                        if h > 0:
                            dve.wait_ge(exp_ready, a_0 + h)
                        for i, (lo, hi, at) in enumerate(((0, S1, 0), (S1, SW, 1024))):
                            ins = v.tensor_tensor_reduce(out=s[:, lo:hi], in0=psf[:, at:at + hi - lo], in1=masks[i], scale=-1.0,
                                                         scalar=3.0e38, op0=ALU.add, op1=ALU.min, accum_out=nmax[:, h % 2, i:i + 1])
                        ins.then_inc(max_ready, 1)
                    if 1 <= h <= HEADS:
                        dve.wait_ge(p_T, a_0 + h)
                        if h >= 2:
                            dve.wait_ge(o_sum, a_0 + h - 1)
                        if G == 1:
                            ins = v.tensor_copy(probT[:, 0:SW], psf[:, 1536:1536 + SW])
                        else:
                            v.tensor_copy(probT[:, 0:512], psf[:, 1536:2048])
                            ins = v.tensor_copy(probT[:, 1024:SW], psf[:, 2560:1536 + SW])
                        ins.then_inc(pT_dve, 1)
                    if h >= 2:
                        out_head(h - 2)
                    for layer, q, r in beside[h * share:(h + 1) * share]:
                        mod_quarter(q, q + MODQ * layer - FIRST, r)

            def attention_out(k, name):
                for b in range(4):
                    dve.wait_ge(oT_hi, 4 * k + b + 1)
                    two = slice(2 * b, 2 * b + 2)
                    v.tensor_tensor(h_lo[:, two, :].rearrange("p c t -> p (c t)"), ps[:, b, :],
                                    h_hi[:, two, :].rearrange("p c t -> p (c t)"), ALU.subtract).then_inc(oT_lo, 1)
                split(BASE[name] + 4, BASE[name] + 8 + LEAD)

            def mixer(l):
                q0 = BASE[f"mix{l}"]
                bA, bC, bD = MIX_BANKS[0:3]
                dve.wait_ge(mix_in, 48 + 32 * l)
                tick.mark(v.memset(cv[:, :, 0:TAPS - 1], 0.0))
                tri = ntri[:, 0:P].unsqueeze(1).broadcast_to([P, 4, P])
                ws = mixw[:, 0:4 * P].rearrange("p (g t) -> p g t", g=4)
                tick.mark(v.scalar_tensor_tensor(out=ws, in0=ws, scalar=-1.0, in1=tri, op0=ALU.mult, op1=ALU.mult))
                split_step(q0)
                dve.wait_ge(a_sig, l + 1)
                v.tensor_tensor(ac, ps[:, bA:bA + 2, 0:C2], wb[:, 0:512].rearrange("p (t n) -> p t n", t=NT), ALU.mult).then_inc(a_gated, 1)
                split_step(q0 + 4)
                dve.wait_ge(c_copied, l + 1)
                qv = cq[:, :, 0:384].rearrange("p t (h d) -> p t h d", d=HD)
                ov = rot[:, :, :].rearrange("p t (h d) -> p t h d", d=HD)
                x1, x2 = qv[:, :, :, 0:32], qv[:, :, :, 32:64]
                c, s = [k2[:, KONST2[n]:KONST2[n] + 64].rearrange("p (t d) -> p t d", t=NT).unsqueeze(2).broadcast_to([P, NT, 6, 32]) for n in ("cos", "sin")]
                t = [w.rearrange("p (t h d) -> p t h d", t=NT, d=32) for w in (wa[:, 0:384], wa[:, 512:896], wb[:, 512:896], wc[:, 512:896])]
                for dst, xx, cs in ((t[0], x1, c), (t[1], x2, s), (t[2], x2, c), (t[3], x1, s)):
                    tick.mark(v.tensor_tensor(dst, xx, cs, ALU.mult))
                tick.settle()
                v.tensor_tensor(ov[:, :, :, 0:32], t[0], t[1], ALU.subtract)
                v.tensor_tensor(ov[:, :, :, 32:64], t[2], t[3], ALU.add).then_inc(rot_ready, 1)
                split_step(q0 + 8)
                dve.wait_ge(cv_ready, l + 1)
                split(q0 + 15, q0 + 16)
                dve.wait_ge(qkT_ready, l + 1)
                for w in range(2):
                    src = qkT[:, (6 + w) * T:(7 + w) * T].rearrange("p (n i) -> p i n", i=CMP_STRIDE)
                    o = 2 * CMP_LEN * HD + 2 * HD + w * CMP_LEN
                    for part in range(2):
                        pe_col = nsaw[:, o + part * 16:o + part * 16 + 16].unsqueeze(2).broadcast_to([HD, 16, NCMP])
                        ins = v.tensor_tensor(blk[:, w, part * 16:part * 16 + 16, :], src[:, :, part:part + NCMP], pe_col, ALU.add)
                ins.then_inc(blk_ready, 1)
                split(q0 + 16, q0 + 20)
                dve.wait_ge(b_gelu, l + 1)
                for tt in range(NT):
                    tick.mark(v.bn_stats(bnst[:, tt * 6:tt * 6 + 6], zg[:, tt, C2:512]))
                tick.settle()
                for tt in range(NT):
                    ins = v.bn_aggr(lnv[:, 2 * tt:2 * tt + 2], bnst[:, tt * 6:tt * 6 + 6])
                ins.then_inc(zvar_ready, 1)
                dve.wait_ge(zstd_ready, l + 1)
                tick.mark(v.reciprocal(lnv[:, 4:6], lnv[:, 4:6]))
                tick.settle()
                for tt in range(NT):
                    tick.mark(v.tensor_scalar(vn[:, tt, :], zg[:, tt, C2:512], lnv[:, 2 * tt:2 * tt + 1], lnv[:, 4 + tt:5 + tt], ALU.subtract, ALU.mult))
                tick.settle()
                ln = [mixw[:, 4 * P + 2 * HD + i * C2:4 * P + 2 * HD + (i + 1) * C2].unsqueeze(1).broadcast_to([P, NT, C2]) for i in range(2)]
                tick.mark(v.tensor_tensor(vn, vn, ln[0], ALU.mult))
                tick.settle()
                v.tensor_tensor(vn, vn, ln[1], ALU.add).then_inc(vn_ready, 1)
                dve.wait_ge(kv_sum, l + 1)
                v.tensor_copy(kcT, ps[0:HD, 6, 32:32 + NCMP])
                v.tensor_copy(vc, ps[0:NCMP, 6, 64:64 + HD]).then_inc(kv_ready, 1)
                dve.wait_ge(sgu_sum, l + 1)
                fv = ps[:, 6, :].rearrange("p (t n) -> p t n", t=NT)
                for g in range(4):
                    gs = slice(g * HD, (g + 1) * HD)
                    ins = v.scalar_tensor_tensor(out=ysg[:, :, gs], in0=fv[:, :, gs], scalar=col("sgu_b", 4 * l + g), in1=zg[:, :, gs], op0=ALU.add, op1=ALU.mult)
                ins.then_inc(sgu_ready, 1)
                dve.wait_ge(pool_hi, l + 1)
                for c in range(2):
                    ins = v.scalar_tensor_tensor(out=h_lo[:, 6 + c, :], in0=ps[:, 7, c * T:(c + 1) * T], scalar=col("pool_s", 2 * l + c),
                                                 in1=h_hi[:, 6 + c, :], op0=ALU.mult, op1=ALU.subtract)
                ins.then_inc(pool_out, 1)
                segs = [(0, T, 0, 0), (T, 2 * T, 0, T), (NS1, NS1 + P, 1, 0), (NS1 + P, NS1 + 2 * P, 1, P),
                        (NS1 + 2 * P, NS1 + 2 * P + NCMP, 1, 2 * P), (NS1 + 2 * P + NCMP, NS1 + NS0, 1, 2 * P + NCMP)]
                branch = [(1, 1), (1, 2), (0, 1), (0, 2), (0, 0), (1, 0)]

                def weigh(h):
                    i = NH * l + h
                    dve.wait_ge(nexp_ready, i + 1)
                    tick.mark(v.reciprocal(rsum[:, h % 2, 0:6], lsum[:, h % 4, 0:6]))
                    tick.settle()
                    for k, (tt, b) in enumerate(branch):
                        tick.mark(v.tensor_tensor(rsum[:, h % 2, k:k + 1], rsum[:, h % 2, k:k + 1], gt[:, tt, 3 * h + b:3 * h + b + 1], ALU.mult))
                    tick.settle()
                    v.tensor_tensor(rsum[:, h % 2, 4:5], rsum[:, h % 2, 4:5], k2[:, KONST2["late"]:KONST2["late"] + 1], ALU.mult).then_inc(nw_ready, 1)

                for h in range(NH + 2):
                    i = NH * l + h
                    if h < NH:
                        dve.wait_ge(ns_done, i + 1)
                        if h >= 2:
                            dve.wait_ge(nexp_ready, i - 1)
                        for k, (lo, hi, b, o) in enumerate(segs):
                            m = KONST2["nsa1"] + lo if lo < NS1 else KONST2["nsa0"] + lo - NS1
                            ins = v.tensor_tensor_reduce(out=nsaS[h % 2][:, lo:hi], in0=ps[:, (bC, bA)[h % 2] + b, o:o + hi - lo], in1=k2[:, m:m + hi - lo], scale=-1.0,
                                                         scalar=3.0e38, op0=ALU.add, op1=ALU.min, accum_out=nmax[:, h % 2, k:k + 1])
                        ins.then_inc(nmax_ready, 1)
                    if 1 <= h <= NH:
                        weigh(h - 1)
                    if h >= 2:
                        dve.wait_ge(np_T, i - 1)
                        if h >= 3:
                            dve.wait_ge(no_sum, i - 2)
                        v.tensor_copy(nsaT[:, 0:768], psf[:, bD * 512:bD * 512 + 768])
                        v.tensor_copy(nsaT[0:NCMP, 768:1024], ps[0:NCMP, bD + 1, C2:512]).then_inc(npT_copied, 1)
                dve.wait_ge(mu_sum, l + 1)
                v.tensor_tensor(cd, cacc, ps[:, bA, 0:T].unsqueeze(1).broadcast_to([P, 2, T]), ALU.subtract).then_inc(cd_ready, 1)
                dve.wait_ge(no_sum, NH * (l + 1))
                tick.settle()
                ov = ps[:, 7, :].rearrange("p (h t d) -> p t h d", h=NH, t=NT)
                v.tensor_copy(osm[:, 0, :].rearrange("p (h d) -> p h d", d=HD), ov[:, 0, :, :])
                v.tensor_copy(osm[:, 1, :].rearrange("p (h d) -> p h d", d=HD), ov[:, 1, :, :]).then_inc(no_copied, 1)
                dve.wait_ge(cstd_ready, l + 1)
                tick.mark(v.reciprocal(wb[:, 0:T], wb[:, 0:T]))
                tick.settle()
                dve.wait_ge(cd_ready, l + 1)
                v.tensor_tensor(cd, cd, wb[:, 0:T].unsqueeze(1).broadcast_to([P, 2, T]), ALU.mult).then_inc(cn_ready, 1)
                flat = lambda w, c: w[:, c:c + 2, :].rearrange("p c t -> p (c t)")
                for hi, bank, c, done in ((sgu_hi, 6, 4, sgu_out), (no_hi, 7, 2, no_out)):
                    dve.wait_ge(hi, l + 1)
                    v.tensor_tensor(flat(h_lo, c), ps[:, bank, :], flat(h_hi, c), ALU.subtract).then_inc(done, 1)
                dve.wait_ge(conv_hi, l + 1)
                v.tensor_tensor(flat(h_lo, 0), flat(hT, 0), flat(h_hi, 0), ALU.subtract).then_inc(conv_out, 1)
                split(q0 + 20, q0 + 24 + LEAD)

            dve.wait_ge(cact_ready, 1)
            mod_begin(0, 2)
            dve.wait_ge(x_in, 16 * 2)
            dve.wait_ge(konst_in, 16 * 3)
            norm(0)
            mod_begin(2, FIRST)
            split(0, LEAD)
            mod_cols(0, [0], 1)
            norm_parts(0)
            dve.wait_ge(wf_hi_ready, 1)
            v.tensor_tensor(wf_lo[:, :, :], wf[:, :, :], wf_hi[:, :, :], ALU.subtract).then_inc(wf_ready, 1)
            ffn(0)
            mod_cols(0, [1], 2)
            norm(1)
            norm_parts(1)
            forget_logit()
            qk(BASE["fox"], 0, 1)
            gates(0, [1])
            angles()
            split(BASE["fox_out"] + LEAD, BASE["fox_out"] + 4)
            causal, far = KONST["causal"], KONST["dil"]
            attention(1, 0, fox_bufs, [konst[:, causal:causal + T], konst[:, causal + T:causal + T + P]],
                      [(1, q, r) for q in range(FIRST) for r in range(4)])
            attention_out(0, "fox_out")
            update(1, BASE["fox_out"] + 8, 1, 1.0, 4)
            mod_cols(0, [2], 3)
            norm(2)
            norm_parts(2)
            gates(0, [2], 2)
            ffn(1)
            mod_cols(1, [0, 1, 2], 4)
            norm(3)
            norm_parts(3)
            ffn(2)
            norm(4)
            norm_parts(4)
            qk(BASE["dil"], 4, GROUPS)
            split(BASE["dil_out"] + LEAD, BASE["dil_out"] + 4)
            dve.wait_ge(late_in, 32)
            attention(GROUPS, HEADS, dil_bufs, [gate[:, 0, 0:GROUPS * T], konst[:, far:far + GROUPS * P]])
            attention_out(1, "dil_out")
            update(4, BASE["dil_out"] + 8, 1, 1.0, 4)
            norm(5)
            norm_parts(5)
            ffn(3)
            dve.wait_ge(gate_in, 48)
            for l in range(LAYERS):
                norm(6 + 2 * l)
                norm_parts(6 + 2 * l)
                mixer(l)
                update_normed(2 * l, 2 * l, 4)
                norm(7 + 2 * l)
                norm_parts(7 + 2 * l)
                ffn_conv(4 + l)
                if l == 1:
                    dve.wait_ge(gate_in, 64)
                update_normed(2 * l + 1, (2 * l + 1) % 3, DOWN_BANK)


def _steps(w):
    n = w.shape[1] // 512
    return w.reshape(KC, P, n, 512).transpose(2, 1, 0, 3).reshape(n, P, STEP)


def _halves(steps):
    return steps.reshape(-1, P, 2, HALF).transpose(0, 2, 1, 3).reshape(-1, P, HALF)


def _down(w):
    n = w.shape[0] // (2 * P)
    return w.reshape(n, 2, P, D).transpose(0, 2, 1, 3).reshape(n, P, HALF)


def _gate_up(g, u):
    return _halves(_steps(np.stack([g.reshape(D, UPS, C2), u.reshape(D, UPS, C2)], axis=2).reshape(D, 2 * FF)))


def _columns(v):
    return v.reshape(-1, P).T


def _constants():
    t = np.arange(T)
    q, k = t[:, None], t[None, :]

    def tiles(seen):
        far = np.where(seen, np.float32(0), np.float32(-FAR)).astype(np.float32)
        return far[P:, :], far[:P, :P]
    causal = k <= q
    c1, c0 = tiles(causal)
    dil = [tiles(causal & ((q - k) % d == 0) & (q - k <= w)) for w, d in ((128, 1), (512, 4), (2048, 16))]
    eye = np.eye(P, dtype=np.float32)
    one = np.ones((P, P), np.float32)
    ntri = np.concatenate([-np.triu(one), -one], axis=1)
    first = [eye, one, ntri, one[:, :1] * np.float32(EPS), one[:, :1] * np.float32(LN_EPS), c1, c0] + [d[1] for d in dil]

    pool = []
    for w in POOLS:
        cnt = np.minimum(t + 1, w).astype(np.float32)[:, None]
        m = (np.where(causal & (q - k < w), np.float32(1), np.float32(0)) / cnt - np.eye(T, dtype=np.float32)).T.astype(np.float32)
        pool += [m[:P, :], m[P:, P:]]
    ends = np.arange(NCMP) * CMP_STRIDE + CMP_LEN - 1
    cmp_far = np.where(ends[None, :] <= q, np.float32(0), np.float32(-FAR)).astype(np.float32)
    inv = (np.float32(10000.0) ** (-np.arange(32, dtype=np.float32) * np.float32(2.0) / np.float32(HD))).astype(np.float32)
    ang = (t.astype(np.float32)[:, None] * inv[None, :]).astype(np.float32)

    def by_tile(v):
        return v.reshape(NT, P, -1).transpose(1, 0, 2).reshape(P, -1)
    late = (np.arange(P) >= CMP_LEN - 1).astype(np.float32)[:, None]
    second = pool + [c1, c1, c0, c0, cmp_far[:P], cmp_far[P:], by_tile(np.cos(ang)), by_tile(np.sin(ang)),
                     np.full((P, P), 1.0 / C2, np.float32), late]
    sel = np.repeat(np.eye(HEADS, dtype=np.float32), P, axis=1)
    cat = lambda parts: np.ascontiguousarray(np.concatenate(parts, axis=1), np.float32)
    return cat(first), cat(second), cat([d[0] for d in dil]), sel


def kernel(x, c, positions, mod_w, mod_b, norm_g, ffn_w_gate, ffn_w_up, ffn_w_down, fox_w_in, fox_b_f,
           fox_q_g, fox_k_g, fox_w_out, dil_w_in, dil_q_g, dil_k_g, dil_w_out, norm_mix_pre_2,
           norm_mix_post_2, norm_ffn_pre_2, norm_ffn_post_2, w_in_2, w_out_2, conv_dw_w_2, conv_dw_b_2,
           conv_ln_g_2, conv_ln_b_2, nsa_pe_k_2, nsa_pe_v_2, nsa_ck_w1_2, nsa_ck_w2_2, nsa_cv_w1_2,
           nsa_cv_w2_2, sgu_ln_g_2, sgu_ln_b_2, sgu_w_2, sgu_b_2, pool_w_2, pool_scale_2, ffn_up_2,
           ffn_conv_w_2, ffn_conv_b_2, ffn_down_2):
    import concourse.bacc as bacc
    from concourse.bass_utils import run_bass_kernel_spmd as run

    qkv = HEADS * HD
    parts = []
    for i in range(LAYERS):
        for j in range(2):
            ffn = [_gate_up(np.asarray(ffn_w_gate)[i, j], np.asarray(ffn_w_up)[i, j]), _down(np.asarray(ffn_w_down)[i, j])]
            if j == 1:
                parts += [_halves(_steps(np.asarray(fox_w_in)[0][:, :3 * qkv])), _down(np.asarray(fox_w_out)[0])] if i == 0 else \
                         [_halves(_steps(np.asarray(dil_w_in)[0])), _down(np.asarray(dil_w_out)[0])]
            parts += ffn
    at = [0, 256, 512, 768, 1152, 1164, 1420, 1676, 1932]
    for l in range(LAYERS):
        w = np.asarray(w_in_2)[l]
        kv = [w[:, 768 + HD * i:768 + HD * (i + 1)] for i in range(6)]
        order = [w[:, 0:512], w[:, 512:768], kv[2], kv[4], kv[0], kv[1], w[:, 1676:1932], kv[3], kv[5], w[:, 1152:1164],
                 np.zeros((D, 512 - 396), w.dtype), w[:, 1164:1676]]
        up = np.asarray(ffn_up_2)[l]
        parts += [_halves(_steps(np.concatenate(order, axis=1))), _down(np.asarray(w_out_2)[l]),
                  _gate_up(up[:, :FF], up[:, FF:]), _down(np.asarray(ffn_down_2)[l])]
    konst, konst2, dil_mask, sel = _constants()
    inv_freq = np.float32(500000.0) ** (-(np.arange(ROPE_HALF, dtype=np.float32) * np.float32(2.0) / np.float32(2 * ROPE_HALF)))
    as_np = np.asarray
    cols = np.concatenate([_columns(as_np(v)) for v in (
        mod_b, norm_g, norm_mix_pre_2, norm_ffn_pre_2, conv_dw_w_2, conv_dw_b_2, conv_ln_g_2, conv_ln_b_2,
        pool_scale_2, ffn_conv_w_2, ffn_conv_b_2, sgu_b_2, c)], axis=1)
    rows = np.concatenate([as_np(v).reshape(-1) for v in (fox_q_g, fox_k_g, dil_q_g, dil_k_g, fox_b_f)] + [inv_freq.astype(np.float32)])
    mb = as_np(mod_b).reshape(LAYERS, 3, 3, D)
    post = [as_np(norm_mix_post_2), as_np(norm_ffn_post_2)]
    wide = np.concatenate([mb[0, :, 2], mb[1, :, 2]] + [post[k][l:l + 1] for l in range(LAYERS) for k in range(2)], axis=0)
    w1 = [as_np(v).reshape(LAYERS, CMP_LEN, HD, HD).transpose(0, 2, 1, 3).reshape(LAYERS, HD, CMP_LEN * HD) for v in (nsa_ck_w1_2, nsa_cv_w1_2)]
    nsaw = np.concatenate(w1 + [as_np(nsa_ck_w2_2), as_np(nsa_cv_w2_2), as_np(nsa_pe_k_2).transpose(0, 2, 1), as_np(nsa_pe_v_2).transpose(0, 2, 1)], axis=2)
    mixw = np.concatenate(
        [as_np(sgu_w_2).transpose(0, 3, 1, 2).reshape(LAYERS, P, 4 * P),
         as_np(pool_w_2).reshape(LAYERS, 2, 2, HD, HD).transpose(0, 2, 3, 1, 4).reshape(LAYERS, P, 2 * HD)] +
        [np.broadcast_to(as_np(v)[:, None, :], (LAYERS, P, C2)) for v in (sgu_ln_g_2, sgu_ln_b_2)], axis=2)
    arrays = {
        "stream": np.concatenate(parts, axis=0),
        "mod": np.concatenate([_steps(as_np(mod_w)[i]) for i in range(LAYERS)], axis=0),
        "cols": cols, "rows": rows, "wide": wide, "konst": konst, "konst2": konst2, "dil_mask": dil_mask, "sel": sel,
        "wf": as_np(fox_w_in)[0][:, 3 * qkv:].reshape(KC, P, HEADS).transpose(1, 0, 2),
        "x": as_np(x)[0].reshape(NT, P, D).transpose(1, 0, 2),
        "pos": as_np(positions)[0].reshape(NT, P).T,
        "nsaw": nsaw, "mixw": mixw,
    }
    arrays = {f"in_{k}": np.ascontiguousarray(v) for k, v in arrays.items()}
    assert arrays["in_stream"].shape == (HALVES, P, HALF) and arrays["in_cols"].shape == (P, NCOLS)
    assert arrays["in_rows"].shape == (NROWS,) and arrays["in_konst"].shape == (P, NKONST) and arrays["in_konst2"].shape == (P, NKONST2)
    assert arrays["in_nsaw"].shape == (LAYERS, HD, NSA_W) and arrays["in_mixw"].shape == (LAYERS, P, MIX_W)
    nc = bacc.Bacc("TRN2", target_bir_lowering=False, num_devices=1)
    a = {k[3:]: nc.dram_tensor(k, v.shape, mybir.dt.from_np(v.dtype), kind="ExternalInput").ap() for k, v in arrays.items()}
    out = nc.dram_tensor("out", (T, D), F32, kind="ExternalOutput").ap()
    build(nc, a, out)
    r = run(nc, [arrays], core_ids=[0])
    return r.results[0]["out"].reshape(1, T, D)
```
